# Optimizing a Trainium2 kernel written in Bass

```python
import jax, jax.numpy as jnp
from jax import lax
import numpy as np

"""Hybrid diffusion / flow-matching backbone: DEPTH layers over SEQ latent tokens with an
un-noised context prefix sharing the same layer weights.

Each layer = sandwich-normed, adaLN-modulated parallel-head-group token mixer
(2-D neighbourhood attention heads || bidirectional gated DeltaNet heads, one combined
input projection, one output projection) followed by a sandwich-normed, adaLN-modulated
gated ConvFFN.

Inputs:  x (BATCH, SEQ, D_MODEL) latent tokens, c (BATCH, D_MODEL) conditioning vector,
         ctx (BATCH, CTX_LEN, D_MODEL) context tokens, c_ctx (D_MODEL,) context modulation
         vector, plus per-layer weights stacked on a leading DEPTH axis.
Output:  latent stream (BATCH, SEQ, D_MODEL).
"""

D_MODEL = 1024
BATCH = 1
SEQ = 512
DEPTH = 2

CTX_LEN = 256
GRID_W = 64
HEAD_DIM = 64
NA_HEADS = 8
GDN_HEADS = 8
NA_W = NA_HEADS * HEAD_DIM
GDN_W = GDN_HEADS * HEAD_DIM
MIX_W = NA_W + GDN_W
NA_KH = 8
NA_KW = 16
GDN_CHUNK = 64
QKV_CONV = 3
FFN_CONV = 3
D_FF = 2816
ROPE_BASE = 10000.0
ROT_PAIRS_PER_AXIS = HEAD_DIM // 4
RMS_EPS = 1e-6
N_MOD = 6
IN_SPLITS = (NA_W, 2 * NA_W, 3 * NA_W, 3 * NA_W + 3 * GDN_W, 3 * NA_W + 4 * GDN_W,
             3 * NA_W + 4 * GDN_W + 2 * GDN_HEADS)
IN_W = 3 * NA_W + 4 * GDN_W + 4 * GDN_HEADS

kernel_name = 'hybrid_na_gdn_dit_block'

def rms_norm(x, g):
    xf = x.astype(jnp.float32)
    y = xf * lax.rsqrt(jnp.mean(xf * xf, axis=-1, keepdims=True) + RMS_EPS) * g.astype(jnp.float32)
    return y.astype(x.dtype)

def l2_norm(x):
    return x * lax.rsqrt(jnp.sum(x * x, axis=-1, keepdims=True) + RMS_EPS)

def modulate(h, shift, scale):
    return h * (1.0 + scale) + shift

def depthwise_conv_centred(x, w):
    return lax.conv_general_dilated(
        x, w[:, None, :].astype(x.dtype), window_strides=(1,), padding='SAME',
        dimension_numbers=('NWC', 'WIO', 'NWC'), feature_group_count=x.shape[-1])

def axial_rotary_tables(n_tokens):
    t = jnp.arange(n_tokens)
    row = (t // GRID_W).astype(jnp.float32)
    col = (t % GRID_W).astype(jnp.float32)
    inv_freq = ROPE_BASE ** (-jnp.arange(ROT_PAIRS_PER_AXIS, dtype=jnp.float32) / ROT_PAIRS_PER_AXIS)
    ang = jnp.concatenate([row[:, None] * inv_freq, col[:, None] * inv_freq], axis=-1)
    return jnp.cos(ang), jnp.sin(ang)

def apply_rotary(x, cos, sin):
    x1, x2 = jnp.split(x, 2, axis=-1)
    cos = cos[None, :, None, :]
    sin = sin[None, :, None, :]
    return jnp.concatenate([x1 * cos - x2 * sin, x1 * sin + x2 * cos], axis=-1)

def neighbourhood_attention(q, k, v, k_ctx, v_ctx, rpb):
    B, T, H, DH = q.shape
    rows = T // GRID_W
    kh = min(NA_KH, rows)
    kw = NA_KW
    qg = q.reshape(B, rows, GRID_W, H, DH)
    kg = k.reshape(B, rows, GRID_W, H, DH)
    vg = v.reshape(B, rows, GRID_W, H, DH)
    cols = jnp.arange(GRID_W)
    col_start = jnp.clip(cols - kw // 2, 0, GRID_W - kw)
    col_idx = col_start[:, None] + jnp.arange(kw)[None, :]
    dc = col_idx - cols[:, None] + (NA_KW - 1)

    def row_block(r):
        rs = jnp.clip(r - kh // 2, 0, rows - kh)
        k_blk = lax.dynamic_slice_in_dim(kg, rs, kh, axis=1)
        v_blk = lax.dynamic_slice_in_dim(vg, rs, kh, axis=1)
        k_win = k_blk[:, :, col_idx]
        v_win = v_blk[:, :, col_idx]
        q_r = lax.dynamic_index_in_dim(qg, r, axis=1, keepdims=False)
        dr = rs + jnp.arange(kh) - r + (NA_KH - 1)
        bias = rpb[:, dr][:, :, dc]
        s_win = jnp.einsum('bwhd,biwjhd->bwhij', q_r, k_win) + jnp.transpose(bias, (2, 0, 1, 3))[None]
        s_ctx = jnp.einsum('bwhd,blhd->bwhl', q_r, k_ctx)
        s = jnp.concatenate([s_win.reshape(B, GRID_W, H, kh * kw), s_ctx], axis=-1)
        p = jax.nn.softmax(s.astype(jnp.float32), axis=-1).astype(v.dtype)
        p_win = p[..., :kh * kw].reshape(B, GRID_W, H, kh, kw)
        p_ctx = p[..., kh * kw:]
        return (jnp.einsum('bwhij,biwjhd->bwhd', p_win, v_win)
                + jnp.einsum('bwhl,blhd->bwhd', p_ctx, v_ctx))

    o = lax.map(row_block, jnp.arange(rows))
    return jnp.transpose(o, (1, 0, 2, 3, 4)).reshape(B, T, H, DH)

def context_attention(q, k, v):
    s = jnp.einsum('blhd,bmhd->bhlm', q, k)
    p = jax.nn.softmax(s.astype(jnp.float32), axis=-1).astype(v.dtype)
    return jnp.einsum('bhlm,bmhd->blhd', p, v)

def gated_delta_rule_chunked(q, k, v, g, beta, state0):
    B, T, H, DK = q.shape
    DV = v.shape[-1]
    C = GDN_CHUNK
    N = T // C

    def chunks(t):
        t = t.astype(jnp.float32).reshape(B, N, C, H, *t.shape[3:])
        return jnp.moveaxis(t, 3, 2)

    q, k, v, g, beta = (chunks(t) for t in (q, k, v, g, beta))
    g = jnp.cumsum(g, axis=-1)
    idx = jnp.arange(C)
    lower = idx[:, None] >= idx[None, :]
    strict = idx[:, None] > idx[None, :]
    decay = jnp.exp(jnp.where(lower, g[..., :, None] - g[..., None, :], -jnp.inf))
    kb = k * beta[..., None]
    vb = v * beta[..., None]
    m = jnp.where(strict, jnp.einsum('bnhid,bnhjd->bnhij', kb, k) * decay, 0.0)
    a = m + jnp.eye(C, dtype=jnp.float32)
    rhs = jnp.concatenate([vb, kb * jnp.exp(g)[..., None]], axis=-1)
    sol = lax.linalg.triangular_solve(a, rhs, left_side=True, lower=True, unit_diagonal=True)
    u, w = sol[..., :DV], sol[..., DV:]
    qk = jnp.einsum('bnhid,bnhjd->bnhij', q, k) * decay

    def step(S, inp):
        q_c, k_c, u_c, w_c, g_c, qk_c = inp
        v_new = u_c - jnp.einsum('bhck,bhkv->bhcv', w_c, S)
        o = (jnp.einsum('bhck,bhkv->bhcv', q_c * jnp.exp(g_c)[..., None], S)
             + jnp.einsum('bhij,bhjv->bhiv', qk_c, v_new))
        g_last = g_c[..., -1:]
        S = (S * jnp.exp(g_last)[..., None]
             + jnp.einsum('bhck,bhcv->bhkv', k_c * jnp.exp(g_last - g_c)[..., None], v_new))
        return S, o

    xs = tuple(jnp.moveaxis(t, 1, 0) for t in (q, k, u, w, g, qk))
    S, o = lax.scan(step, state0.astype(jnp.float32), xs)
    o = jnp.moveaxis(jnp.moveaxis(o, 0, 1), 2, 3).reshape(B, T, H, DV)
    return o, S

def gdn_qkv(qkv, conv_w, cos=None, sin=None):
    qkv = jax.nn.silu(depthwise_conv_centred(qkv, conv_w)).astype(jnp.float32)
    q, k, v = jnp.split(qkv, 3, axis=-1)
    heads = lambda t: t.reshape(*t.shape[:-1], GDN_HEADS, HEAD_DIM)
    q, k, v = l2_norm(heads(q)), l2_norm(heads(k)), heads(v)
    if cos is not None:
        q, k = apply_rotary(q, cos, sin), apply_rotary(k, cos, sin)
    return q * HEAD_DIM ** -0.5, k, v

def gdn_gates(beta_logits, decay_in, a_log, dt_bias, d):
    sl = slice(d * GDN_HEADS, (d + 1) * GDN_HEADS)
    beta = jax.nn.sigmoid(beta_logits[..., sl].astype(jnp.float32))
    g = -jnp.exp(a_log[d]) * jax.nn.softplus(decay_in[..., sl].astype(jnp.float32) + dt_bias[d])
    return g, beta

def hybrid_mixer(h_lat, h_ctx, w_in, qkv_conv, a_log, dt_bias, gdn_norm, rpb, w_out, cos, sin):
    B = h_lat.shape[0]
    na_q_l, na_k_l, na_v_l, gqkv_l, z_l, beta_l, dec_l = jnp.split(h_lat @ w_in, IN_SPLITS, axis=-1)
    na_q_c, na_k_c, na_v_c, gqkv_c, z_c, beta_c, dec_c = jnp.split(h_ctx @ w_in, IN_SPLITS, axis=-1)
    na_heads = lambda t: t.reshape(*t.shape[:-1], NA_HEADS, HEAD_DIM)
    scale = HEAD_DIM ** -0.5

    k_c, v_c = na_heads(na_k_c), na_heads(na_v_c)
    o_na_lat = neighbourhood_attention(na_heads(na_q_l) * scale, na_heads(na_k_l), na_heads(na_v_l),
                                       k_c, v_c, rpb)
    o_na_ctx = context_attention(na_heads(na_q_c) * scale, k_c, v_c)

    q_l, k_l, v_l = gdn_qkv(gqkv_l, qkv_conv, cos, sin)
    q_c, k_c2, v_c2 = gdn_qkv(gqkv_c, qkv_conv)
    s0 = jnp.zeros((B, GDN_HEADS, HEAD_DIM, HEAD_DIM), jnp.float32)
    flip = lambda t: jnp.flip(t, axis=1)
    g_lf, b_lf = gdn_gates(beta_l, dec_l, a_log, dt_bias, 0)
    g_cf, b_cf = gdn_gates(beta_c, dec_c, a_log, dt_bias, 0)
    g_lb, b_lb = gdn_gates(beta_l, dec_l, a_log, dt_bias, 1)
    g_cb, b_cb = gdn_gates(beta_c, dec_c, a_log, dt_bias, 1)
    o_cf, s_cf = gated_delta_rule_chunked(q_c, k_c2, v_c2, g_cf, b_cf, s0)
    o_lf, _ = gated_delta_rule_chunked(q_l, k_l, v_l, g_lf, b_lf, s_cf)
    o_cb, s_cb = gated_delta_rule_chunked(flip(q_c), flip(k_c2), flip(v_c2), flip(g_cb), flip(b_cb), s0)
    o_lb, _ = gated_delta_rule_chunked(flip(q_l), flip(k_l), flip(v_l), flip(g_lb), flip(b_lb), s_cb)
    gdn_heads = lambda t: t.reshape(*t.shape[:-1], GDN_HEADS, HEAD_DIM)
    o_gdn_lat = rms_norm(o_lf + flip(o_lb), gdn_norm) * jax.nn.silu(gdn_heads(z_l).astype(jnp.float32))
    o_gdn_ctx = rms_norm(o_cf + flip(o_cb), gdn_norm) * jax.nn.silu(gdn_heads(z_c).astype(jnp.float32))

    def merge(o_na, o_gdn, ref):
        o = jnp.concatenate([o_na.reshape(*o_na.shape[:2], NA_W),
                             o_gdn.reshape(*o_gdn.shape[:2], GDN_W).astype(o_na.dtype)], axis=-1)
        return (o @ w_out).astype(ref.dtype)

    return merge(o_na_lat, o_gdn_lat, h_lat), merge(o_na_ctx, o_gdn_ctx, h_ctx)

def conv_ffn(h, w_up, conv_w, w_down):
    u = depthwise_conv_centred(h @ w_up, conv_w)
    gate, val = jnp.split(u, 2, axis=-1)
    return (jax.nn.silu(gate) * val) @ w_down

def setup_inputs(seed: int = 0) -> dict:
    key = jax.random.key(seed)
    ks = jax.random.split(key, 24)
    f32 = jnp.float32
    nrm = lambda k, shape, s: jax.random.normal(k, shape, f32) * s
    gain = lambda k, shape: 1.0 + 0.1 * jax.random.normal(k, shape, f32)
    dt = jax.random.uniform(ks[11], (DEPTH, 2, GDN_HEADS), f32, 0.001, 0.1)
    return {
        'x': nrm(ks[0], (BATCH, SEQ, D_MODEL), 1.0),
        'c': nrm(ks[1], (BATCH, D_MODEL), 1.0),
        'ctx': nrm(ks[2], (BATCH, CTX_LEN, D_MODEL), 1.0),
        'c_ctx': nrm(ks[3], (D_MODEL,), 1.0),
        'ada_w': nrm(ks[4], (DEPTH, D_MODEL, N_MOD * D_MODEL), D_MODEL ** -0.5),
        'ada_b': nrm(ks[5], (DEPTH, N_MOD * D_MODEL), 0.01),
        'norm_mix_pre': gain(ks[6], (DEPTH, D_MODEL)),
        'norm_mix_post': gain(ks[7], (DEPTH, D_MODEL)),
        'w_in': nrm(ks[8], (DEPTH, D_MODEL, IN_W), D_MODEL ** -0.5),
        'qkv_conv': nrm(ks[9], (DEPTH, QKV_CONV, 3 * GDN_W), QKV_CONV ** -0.5),
        'a_log': jnp.log(jax.random.uniform(ks[10], (DEPTH, 2, GDN_HEADS), f32, 1.0, 16.0)),
        'dt_bias': dt + jnp.log(-jnp.expm1(-dt)),
        'gdn_norm': gain(ks[12], (DEPTH, HEAD_DIM)),
        'rpb': nrm(ks[13], (DEPTH, NA_HEADS, 2 * NA_KH - 1, 2 * NA_KW - 1), 0.5),
        'w_out': nrm(ks[14], (DEPTH, MIX_W, D_MODEL), MIX_W ** -0.5),
        'norm_ffn_pre': gain(ks[15], (DEPTH, D_MODEL)),
        'norm_ffn_post': gain(ks[16], (DEPTH, D_MODEL)),
        'ffn_up': nrm(ks[17], (DEPTH, D_MODEL, 2 * D_FF), D_MODEL ** -0.5),
        'ffn_conv': nrm(ks[18], (DEPTH, FFN_CONV, 2 * D_FF), FFN_CONV ** -0.5),
        'ffn_down': nrm(ks[19], (DEPTH, D_FF, D_MODEL), D_FF ** -0.5),
    }

def reference(x, c, ctx, c_ctx, ada_w, ada_b, norm_mix_pre, norm_mix_post, w_in, qkv_conv, a_log,
              dt_bias, gdn_norm, rpb, w_out, norm_ffn_pre, norm_ffn_post, ffn_up, ffn_conv, ffn_down):
    cos, sin = axial_rotary_tables(x.shape[1])
    xc = ctx
    for l in range(DEPTH):
        last = l == DEPTH - 1
        m_lat = [m[:, None, :] for m in jnp.split(jax.nn.silu(c) @ ada_w[l] + ada_b[l], N_MOD, axis=-1)]
        m_ctx = jnp.split(jax.nn.silu(c_ctx) @ ada_w[l] + ada_b[l], N_MOD, axis=-1)

        h_lat = modulate(rms_norm(x, norm_mix_pre[l]), m_lat[0], m_lat[1])
        h_ctx = modulate(rms_norm(xc, norm_mix_pre[l]), m_ctx[0], m_ctx[1])
        y_lat, y_ctx = hybrid_mixer(h_lat, h_ctx, w_in[l], qkv_conv[l], a_log[l], dt_bias[l], gdn_norm[l],
                                    rpb[l], w_out[l], cos, sin)
        x = x + m_lat[2] * rms_norm(y_lat, norm_mix_post[l])
        if not last:
            xc = xc + m_ctx[2] * rms_norm(y_ctx, norm_mix_post[l])

        f_lat = conv_ffn(modulate(rms_norm(x, norm_ffn_pre[l]), m_lat[3], m_lat[4]),
                         ffn_up[l], ffn_conv[l], ffn_down[l])
        x = x + m_lat[5] * rms_norm(f_lat, norm_ffn_post[l])
        if not last:
            f_ctx = conv_ffn(modulate(rms_norm(xc, norm_ffn_pre[l]), m_ctx[3], m_ctx[4]),
                             ffn_up[l], ffn_conv[l], ffn_down[l])
            xc = xc + m_ctx[5] * rms_norm(f_ctx, norm_ffn_post[l])
    return x


_drawn_inputs = setup_inputs


def setup_inputs(seed=0):
    import zlib

    import numpy as np

    out = dict(_drawn_inputs(seed))
    spreads = {}
    factors = {}
    for name, (base, spread) in spreads.items():
        noise = np.random.default_rng([zlib.crc32(name.encode()), seed]).standard_normal(out[name].shape)
        drawn = base * np.exp(spread * noise) if base else spread * noise
        out[name] = __import__('jax').numpy.asarray(drawn.astype(out[name].dtype))
    for name, factor in factors.items():
        out[name] = (out[name] * factor).astype(out[name].dtype)
    return out
```

```python
from contextlib import ExitStack

import numpy as np

import concourse.bass as bass
from concourse import mybir

ALU = mybir.AluOpType
ACT = mybir.ActivationFunctionType
AX = mybir.AxisListType
F32 = mybir.dt.float32
F32R = mybir.dt.float32r
I32 = mybir.dt.int32
ds = bass.ds

P = 128
D = 1024
KT = D // P
LAT, CTX = 512, 256
TOK = LAT + CTX
NT, LT = TOK // P, LAT // P
H, DH = 8, 64
HP = H // 2
W = H * DH
DEPTH = 2
IN_W = 3 * W + 4 * W + 4 * H
DFF = 2816
FT = DFF // P
NMOD = 6
GRID, ROWS = 64, 8
KH, KW = 8, 16
C = 64
LEVELS = 6
EPS = 1e-6
CHUNKS = 28 + 8 + 2 * FT + FT
NEG = -1e30

C_ID = 0
C_A = C_ID + P
C_ONE = C_A + 4 * P
C_B = C_ONE + 2 * P
C_CS = C_B + 4 * C
C_NEG = C_CS + LT * 2 * 32
C_TI = C_NEG + 2 * ROWS * 32
C_XQ = C_TI + C
C_W = C_XQ + P
LE, GE, GT, LT_ = 0, 1, 2, 3


def constants():
    m = np.arange(P)
    same = (m[:, None] // C) == (m[None, :] // C)
    r, k = m[:, None], m[None, :]
    a = [same & (r <= k), same & (r >= k), same & (r > k), same & (r < k)]
    one = [np.repeat((m // C == c)[:, None], P, 1) for c in range(2)]
    pc, col = (m % C)[:, None], np.arange(C)[None, :]
    b = [pc > col, pc < col, pc <= col, pc >= col]
    t = np.arange(LAT)
    inv = (10000.0 ** (-np.arange(16, dtype=np.float32) / 16)).astype(np.float32)
    ang = np.concatenate([(t // GRID)[:, None].astype(np.float32) * inv,
                          (t % GRID)[:, None].astype(np.float32) * inv], 1)
    cs = np.stack([np.cos(ang), np.sin(ang)], 1).reshape(LT, P, 2, 32).transpose(1, 0, 2, 3)
    k32 = np.arange(32)[None, None, :]
    qc = (m % 16)[:, None, None]
    inner = (k32 - qc >= 0) & (k32 - qc <= 15)
    edge = np.where(((m % 16) // 8)[:, None, None] == 0, k32 < 16, k32 >= 16)
    neg = np.stack([np.broadcast_to(np.where(x, 0.0, NEG), (P, ROWS, 32)) for x in (inner, edge)], 1)
    ti = pc == col
    xq = (m[:, None] % C) == (m[None, :] % C)
    parts = [np.eye(P), *a, *one, *b, cs.reshape(P, -1), neg.reshape(P, -1), ti, xq]
    cns = np.concatenate([np.asarray(x, np.float32) for x in parts], 1)
    i, kk = np.arange(C)[None, :], pc
    lev = []
    for d in range(2):
        for s in range(LEVELS):
            w = 1 << s
            blk = (kk // (2 * w)) == (i // (2 * w))
            lo, hi = (kk // w) % 2 == 0, (i // w) % 2 == 1
            lev.append(blk & lo & hi if d == 0 else blk & ~lo & ~hi)
    return np.ascontiguousarray(cns), np.ascontiguousarray(np.concatenate(lev, 1).astype(np.int32))


def per_layer():
    t = {}
    for names, n in (("bd_done bd_h bd_split dec_abs dec_ln decays e_ready gates mods_done mods o_root qk_root "
                      "rb_masked sums rms0 rms1 y_rms0 y_rms1", 1),
                     ("vec_t v_out_a v_out_d", 3),
                     ("gate_done0 gate_done1 gate_out0 gate_out1 gdiag0 gdiag1 o_out o_turned ov_out", HP),
                     ("y_out_a0 y_out_a1 y_out_d0 y_out_d1 normed0 normed1 o_normed o_sq o_summed qk_normed qk_out "
                      "qk_sq qk_summed qk_turned", NT),
                     ("proj_free o_high o_split valued", H),
                     ("conv mid taps gram_out gram group_done m_ready o_added0 o_added1 st_ready_d state0 state1 "
                      "vnew_done0 vnew_done1 vnew0 vnew1 w_out_q", 2 * NT),
                     ("turned qkv_out", 2 * NT + 2),
                     ("h_ready0 h_ready1 hid_h0 hid_h1 hid_t0 hid_t1 hid_v0 hid_v1", 2 * KT),
                     ("chained diffs egi em exps kq st_ready_a", 4 * NT),
                     ("ra exped maxed p_turned probs scored", H * NT),
                     ("p_done0 p_done1 xt_new0 xt_new1 z_done0 z_done1 zb_a0 zb_a1 zb_d0 zb_d1", NT * LEVELS),
                     ("xq_new0 xq_new1 xt_turned0 xt_turned1", NT * (LEVELS - 1)),
                     ("pt_even pt_odd", H * NT // 2), ("g_done", FT + 2), ("g_used up_silu", FT), ("g_high g_split up_mid", 2 * FT), ("up_taps", 2 * FT + 4),
                     ("rb", 16 * (2 * ROWS + 1)), ("rows", 16 * 11)):
        for name in names.split():
            t[name] = n
    return t


SIGNALS = per_layer()


def before(l, name):
    return l * SIGNALS[name]


class Chain:

    def __init__(self, eng, sem):
        self.eng, self.sem, self.n, self.i, self.base, self.per = eng, sem, 0, None, 0, 0

    def did(self, ins):
        ins.then_inc(self.sem, 1)
        self.n += 1
        return ins

    def enter(self, i, per):
        self.base, self.i, self.per, self.n = self.n, i, per, 0

    def leave(self, trips):
        assert self.n == self.per
        self.n, self.i = self.base + trips * self.per, None

    def wait(self):
        if self.i is None:
            self.eng.wait_ge(self.sem, self.n)
        else:
            self.eng.wait_ge(self.sem, self.i * self.per + (self.base + self.n))


def build(nc, a):
    ctx = ExitStack()
    with ctx:
        sems = {}

        def sem(name):
            if name not in sems:
                sems[name] = ctx.enter_context(nc.semaphore(name))
            return sems[name]

        here = [512]

        def perm(name, shape, dt=F32):
            t = nc.alloc_sbuf_tensor_at(name, shape, dt, offset=here[0])
            here[0] += -(-int(np.prod(shape[1:])) * 4 // 64) * 64
            return t

        cns = perm("cns", [P, C_W])
        lev = perm("lev", [P, 2, LEVELS, C], I32)
        w_raw = perm("w_raw", [P, 2, D])
        w_hi = perm("w_hi", [P, 2, D], F32R)
        w_lo = perm("w_lo", [P, 2, D], F32R)
        taps = [perm(f"taps{l}", [P, 3 * 2 * FT]) for l in range(DEPTH)]
        vec = [perm(f"vec{l}", [P, P]) for l in range(DEPTH)]
        cond = perm("cond", [P, 2 * KT])
        mod = perm("mod", [P, NMOD * KT, 2])
        mod_raw = perm("mod_raw", [P, NMOD * KT, 2])
        sc_pre = perm("sc_pre", [P, 2, KT, 2])
        gate_c = perm("gate_c", [P, 2, KT, 2])
        ones = perm("ones", [P, P])
        eps_t = perm("eps_t", [P, 1])
        stat = perm("stat", [P, 64])
        stat2 = perm("stat2", [P, 64])
        al_dt = perm("al_dt", [P, DEPTH, 2, 16])
        bd = perm("bd", [P, NT, 32])
        beta = perm("beta", [P, NT, 16])
        graw = perm("graw", [P, NT, 16])
        gtmp = perm("gtmp", [P, 2, NT, 16])
        e_cum = perm("e_cum", [P, 2, NT, H])
        e_tail = perm("e_tail", [P, 2, NT, H])
        e_tot = perm("e_tot", [P, 2, NT, 16])
        nbe = perm("nbe", [P, NT, 16])
        nbec = perm("nbec", [P, 2, NT, H])
        qk_ss = perm("qk_ss", [P, NT, 2 * H])
        qk_rt = perm("qk_rt", [P, NT, 2 * H])
        arena = here[0]
        KB = 1024

        def at(name, kb, shape, dt=F32):
            return nc.alloc_sbuf_tensor_at(name, shape, dt, offset=arena + kb * KB)

        x_sb = at("x_sb", 151, [P, NT, D])
        xn = at("xn", 0, [P, NT, D])
        v_nat = at("v_nat", 88, [P, LT, W])
        row_ffn = at("row_ffn", 64, [P, P])
        row_vec = at("row_vec", 65, [P, P])
        row_c = at("row_c", 66, [16, P])
        bd_raw = at("bd_raw", 84, [P, KT, 32])
        bd_hi = at("bd_hi", 85, [P, KT, 32], F32R)
        bd_lo = at("bd_lo", 86, [P, KT, 32], F32R)
        ada_first = [at(f"ada_first{i}", (103, 119, 135, 24)[i], [P, KT, 4 * P]) for i in range(4)]
        ada_ring = at("ada_ring", 143, [P, 2, KT, 4 * P])
        mod_first = at("mod_first", 69, [2, 4, 512])
        mod_row = at("mod_row", 100, [2, 512])
        v_ring = at("v_ring", 96, [P, 2, 512])
        h_hi = at("h_hi", 103, [P, KT, TOK], F32R)
        h_lo = at("h_lo", 127, [P, KT, TOK], F32R)
        qkv = at("qkv", 0, [P, NT, 3 * W])
        z_sb = at("z_sb", 36, [P, NT, W])
        na_q = at("na_q", 48, [P, HP, TOK])
        na_k = at("na_k", 60, [P, HP, TOK])
        na_v = at("na_v", 72, [P, NT, W])
        cv = at("cv", 151, [P, 2, TOK])
        cvs = at("cvs", 157, [P, 2, TOK])
        o_t = at("o_t", 84, [P, HP, TOK])
        rb = at("rb", 103, [P, 2, H, ROWS, 32])
        prob = at("prob", 119, [P, 2, 512])
        pt = at("pt", 123, [P, 2, 20, P])
        o_g = at("o_g", 48, [P, NT, W])
        q_t = at("q_t", 60, [P, HP, TOK])
        k_t = at("k_t", 72, [P, HP, TOK])
        sq = at("sq", 96, [P, D])
        rot = at("rot", 100, [P, 2, D])
        e1 = [at(f"e1_{d}", 96 + 20 * d, [P, H, C]) for d in range(2)]
        e2 = [at(f"e2_{d}", 98 + 20 * d, [P, H, C]) for d in range(2)]
        ra = [at(f"ra_{d}", 100 + 20 * d, [P, H, C]) for d in range(2)]
        rbb = [at(f"rbb_{d}", 102 + 20 * d, [P, H, C]) for d in range(2)]
        xtc = [at(f"xtc_{d}", 104 + 20 * d, [P, H, C]) for d in range(2)]
        xtb = [at(f"xtb_{d}", 106 + 20 * d, [P, H, 2, C]) for d in range(2)]
        xq = [at(f"xq_{d}", 110 + 20 * d, [P, HP, P]) for d in range(2)]
        zb = [at(f"zb_{d}", 112 + 20 * d, [P, HP, 2, 2, C]) for d in range(2)]
        st_a = [at(f"st_a_{d}", 136 + 4 * d, [P, 2, H, C]) for d in range(2)]
        st_b = [at(f"st_b_{d}", 144 + 8 * d, [P, 2, H, P]) for d in range(2)]
        mv_a = [at(f"mv_a_{d}", 160 + 4 * d, [P, 2, H, C]) for d in range(2)]
        mv_b = [at(f"mv_b_{d}", 168 + 2 * d, [P, H, C]) for d in range(2)]
        o_hi = at("o_hi", 103, [P, KT, TOK], F32R)
        o_lo = at("o_lo", 127, [P, KT, TOK], F32R)
        on = at("on", 60, [P, NT, W])
        ov = at("ov", 72, [P, 2, TOK])
        osq = at("osq", 78, [P, W])
        o_ss = at("o_ss", 80, [P, NT * H])
        o_rt = at("o_rt", 81, [P, NT * H])
        v_junk = at("v_junk", 60, [P, D])[:]
        y_sb = at("y_sb", 0, [P, NT, D])
        gate_b = at("gate_b", 24, [P, 2, D])
        gdiag = at("gdiag", 32, [P, 512])
        zeros = at("zeros", 67, [P, 512])
        junk = at("junk", 96, [P, D])
        g_sb = at("g_sb", 0, [P, FT, TOK])
        cg = at("cg", 68, [P, 2, TOK])
        cw = at("cw", 74, [P, 2, TOK])
        g_hi = at("g_hi", 80, [P, 2, TOK], F32R)
        g_lo = at("g_lo", 86, [P, 2, TOK], F32R)
        y2_sb = at("y2_sb", 103, [P, NT, D])
        gate_b2 = at("gate_b2", 127, [P, 2, D])
        gdiag2 = at("gdiag2", 135, [P, 512])
        junk2 = at("junk2", 140, [P, D])

        ps = ctx.enter_context(nc.psum_tensor("ps", [P, 8, 512], F32))
        x_mid = nc.dram_tensor("x_mid", (P, NT, D), F32, kind="Internal").ap()
        v_mid = nc.dram_tensor("v_mid", (LAT, W), F32, kind="Internal").ap()
        bias_rows = nc.dram_tensor("bias_rows", (DEPTH, ROWS, 64, 31), F32, kind="Internal").ap()
        bias_wide = nc.dram_tensor("bias_wide", (DEPTH, ROWS, 16, 64, 48), F32, kind="Internal").ap()

        ident = cns[:, C_ID:C_ID + P]
        amask = [cns[:, C_A + P * i:C_A + P * (i + 1)] for i in range(4)]
        onec = [cns[:, C_ONE + P * i:C_ONE + P * (i + 1)] for i in range(2)]
        bmask = [cns[:, C_B + C * i:C_B + C * (i + 1)] for i in range(4)]
        cs = cns[:, C_CS:C_CS + LT * 64].rearrange("p (t a c) -> p t a c", t=LT, a=2)
        negm = cns[:, C_NEG:C_NEG + 512].rearrange("p (v r c) -> p v r c", v=2, r=ROWS)
        ti = cns[:, C_TI:C_TI + C]
        xq0 = cns[:, C_XQ:C_XQ + P]

        phase_end = sem("phase_end")
        block = ctx.enter_context(nc.Block())

        def phase_ends(eng, counts, n):
            if counts:
                eng.drain().then_inc(phase_end, 1)
            eng.wait_ge(phase_end, 4 * n)

        PH = 7
        UNITS = DEPTH * NMOD * 2 - 4
        def lat_only(l):
            return l == DEPTH - 1

        def col(t):
            return slice(t * P, (t + 1) * P)

        def unit(tile, parity):
            return tile * 2 + parity

        def turned(n, u, h):
            pairs = []
            if u < LT:
                i0, i1 = ((0, 2), (3, 4), (5, 6), (1, 7))[u]
                pairs.append((pt[:, h % 2, i0:i1 + 1:i1 - i0, :], ps[:, 2 + n % 2, 0:256].rearrange("p (a b) -> p a b", a=2)))
            c = ((8 + u, 12 + u) if u < LT else (12 + u, 14 + u))
            pairs.append((pt[:, h % 2, c[0]:c[1] + 1:c[1] - c[0], :], ps[:, 2 + n % 2, 256:512].rearrange("p (a b) -> p a b", a=2)))
            return pairs

        FWD, BWD = [4, 5, 0, 1, 2, 3], [5, 4, 3, 2, 1, 0]
        TILES = [FWD, BWD]

        @block.sync
        def _(sp):
            wl = [sem("w_landed0"), sem("w_landed1")]
            al = [sem(f"ada_landed{i}") for i in range(2)]
            w_free, ada_used = sem("w_lo_ready"), sem("ada_used")
            consts = sem("consts")
            sp.dma_start(cns[:], a["cns"]).then_inc(consts, 16)
            sp.dma_start(lev[:].rearrange("p a b c -> p (a b c)"), a["lev"]).then_inc(consts, 16)
            for l in range(DEPTH):
                for k, v in enumerate(("a_log", "dt_bias")):
                    src = a[v][l].rearrange("a b -> (a b)").unsqueeze(0).to_broadcast([P, 16])
                    sp.dma_start(al_dt[:, l, k, :], src).then_inc(consts, 16)
            sp.dma_start(row_c[0:8, :], a["c"].rearrange("a (k p) -> (a k) p", p=P)).then_inc(consts, 16)
            sp.dma_start(row_c[8:16, :], a["c_ctx"].rearrange("(k p) -> k p", p=P)).then_inc(consts, 16)

            def w_chunk(n, src, split, first):
                slot = n % 2 if isinstance(n, int) else first % 2
                sp.wait_ge(w_free, n + 1)
                dst = w_raw[:, slot, :]
                if split:
                    dst = dst.rearrange("p (k n) -> p k n", k=split)
                sp.dma_start(dst, src).then_inc(wl[slot], 16)

            def columns(base, w, col0, tiles):
                v = w.rearrange("(k p) n -> p k n", p=P)
                with sp.Fori(0, tiles // 2) as i:
                    for j in range(2):
                        w_chunk(i * 2 + (base + j), v[:, :, ds(i * 256 + (col0 + j * P), P)], KT, base + j)

            def rows(base, w, col0, chunks):
                v = w.rearrange("(j two p) n -> j p two n", p=P, two=2)
                for j in range(chunks):
                    w_chunk(base + j, v[j, :, :, col0:col0 + 512], 2, base + j)

            for l in range(DEPTH):
                w_in, base, ph = a["w_in"][l], l * CHUNKS, l * PH
                toks = LT if lat_only(l) else NT
                if l:
                    sp.wait_ge(phase_end, 4 * ph)
                if l == 0:
                    sp.dma_start(x_sb[:, 0:LT, :], a["x"][0].rearrange("(t p) n -> p t n", p=P)).then_inc(sem("x_landed"), 16)
                    sp.dma_start(x_sb[:, LT:NT, :], a["ctx"][0].rearrange("(t p) n -> p t n", p=P)).then_inc(sem("x_landed"), 16)
                rows_l = sem("rows")
                cvw = a["ffn_conv"][l].rearrange("t (f p) -> (t f) p", p=P)
                sp.dma_start(row_ffn[:], cvw[0:P]).then_inc(rows_l, 16)
                sp.dma_start(row_vec[0:4, :], cvw[P:P + 4]).then_inc(rows_l, 16)
                sp.dma_start(row_vec[4:40, :], a["qkv_conv"][l].rearrange("t (f p) -> (t f) p", p=P)).then_inc(rows_l, 16)
                sp.dma_start(row_vec[40:88, :], a["ada_b"][l].rearrange("(f p) -> f p", p=P)).then_inc(rows_l, 16)
                for k, v in enumerate(("norm_mix_pre", "norm_mix_post", "norm_ffn_pre", "norm_ffn_post")):
                    sp.dma_start(row_vec[88 + 8 * k:96 + 8 * k, :], a[v][l].rearrange("(f p) -> f p", p=P)).then_inc(rows_l, 16)
                for k in range(2):
                    sp.dma_start(row_vec[120:121, 64 * k:64 * k + 64], a["gdn_norm"][l].unsqueeze(0)).then_inc(rows_l, 16)
                sp.dma_start(bd_raw[:], w_in.rearrange("(k p) n -> p k n", p=P)[:, :, 7 * W:7 * W + 32]).then_inc(rows_l, 16)
                av = a["ada_w"][l].rearrange("(k p) n -> p k n", p=P)
                if l == 0:
                    for i in range(4):
                        sp.dma_start(ada_first[i][:], av[:, :, i * 4 * P:(i + 1) * 4 * P]).then_inc(sem("ada_first"), 16)
                columns(base, w_in, 0, 4)
                columns(base + 4, w_in, W, 4)
                columns(base + 8, w_in, 3 * W, 12)
                rows(base + 20, w_in, 2 * W, 4)
                rows(base + 24, w_in, 6 * W, 4)
                sp.wait_ge(sem("v_out_a"), before(l, "v_out_a") + 3)
                sp.wait_ge(sem("v_out_d"), before(l, "v_out_d") + 3)
                sp.dma_start(v_mid.rearrange("(t p) n -> p t n", p=P), v_nat[:]).then_inc(sem("v_saved"), 16)
                sp.wait_ge(sem("v_saved"), 16 * (l + 1))
                for j in range(LT):
                    sp.dma_start(na_v[:, j, :], v_mid.rearrange("(r j c) n -> j r c n", j=4, c=16)[j]).then_inc(sem("v_sorted"), 16)
                sp.wait_ge(phase_end, 4 * (ph + 2))
                rb_l = sem("rb")
                if l == 0:
                    sp.wait_ge(sem("bias_spread"), 16 * DEPTH * ROWS)
                src = lambda q, c0, c1, at_: bias_wide[l, q, c0:c1, :, at_:at_ + 32]
                sp.dma_start(rb[:, 0].rearrange("p h r c -> p (h r) c"),
                             bias_wide[l].rearrange("q c r k -> (q c) r k")[:, :, 8:40]).then_inc(rb_l, 16)
                for q in range(ROWS):
                    for e in range(2):
                        sp.dma_start(rb[16 * q + 8 * e:16 * q + 8 * e + 8, 1].rearrange("p h r c -> p (h r) c"),
                                     src(q, 8 * e, 8 * e + 8, 16 - 16 * e)).then_inc(rb_l, 16)
                if l == 0:
                    for la, i0, i1 in ((0, 2, 6), (1, 0, 6)):
                        va = a["ada_w"][la].rearrange("(k p) n -> p k n", p=P)
                        with sp.Fori(i0, i1) as i:
                            for j in range(2):
                                sp.wait_ge(ada_used, i * 2 + ((12 if la else 0) + j + 1))
                                sp.dma_start(ada_ring[:, j], va[:, :, ds(i * 1024 + j * 512, 512)]).then_inc(al[j], 16)
                for h in range(2):
                    rows(base + 28 + 4 * h, a["w_out"][l], 512 * h, 4)
                sp.wait_ge(phase_end, 4 * (ph + 4))
                if l == 0:
                    sp.dma_start(x_sb[:, 0:LT, :], a["x"][0].rearrange("(t p) n -> p t n", p=P)).then_inc(sem("x_landed"), 16)
                    sp.dma_start(x_sb[:, LT:NT, :], a["ctx"][0].rearrange("(t p) n -> p t n", p=P)).then_inc(sem("x_landed"), 16)
                else:
                    sp.dma_start(x_sb[:, 0:LT, :], x_mid[:, 0:LT, :]).then_inc(sem("x_landed"), 16)
                    sp.dma_start(x_sb[:, LT:NT, :], x_mid[:, LT:NT, :]).then_inc(sem("x_landed"), 16)
                up = a["ffn_up"][l].rearrange("(k p) n -> p k n", p=P)
                with sp.Fori(0, FT) as i:
                    for j in range(2):
                        w_chunk(i * 2 + (base + 36 + j), up[:, :, ds(i * P + j * DFF, P)], KT, j)
                for h in range(2):
                    rows(base + 36 + 2 * FT + 11 * h, a["ffn_down"][l], 512 * h, 11)
                sp.wait_ge(phase_end, 4 * (ph + PH))
                if l < DEPTH - 1:
                    sp.dma_start(x_mid, x_sb[:]).then_inc(sem("x_saved"), 16)
                    sp.wait_ge(sem("x_saved"), 16)
                else:
                    sp.dma_start(a["out"][0].rearrange("(t p) n -> p t n", p=P), x_sb[:, 0:LT, :]).then_inc(sem("stored"), 16)
                    sp.wait_ge(sem("stored"), 16)

        @block.gpsimd
        def _(pool):
            w_hi_ready, w_lo_ready, w_used = sem("w_hi_ready"), sem("w_lo_ready"), sem("w_used")
            own = Chain(pool, sem("pool_steps"))
            own.did(pool.memset(eps_t[:], EPS))
            own.did(pool.memset(ones[:], 1.0))
            pool.memset(zeros[:], 0.0).then_inc(sem("zero_tile"), 1)
            pool.drain().then_inc(w_lo_ready, 2)

            def low_parts(first, chunks):
                with pool.Fori(0, chunks // 2) as i:
                    for j in range(2):
                        pool.wait_ge(w_hi_ready, i * 2 + (first + j + 1))
                        pool.wait_ge(w_used, i * 2 + (first + j + 1))
                        pool.tensor_tensor(w_lo[:, j, :], w_raw[:, j, :], w_hi[:, j, :].bitcast(F32),
                                           ALU.subtract).then_inc(w_lo_ready, 1)

            def delta(l):
                for k in range(NT):
                    for d in range(2):
                        t, g = TILES[d][k], 2 * k + d
                        if g == 0:
                            pool.wait_ge(sem("gates"), before(l, "gates") + 1)
                            pool.wait_ge(sem("qk_normed"), before(l, "qk_normed") + NT)
                        if k:
                            pool.wait_ge(sem("group_done"), before(l, "group_done") + g - 1)
                            pool.wait_ge(sem("st_ready_d"), before(l, "st_ready_d") + g - 1)
                        if g:
                            pool.wait_ge(sem("egi"), before(l, "egi") + 2 * g)
                        gb = graw[:, t, 8 * d:8 * d + 8].unsqueeze(2).to_broadcast([P, H, C])
                        pool.tensor_tensor(ra[d][:], bmask[d].unsqueeze(1).to_broadcast([P, H, C]), gb, ALU.mult).then_inc(sem("ra"), 1)
                        pool.tensor_tensor(rbb[d][:], bmask[2 + d].unsqueeze(1).to_broadcast([P, H, C]), gb, ALU.mult).then_inc(sem("ra"), 1)
                        pool.tensor_copy(xtc[d][:], ti.unsqueeze(1).to_broadcast([P, H, C])).then_inc(sem("ra"), 1)
                        pool.tensor_copy(xtb[d][:].rearrange("p h a b -> p h (a b)"),
                                         ident.unsqueeze(1).to_broadcast([P, H, P])).then_inc(sem("ra"), 1)
                        nb = nbe[:, t, 8 * d:8 * d + 8].unsqueeze(2).to_broadcast([P, H, C])
                        pool.wait_ge(sem("exps"), before(l, "exps") + 2 * g + 2)
                        own.did(pool.tensor_tensor(e1[d][:], e1[d][:], nb, ALU.mult))
                        pool.tensor_tensor(e2[d][:], e2[d][:], bmask[2 + d].unsqueeze(1).to_broadcast([P, H, C]), ALU.mult).then_inc(sem("em"), 1)
                        own.wait()
                        pool.tensor_tensor(e1[d][:], e1[d][:], bmask[d].unsqueeze(1).to_broadcast([P, H, C]), ALU.mult).then_inc(sem("em"), 1)
                        pool.wait_ge(sem("diffs"), before(l, "diffs") + 2 * g + 2)
                        kk = qkv[:, t, W:2 * W].rearrange("p (h c) -> p h c", h=H)
                        qq = qkv[:, t, 0:W].rearrange("p (h c) -> p h c", h=H)
                        pool.tensor_tensor(ra[d][:], kk, nbec[:, d, t, :].unsqueeze(2).to_broadcast([P, H, C]), ALU.mult).then_inc(sem("kq"), 1)
                        pool.tensor_tensor(rbb[d][:], qq, e_cum[:, d, t, :].unsqueeze(2).to_broadcast([P, H, C]), ALU.mult).then_inc(sem("kq"), 1)
                        if k:
                            pool.wait_ge(sem("chained"), before(l, "chained") + 4 * k - 1 + d)
                        pool.wait_ge(sem("kq"), before(l, "kq") + 2 * g + 2)
                        for c in range(2):
                            tot = e_tot[64:128, c, t, 8 * d:8 * d + 8].unsqueeze(2).to_broadcast([64, H, C])
                            pool.tensor_tensor(st_b[d][64:128, c, :, 64:128], ti[64:128].unsqueeze(1).to_broadcast([64, H, C]), tot, ALU.mult).then_inc(sem("egi"), 1)

            for l in range(DEPTH):
                ph, base = l * PH, l * CHUNKS
                phase_ends(pool, True, ph + 1)
                low_parts(base, 28)
                phase_ends(pool, True, ph + 2)
                phase_ends(pool, True, ph + 3)
                delta(l)
                phase_ends(pool, True, ph + 4)
                low_parts(base + 28, 8)
                phase_ends(pool, True, ph + 5)
                phase_ends(pool, True, ph + 6)
                low_parts(base + 36, 3 * FT)
                phase_ends(pool, True, ph + 7)

        @block.tensor
        def _(pe):
            w_lo_ready, w_used = sem("w_lo_ready"), sem("w_used")
            al = [sem(f"ada_landed{i}") for i in range(2)]
            pe.drain().then_inc(w_used, 2)
            pe.drain().then_inc(sem("ada_used"), 2)
            pe.wait_ge(sem("consts"), 16 * (4 + 2 * DEPTH))
            pe.wait_ge(sem("pool_steps"), 2)

            def spans(l):
                return [(0, 0, LAT)] if lat_only(l) else [(0, 0, LAT), (1, LAT, CTX)]

            def column_tile(slot, bank, sp_):
                for b, c0, n in sp_:
                    for k in range(KT):
                        wk = slice(k * P, k * P + P)
                        o = ps[:, bank + b, 0:n]
                        pe.matmul(o, w_hi[:, slot, wk], h_hi[:, k, c0:c0 + n], start=(k == 0), stop=False)
                        pe.matmul(o, w_hi[:, slot, wk], h_lo[:, k, c0:c0 + n], start=False, stop=False)
                        last = pe.matmul(o, w_lo[:, slot, wk], h_hi[:, k, c0:c0 + n], start=False, stop=(k == KT - 1))
                last.then_inc(w_used, 1)

            def row_chunk(n, hi, lo, tiles, first, last_, banks=0):
                pe.wait_ge(w_lo_ready, n + 3)
                s = n % 2
                for kk in range(2):
                    rhs_h, rhs_l = w_hi[:, s, kk * 512:kk * 512 + 512], w_lo[:, s, kk * 512:kk * 512 + 512]
                    for t in range(tiles):
                        o = ps[:, banks + t, :]
                        pe.matmul(o, hi(kk, t), rhs_h, start=(first and kk == 0), stop=False)
                        pe.matmul(o, hi(kk, t), rhs_l, start=False, stop=False)
                        m = pe.matmul(o, lo(kk, t), rhs_h, start=False, stop=(last_ and kk == 1))
                m.then_inc(w_used, 1)

            def vectors(l):
                pe.wait_ge(sem("rows"), before(l, "rows") + 16 * 11)
                pe.transpose(ps[:, 0, 0:P], row_ffn[:], ident).then_inc(sem("vec_t"), 1)
                pe.transpose(ps[:, 1, 0:121], row_vec[0:121, :], ident[0:121, 0:121]).then_inc(sem("vec_t"), 1)
                if l == 0:
                    pe.transpose(ps[:, 2, 0:16], row_c[:], ident[0:16, 0:16]).then_inc(sem("vec_t"), 1)
                    pe.wait_ge(sem("cond_ready"), 1)
                    pe.wait_ge(sem("ada_first"), 64)
                    for u in range(4):
                        for half in range(2):
                            modulation(ps[0:2, 4 + u, :], ada_first[u], half)
                    pe.wait_ge(sem("mod_rows"), 4)
                    for u in range(4):
                        m = mod_columns(ps[:, 3, 8 * u:8 * u + 8], mod_first[:, u])
                    m.then_inc(sem("mods_done"), 1)

            def modulation(o, w, half):
                cc = cond[:].rearrange("p (s k) -> p k s", s=2)
                for k in range(half * KT // 2, (half + 1) * KT // 2):
                    m = pe.matmul(o, cc[:, k, :], w[:, k, :], start=(k == 0), stop=(k == KT - 1))
                if half:
                    m.then_inc(sem("ada_used"), 1)

            def mod_columns(o, rows_):
                for i in range(4):
                    m = pe.transpose(o[:, 2 * i:2 * i + 2], rows_[:, i * P:i * P + P], ident[0:2, 0:2])
                return m

            def hidden(l, which):
                s = sem(f"hid_t{which}")
                tiles = LT if (which and lat_only(l)) else NT
                for k in range(KT):
                    for b, t0, t1 in ((0, 0, LT), (1, LT, tiles)):
                        if k >= 2:
                            pe.wait_ge(sem(f"hid_v{which}"), before(l, f"hid_v{which}") + (k - 1) * (2 if tiles == NT else 1))
                        for t in range(t0, t1):
                            if k == 0:
                                pe.wait_ge(sem(f"normed{which}"), before(l, f"normed{which}") + t + 1)
                            m = pe.transpose(ps[:, 2 * (k % 2) + b, (t - t0) * P:(t - t0 + 1) * P], xn[:, t, k * P:k * P + P], ident)
                        if t1 > t0:
                            m.then_inc(s, 1)

            def project(l):
                base = l * CHUNKS
                free = sem("proj_free")
                sp_ = [(0, 0, LAT), (1, LAT, CTX)]
                pe.wait_ge(sem("h_ready0"), before(l, "h_ready0") + 2 * KT)
                for t in range(8):
                    pe.wait_ge(w_lo_ready, base + t + 3)
                    if t >= 2:
                        pe.wait_ge(free, t - 1)
                    column_tile(t % 2, 2 * (t % 2), sp_)

                def turn(t, r):
                    pe.wait_ge(sem("conv"), before(l, "conv") + t + 1)
                    pe.wait_ge(sem("qkv_out"), before(l, "qkv_out") + t + 1)
                    for tt in range(NT):
                        m = pe.transpose(ps[:, 4 + 2 * r + tt // 4, (tt % 4) * P:(tt % 4 + 1) * P], cvs[:, r, col(tt)], ident)
                    m.then_inc(sem("turned"), 1)

                def pair(i, first):
                    for j in range(2):
                        pe.wait_ge(w_lo_ready, i * 2 + (base + 8 + j + 3))
                        if first:
                            pe.wait_ge(free, 7 + j)
                        else:
                            pe.wait_ge(sem("taps"), before(l, "taps") + i * 2 + (j - 1))
                        column_tile(j, 2 * j, sp_)
                        if not (first and j == 0):
                            turn(i * 2 + (j - 1), (j - 1) % 2)
                pair(0, True)
                with pe.Fori(1, 6) as i:
                    pair(i, False)
                turn(11, 1)
                pe.wait_ge(sem("taps"), before(l, "taps") + 12)
                pe.wait_ge(sem("qkv_out"), before(l, "qkv_out") + 14)
                for j in range(4):
                    row_chunk(base + 20 + j, lambda kk, t: h_hi[:, 2 * j + kk, col(t)],
                              lambda kk, t: h_lo[:, 2 * j + kk, col(t)], NT, j == 0, j == 3)
                pe.wait_ge(sem("bd_split"), before(l, "bd_split") + 1)
                for t in range(NT):
                    for k in range(KT):
                        o = ps[:, 7, 32 * t:32 * t + 32]
                        pe.matmul(o, h_hi[:, k, col(t)], bd_hi[:, k, :], start=(k == 0), stop=False)
                        pe.matmul(o, h_hi[:, k, col(t)], bd_lo[:, k, :], start=False, stop=False)
                        m = pe.matmul(o, h_lo[:, k, col(t)], bd_hi[:, k, :], start=False, stop=(k == KT - 1))
                m.then_inc(sem("bd_done"), 1)
                pe.wait_ge(sem("v_out_a"), before(l, "v_out_a") + 3)
                pe.wait_ge(sem("v_out_d"), before(l, "v_out_d") + 3)
                for j in range(4):
                    row_chunk(base + 24 + j, lambda kk, t: h_hi[:, 2 * j + kk, col(t)],
                              lambda kk, t: h_lo[:, 2 * j + kk, col(t)], NT, j == 0, j == 3)

            def attend(l):
                items = [(h, u) for h in range(H) for u in range(LT if lat_only(l) else NT)]
                per = LT if lat_only(l) else NT
                kt4 = lambda hp_, pr: na_k[64 * hp_:64 * hp_ + 64, pr, 0:LAT].rearrange("p (j n) -> p j n", j=4)

                def scores(n):
                    h, u = items[n]
                    s_, e_ = h % 2, h // 2
                    q = na_q[64 * s_:64 * s_ + 64, e_, u * P:u * P + P]
                    b = n % 2
                    if n >= 2:
                        pe.wait_ge(sem("exped"), before(l, "exped") + n - 1)
                    kc = na_k[64 * s_:64 * s_ + 64, e_, LAT:TOK]
                    if u < LT:
                        win = kt4(s_, e_)[:, u:u + 2, :] if u < 3 else kt4(s_, e_)[:, 0:4:3, :]
                        pe.matmul(ps[:, b, 0:256], q, win, start=True, stop=True)
                        pe.matmul(ps[:, b, 256:512], q, kc, start=True, stop=True).then_inc(sem("scored"), 1)
                    else:
                        pe.matmul(ps[:, b, 256:512], q, kc, start=True, stop=True).then_inc(sem("scored"), 1)

                def turn(n):
                    h, u = items[n]
                    b = 2 + n % 2
                    pe.wait_ge(sem("probs"), before(l, "probs") + n + 1)
                    if l == 0 and n % 2 and 3 <= n < 2 * UNITS + 3:
                        v = (n - 3) // 2
                        pe.wait_ge(sem("mod_rows"), 4 + v + 1)
                        pairs = h // 2 if h % 2 or u >= 5 else h // 2 - 1
                        if pairs > 0:
                            pe.wait_ge(sem("o_out"), pairs)
                        mod_columns(ps[:, 6, 256 + 8 * v:264 + 8 * v], mod_row[:]).then_inc(sem("mods_done"), 1)
                    if n >= 2:
                        out = "pt_odd" if n % 2 else "pt_even"
                        pe.wait_ge(sem(out), before(l, out) + n // 2)
                    for w in range(0 if u < LT else 2, 4):
                        m = pe.transpose(ps[:, b, w * P:w * P + P], prob[:, n % 2, w * P:w * P + P], ident)
                    m.then_inc(sem("p_turned"), 1)

                def values(h):
                    s_, e_, r = h % 2, h // 2, h % 2
                    pe.wait_ge(sem("pt_even"), before(l, "pt_even") + per * (h + 1) // 2)
                    pe.wait_ge(sem("pt_odd"), before(l, "pt_odd") + per * (h + 1) // 2)
                    if h >= 4 and h % 2 == 0:
                        pe.wait_ge(sem("o_out"), before(l, "o_out") + e_ - 1)
                    o = ps[64 * s_:64 * s_ + 64, 4 + e_ % 2, :]
                    vh = lambda t: na_v[:, t, 64 * h:64 * h + 64]
                    for e in range(2):
                        pe.matmul(o, vh(4 + e), pt[:, r, 8 + 4 * e:12 + 4 * e, :], start=(e == 0), stop=False, skip_group_check=True)
                    o4 = o.rearrange("p (u n) -> p u n", u=4)
                    outs = [o4[:, 0:4:3, :], o4[:, 0:2, :], o4[:, 1:3, :], o4[:, 2:4, :]]
                    for j in range(4):
                        m = pe.matmul(outs[j], vh(j), pt[:, r, 2 * j:2 * j + 2, :], start=False, stop=(j == 3), skip_group_check=True)
                    if not lat_only(l):
                        if e_ and s_ == 0:
                            pe.wait_ge(sem("o_out"), before(l, "o_out") + e_)
                        o = ps[64 * s_:64 * s_ + 64, 6, 0:256]
                        for e in range(2):
                            m = pe.matmul(o, vh(4 + e), pt[:, r, 16 + 2 * e:18 + 2 * e, :], start=(e == 0), stop=(e == 1))
                    m.then_inc(sem("valued"), 1)

                pe.wait_ge(sem("rb_masked"), before(l, "rb_masked") + 1)
                pe.wait_ge(sem("v_sorted"), 16 * LT * (l + 1))
                scores(0)
                for n in range(len(items)):
                    if n + 1 < len(items):
                        scores(n + 1)
                    if l == 0 and n < 2 * UNITS:
                        v = n // 2
                        pe.wait_ge(al[v % 2], 16 * (v // 2 + 1))
                        modulation(ps[64 * (v % 2):64 * (v % 2) + 2, 7, :], ada_ring[:, v % 2], n % 2)
                    turn(n)
                    if n % per == 2 and n >= per:
                        values(n // per - 1)
                values(H - 1)

            def delta_prep(l):
                pe.wait_ge(sem("decays"), before(l, "decays") + 1)
                gd = lambda d: graw[:, :, 8 * d:8 * d + 8]
                for d in range(2):
                    pe.matmul(ps[:, 4, 48 * d:48 * d + 48], amask[(LE, GE)[d]], gd(d), start=True, stop=True)
                    pe.matmul(ps[:, 4, 96 + 48 * d:144 + 48 * d], amask[(GT, LT_)[d]], gd(d), start=True, stop=True)
                for c in range(2):
                    m = pe.matmul(ps[:, 5, 96 * c:96 * c + 96], onec[c], graw[:].rearrange("p t n -> p (t n)"), start=True, stop=True)
                m.then_inc(sem("sums"), 1)
                for t in range(NT):
                    pe.wait_ge(sem("qk_normed"), before(l, "qk_normed") + t + 1)
                    if t >= 2:
                        pe.wait_ge(sem("qk_out"), before(l, "qk_out") + t - 1)
                    for i in range(8):
                        m = pe.transpose(ps[:, 2 * (t % 2) + i // 4, (i % 4) * P:(i % 4 + 1) * P], qkv[:, t, i * P:i * P + P], ident)
                    m.then_inc(sem("qk_turned"), 1)
                pe.wait_ge(sem("qk_out"), before(l, "qk_out") + NT)
                pe.wait_ge(sem("gates"), before(l, "gates") + 1)

            def group_start(l, k, d):
                g, t, b = 2 * k + d, TILES[d][k], 2 * d
                pe.wait_ge(sem("ra"), before(l, "ra") + 4 * g + 4)
                if k:
                    pe.wait_ge(sem("w_out_q"), before(l, "w_out_q") + g - 1)
                pe.matmul(ps[:, b, :], amask[(LE, GE)[d]], ra[d][:].rearrange("p h c -> p (h c)"), start=True, stop=True).then_inc(sem("diffs"), 1)
                pe.matmul(ps[:, b + 1, :], amask[(GT, LT_)[d]], rbb[d][:].rearrange("p h c -> p (h c)"), start=True, stop=True).then_inc(sem("diffs"), 1)
                pe.wait_ge(sem("exps"), before(l, "exps") + 2 * g + 2)
                for h in range(H):
                    s_, e_ = h % 2, h // 2
                    for c in range(2):
                        tk = slice(t * P + 64 * c, t * P + 64 * c + 64)
                        kk = k_t[64 * s_:64 * s_ + 64, e_, tk]
                        pe.matmul(ps[64 * c:64 * c + 64, b + s_, 64 * e_:64 * e_ + 64], kk, kk, start=True, stop=True)
                        m = pe.matmul(ps[64 * c:64 * c + 64, b + s_, 256 + 64 * e_:320 + 64 * e_], kk,
                                      q_t[64 * s_:64 * s_ + 64, e_, tk], start=True, stop=True)
                m.then_inc(sem("gram"), 1)

            def level_z(l, k, d, s):
                n = (2 * k + d) * LEVELS + s
                if s == 0:
                    pe.wait_ge(sem("m_ready"), before(l, "m_ready") + 2 * k + d + 1)
                    pe.wait_ge(sem("gram_out"), before(l, "gram_out") + 2 * k + d + 1)
                else:
                    pe.wait_ge(sem(f"xt_new{d}"), before(l, f"xt_new{d}") + k * LEVELS + s)
                    pe.wait_ge(sem(f"xq_new{d}"), before(l, f"xq_new{d}") + k * (LEVELS - 1) + s)
                for h in range(H):
                    m = pe.matmul(ps[64 * (h % 2):64 * (h % 2) + 64, 2 * d, P * (h // 2):P * (h // 2) + P], e1[d][:, h, :],
                                  xtb[d][:, h, :, :].rearrange("p a b -> p (a b)"), start=True, stop=True)
                m.then_inc(sem(f"z_done{d}"), 1)

            def level_p(l, k, d, s):
                i = k * LEVELS + s
                pe.wait_ge(sem(f"zb_a{d}"), before(l, f"zb_a{d}") + i + 1)
                pe.wait_ge(sem(f"zb_d{d}"), before(l, f"zb_d{d}") + i + 1)
                for e_ in range(HP):
                    for c in range(2):
                        lhs = (xq0 if s == 0 else xq[d][:, e_, :])[:, 64 * c:64 * c + 64]
                        m = pe.matmul(ps[64 * c:64 * c + 64, 2 * d + 1, P * e_:P * e_ + P], lhs,
                                      zb[d][:, e_, c, :, :].rearrange("p a b -> p (a b)"), start=True, stop=True)
                m.then_inc(sem(f"p_done{d}"), 1)

            def level_t(l, k, d, s):
                pe.wait_ge(sem(f"xt_new{d}"), before(l, f"xt_new{d}") + k * LEVELS + s + 1)
                for e_ in range(HP):
                    m = pe.transpose(ps[:, 2 * d, P * e_:P * e_ + P], xtc[d][:, 2 * e_:2 * e_ + 2, :].rearrange("p a b -> p (a b)"), ident)
                m.then_inc(sem(f"xt_turned{d}"), 1)

            def group_end(l, k, d):
                g = 2 * k + d
                pe.wait_ge(sem(f"xt_new{d}"), before(l, f"xt_new{d}") + k * LEVELS + LEVELS)
                pe.wait_ge(sem("kq"), before(l, "kq") + 2 * g + 2)
                for h in range(H):
                    pe.matmul(ps[64 * (h % 2):64 * (h % 2) + 64, 2 * d, P * (h // 2):P * (h // 2) + P], ra[d][:, h, :],
                              xtb[d][:, h, :, :].rearrange("p a b -> p (a b)"), start=True, stop=True)
                for e_ in range(HP):
                    m = pe.transpose(ps[:, 2 * d + 1, P * e_:P * e_ + P], rbb[d][:, 2 * e_:2 * e_ + 2, :].rearrange("p a b -> p (a b)"), ident)
                m.then_inc(sem("group_done"), 1)

            def chain_a(l, n, d):
                k, c = n // 2, (n % 2 if d == 0 else 1 - n % 2)
                i = 2 * n + d
                if n % 2 == 0:
                    pe.wait_ge(sem("st_ready_a"), before(l, "st_ready_a") + 2 * (2 * k + d) + 2)
                    pe.wait_ge(sem("st_ready_d"), before(l, "st_ready_d") + 2 * k + d + 1)
                    pe.wait_ge(sem("egi"), before(l, "egi") + 2 * (2 * k + d) + 2)
                if n:
                    pe.wait_ge(sem(f"state{d}"), before(l, f"state{d}") + n)
                for h in range(H):
                    m = pe.matmul(ps[0:64, 4 + d, 64 * h:64 * h + 64], st_a[d][:, c, h, :], mv_a[d][:, c, h, :], start=True, stop=True)
                m.then_inc(sem(f"vnew_done{d}"), 1)

            def chain_b(l, n, d):
                c = n % 2 if d == 0 else 1 - n % 2
                pe.wait_ge(sem(f"vnew{d}"), before(l, f"vnew{d}") + n + 1)
                if n:
                    pe.wait_ge(sem(f"o_added{d}"), before(l, f"o_added{d}") + n)
                for h in range(H):
                    m = pe.matmul(ps[:, 6 + d, 64 * h:64 * h + 64], st_b[d][:, c, h, :], mv_b[d][:, h, :], start=True, stop=True)
                m.then_inc(sem("chained"), 1)

            def delta(l):
                for k in range(NT):
                    for d in range(2):
                        group_start(l, k, d)
                    for s in range(LEVELS):
                        for d in range(2):
                            level_z(l, k, d, s)
                        for d in range(2):
                            level_p(l, k, d, s)
                        if s < LEVELS - 1:
                            for d in range(2):
                                level_t(l, k, d, s)
                    for d in range(2):
                        group_end(l, k, d)
                    for n in (2 * k, 2 * k + 1):
                        for d in range(2):
                            chain_a(l, n, d)
                        for d in range(2):
                            chain_b(l, n, d)

            def mix_out(l):
                tiles = LT if lat_only(l) else NT
                for e_ in range(HP):
                    for b, t0, t1 in ((0, 0, LT), (1, LT, tiles)):
                        for t in range(t0, t1):
                            pe.wait_ge(sem("o_normed"), before(l, "o_normed") + t + 1)
                        if e_ >= 2:
                            pe.wait_ge(sem("ov_out"), before(l, "ov_out") + e_ - 1)
                        for t in range(t0, t1):
                            m = pe.transpose(ps[:, 2 * (e_ % 2) + b, (t - t0) * P:(t - t0 + 1) * P], on[:, t, e_ * P:e_ * P + P], ident)
                    m.then_inc(sem("o_turned"), 1)
                pe.wait_ge(sem("ov_out"), before(l, "ov_out") + HP)
                pe.wait_ge(sem("o_split"), before(l, "o_split") + 2 * HP)
                base = l * CHUNKS + 28
                for half in range(2):
                    if half:
                        pe.wait_ge(sem("y_out_a0"), before(l, "y_out_a0") + tiles // 2)
                        pe.wait_ge(sem("y_out_d0"), before(l, "y_out_d0") + tiles // 2)
                    for j in range(4):
                        row_chunk(base + 4 * half + j, lambda kk, t: o_hi[:, 2 * j + kk, col(t)],
                                  lambda kk, t: o_lo[:, 2 * j + kk, col(t)], tiles, j == 0, j == 3)

            def gate_rows(l, which):
                n = 2 if lat_only(l) else 4
                for i in range(n):
                    pe.wait_ge(sem(f"gdiag{which}"), before(l, f"gdiag{which}") + i + 1)
                    if i >= 2:
                        pe.wait_ge(sem(f"gate_out{which}"), before(l, f"gate_out{which}") + i - 1)
                    pe.matmul(ps[:, 6 + i % 2, :], ones[:], (gdiag2 if which else gdiag)[:], start=True, stop=True).then_inc(sem(f"gate_done{which}"), 1)

            def ffn_up(l):
                base = l * CHUNKS + 36
                pe.wait_ge(sem("h_ready1"), before(l, "h_ready1") + KT * (1 if lat_only(l) else 2))
                free = sem("up_taps")
                with pe.Fori(0, FT // 2) as i:
                    for j in range(2):
                        for gv in range(2):
                            pe.wait_ge(w_lo_ready, i * 4 + (base + 2 * j + gv + 3))
                            pe.wait_ge(free, i * 4 + (2 * j + gv + 1))
                            column_tile(gv, 4 * j + 2 * gv, spans(l))

            def ffn_down(l):
                base = l * CHUNKS + 36 + 2 * FT
                tiles = LT if lat_only(l) else NT
                used = sem("g_used")
                for half in range(2):
                    if half:
                        pe.wait_ge(sem("y_out_a1"), before(l, "y_out_a1") + tiles // 2)
                        pe.wait_ge(sem("y_out_d1"), before(l, "y_out_d1") + tiles // 2)
                    for j in range(11):
                        n = base + 11 * half + j
                        pe.wait_ge(w_lo_ready, n + 3)
                        s = n % 2
                        for kk in range(2):
                            q = 22 * half + 2 * j + kk
                            pe.wait_ge(sem("g_split"), before(l, "g_split") + q + 1)
                            rh, rl = w_hi[:, s, kk * 512:kk * 512 + 512], w_lo[:, s, kk * 512:kk * 512 + 512]
                            for t in range(tiles):
                                o = ps[:, t, :]
                                pe.matmul(o, g_hi[:, kk, col(t)], rh, start=(j == 0 and kk == 0), stop=False)
                                pe.matmul(o, g_hi[:, kk, col(t)], rl, start=False, stop=False)
                                m = pe.matmul(o, g_lo[:, kk, col(t)], rh, start=False, stop=(j == 10 and kk == 1))
                            if kk == 0:
                                m.then_inc(used, 1)
                            else:
                                m.then_inc(w_used, 1)

            for l in range(DEPTH):
                ph = l * PH
                vectors(l)
                hidden(l, 0)
                phase_ends(pe, True, ph + 1)
                project(l)
                phase_ends(pe, True, ph + 2)
                attend(l)
                phase_ends(pe, True, ph + 3)
                delta_prep(l)
                delta(l)
                phase_ends(pe, True, ph + 4)
                mix_out(l)
                gate_rows(l, 0)
                phase_ends(pe, True, ph + 5)
                hidden(l, 1)
                phase_ends(pe, True, ph + 6)
                ffn_up(l)
                ffn_down(l)
                gate_rows(l, 1)
                phase_ends(pe, True, ph + 7)

        @block.scalar
        def _(act):
            own = Chain(act, sem("act_steps"))
            wl = [sem("w_landed0"), sem("w_landed1")]
            w_hi_ready, w_used = sem("w_hi_ready"), sem("w_used")
            act.wait_ge(sem("consts"), 16 * (4 + 2 * DEPTH))
            act.wait_ge(sem("pool_steps"), 2)

            def high(n, slot, landed):
                act.wait_ge(wl[slot], landed)
                act.wait_ge(w_used, n + 1)
                act.activation(w_hi[:, slot, :], w_raw[:, slot, :], ACT.Copy).then_inc(w_hi_ready, 1)

            def high_at(n):
                high(n, n % 2, 16 * (n // 2 + 1))

            def high_loop(i, base, j, per):
                high(i * per + (base + j), j % 2, i * (8 * per) + 16 * ((base + j) // 2 + 1))

            def vectors(l):
                if l == 0:
                    act.wait_ge(sem("vec_t"), before(l, "vec_t") + 3)
                    act.activation(cond[:], ps[:, 2, 0:16], ACT.Silu).then_inc(sem("cond_ready"), 1)

            def sums(l, name, src, tiles, off, jk):
                for t in range(tiles):
                    own.did(act.activation(jk, src[:, t, :], ACT.Square, accum_out=stat[:, off + t:off + t + 1]))
                    own.wait()
                act.activation(stat[:, off + 8:off + 8 + tiles], stat[:, off:off + tiles], ACT.Sqrt, bias=eps_t[:],
                               scale=1.0 / D).then_inc(sem(name), 1)

            def bias_begin():
                act.wait_ge(sem("zero_tile"), 1)
                for l in range(DEPTH):
                    act.dma_start(bias_wide[l].rearrange("q c r k -> (q c) (r k)").rearrange("p (a n) -> p a n", n=512),
                                  zeros[:].unsqueeze(1).to_broadcast([P, 6, 512])).then_inc(sem("bias_begun"), 16)
                    for q in range(ROWS):
                        act.dma_start(bias_rows[l, q].rearrange("(h r) c -> h r c", h=H), a["rpb"][l, :, 7 - q:15 - q, :]).then_inc(sem("bias_begun"), 16)

            def bias_spread():
                act.wait_ge(sem("bias_begun"), 16 * DEPTH * (ROWS + 1))
                for l in range(DEPTH):
                    for q in range(ROWS):
                        wide = bass.AP(bias_wide.tensor, (l * ROWS + q) * 16 * 64 * 48 + 1, [[64 * 48 + 1, 16], [48, 64], [1, 31]])
                        act.dma_start(wide, bias_rows[l, q].unsqueeze(0).to_broadcast([16, 64, 31])).then_inc(sem("bias_spread"), 16)

            def norm(l, which, tiles):
                if which == 0 and l == 0:
                    act.wait_ge(sem("x_landed"), 32)
                sums(l, f"rms{which}", x_sb, tiles, 0, v_junk)
                if which == 0 and l == 0:
                    bias_begin()
                n = 0
                for k in range(KT):
                    for b, c0, w in ((0, 0, LAT), (1, LAT, CTX)):
                        if b and tiles == LT:
                            continue
                        n += 1
                        act.wait_ge(sem(f"hid_t{which}"), before(l, f"hid_t{which}") + n)
                        if n == 1:
                            act.wait_ge(sem("mods"), before(l, "mods") + 1)
                        r = n % 2
                        if n > 2:
                            act.wait_ge(sem(f"h_ready{which}"), before(l, f"h_ready{which}") + n - 2)
                        act.activation(v_ring[:, r, 0:w], ps[:, 2 * (k % 2) + b, 0:w], ACT.Identity,
                                       scale=sc_pre[:, which, k, b:b + 1], bias=mod[:, (3 * which) * KT + k, b:b + 1]).then_inc(sem(f"hid_v{which}"), 1)
                        act.wait_ge(sem(f"hid_v{which}"), before(l, f"hid_v{which}") + n)
                        act.activation(h_hi[:, k, c0:c0 + w], v_ring[:, r, 0:w], ACT.Copy).then_inc(sem(f"hid_h{which}"), 1)

            def project(l):
                base = l * CHUNKS
                free = sem("proj_free")
                high_at(base)
                if l == 0:
                    bias_spread()
                own.did(act.activation(bd_hi[:], bd_raw[:], ACT.Copy))
                act.drain().then_inc(sem("bd_h"), 1)
                for t in range(8):
                    high_at(base + t + 1)
                    act.wait_ge(w_used, base + t + 3)
                    b = 2 * (t % 2)
                    e = t % 4
                    if t < 4:
                        src = ps[:, b, :].rearrange("p (r c) -> p r c", c=GRID)
                        act.activation(na_q[:, e, 0:384].rearrange("p (u r c) -> p u r c", u=3, r=ROWS),
                                       src[:, :, 8:56].rearrange("p r (u c) -> p u r c", c=16), ACT.Copy, scale=DH ** -0.5)
                        for s_ in range(2):
                            act.activation(na_q[:, e, 384:512].rearrange("p (r s c) -> p s r c", r=ROWS, s=2)[:, s_],
                                           src[:, :, 56 * s_:56 * s_ + 8], ACT.Copy, scale=DH ** -0.5)
                        act.activation(na_q[:, e, LAT:TOK], ps[:, b + 1, 0:CTX], ACT.Copy, scale=DH ** -0.5).then_inc(free, 1)
                    else:
                        act.activation(na_k[:, e, 0:LAT].rearrange("p (j r c) -> p j r c", j=4, r=ROWS),
                                       ps[:, b, :].rearrange("p (r j c) -> p j r c", j=4, c=16), ACT.Copy)
                        act.activation(na_k[:, e, LAT:TOK], ps[:, b + 1, 0:CTX], ACT.Copy).then_inc(free, 1)

                def conv(i, j):
                    high_loop(i, base + 8, j + 1, 2)
                    act.wait_ge(w_used, i * 2 + (base + 8 + j + 3))
                    act.wait_ge(sem("turned"), before(l, "turned") + i * 2 + (j + 1))
                    act.activation(cv[:, j, :], ps[:, 2 * j:2 * j + 2, :].rearrange("p a b -> p (a b)")[:, 0:TOK], ACT.Copy,
                                   scale=vec[l][:, ds(i * 2 + (16 + j), 1)]).then_inc(sem("mid"), 1)
                    act.wait_ge(sem("taps"), before(l, "taps") + i * 2 + (j + 1))
                    act.activation(cvs[:, j, :], cv[:, j, :], ACT.Silu).then_inc(sem("conv"), 1)
                act.drain().then_inc(sem("turned"), 2)
                with act.Fori(0, 6) as i:
                    for j in range(2):
                        conv(i, j)
                for j in range(4):
                    high_at(base + 21 + j)
                act.wait_ge(w_used, base + 23 + 3)
                for t in range(0, NT, 2):
                    act.activation((v_nat if t < LT else na_v)[:, t, :], ps[:, t, :], ACT.Copy).then_inc(sem("v_out_a"), 1)
                for j in range(3):
                    high_at(base + 25 + j)
                act.wait_ge(w_used, base + 27 + 3)
                for t in range(NT):
                    own.did(act.activation(z_sb[:, t, :], ps[:, t, :], ACT.Silu))

            def attend(l):
                tiles = LT if lat_only(l) else NT
                items = [(h, u) for h in range(H) for u in range(tiles)]
                steps = len(items)
                for n in range(steps + 1):
                    if n < steps:
                        h, u = items[n]
                        act.wait_ge(sem("maxed"), before(l, "maxed") + n + 1)
                        if n >= 2:
                            act.wait_ge(sem("p_turned"), before(l, "p_turned") + n - 1)
                        c0 = 0 if u < LT else 256
                        own.did(act.activation(prob[:, n % 2, c0:512], ps[:, n % 2, c0:512], ACT.Exp, bias=stat[:, n % 2:n % 2 + 1],
                                               accum_out=stat[:, 2 + n % 2:3 + n % 2]))
                        act.drain().then_inc(sem("exped"), 1)
                    if n >= 1:
                        h, u = items[n - 1]
                        if n % 2:
                            act.wait_ge(sem("p_turned"), before(l, "p_turned") + n)
                            if h >= 2 and u == 0:
                                act.wait_ge(sem("valued"), before(l, "valued") + h - 1)
                            for dst, src in turned(n - 1, u, h):
                                act.activation(dst, src, ACT.Copy)
                            act.drain().then_inc(sem("pt_even"), 1)
                        if u == 3 and h >= 2 and h % 2 == 0:
                            act.wait_ge(sem("p_turned"), before(l, "p_turned") + n)
                            out_pair(l, h // 2 - 1)
                out_pair(l, HP - 1)

            def out_pair(l, e):
                act.wait_ge(sem("valued"), before(l, "valued") + 2 * e + 2)
                b = 4 + e % 2
                dst = o_t[:, e, 0:LAT].rearrange("p (r c) -> p r c", c=GRID)
                act.activation(dst[:, :, 8:56].rearrange("p r (u c) -> p u r c", c=16),
                               ps[:, b, 0:384].rearrange("p (u r c) -> p u r c", u=3, r=ROWS), ACT.Copy)
                for s_ in range(2):
                    own.did(act.activation(dst[:, :, 56 * s_:56 * s_ + 8],
                                           ps[:, b, 384:512].rearrange("p (r s c) -> p s r c", r=ROWS, s=2)[:, s_], ACT.Copy))
                if not lat_only(l):
                    own.did(act.activation(o_t[:, e, LAT:TOK], ps[:, 6, 0:CTX], ACT.Copy))
                act.drain().then_inc(sem("o_out"), 1)

            def delta_prep(l):
                own.did(act.activation(beta[:], bd[:, :, 0:16], ACT.Sigmoid))
                act.wait_ge(sem("dec_abs"), before(l, "dec_abs") + 1)
                own.did(act.activation(gtmp[:, 1], gtmp[:, 1], ACT.Exp, scale=-1.0))
                own.wait()
                act.activation(gtmp[:, 1], gtmp[:, 1], ACT.Ln, bias=1.0)
                own.did(act.activation(stat2[:, 0:16], al_dt[:, l, 0, :], ACT.Exp))
                act.drain().then_inc(sem("dec_ln"), 1)
                act.wait_ge(sem("sums"), before(l, "sums") + 1)
                for d in range(2):
                    act.activation(e_cum[:, d], ps[:, 4, 48 * d:48 * d + 48].rearrange("p (t h) -> p t h", h=H), ACT.Exp)
                    act.activation(e_tail[:, d], ps[:, 4, 96 + 48 * d:144 + 48 * d].rearrange("p (t h) -> p t h", h=H), ACT.Exp)
                own.did(act.activation(e_tot[:], ps[:, 5, 0:192].rearrange("p (c t h) -> p c t h", c=2, t=NT), ACT.Exp))
                act.drain().then_inc(sem("e_ready"), 1)
                for t in range(NT):
                    if t:
                        act.wait_ge(sem("qk_summed"), before(l, "qk_summed") + t)
                    own.did(act.activation(sq[:], qkv[:, t, 0:2 * W], ACT.Square))
                    act.drain().then_inc(sem("qk_sq"), 1)
                act.wait_ge(sem("qk_summed"), before(l, "qk_summed") + NT)
                act.activation(qk_rt[:], qk_ss[:], ACT.Sqrt, bias=eps_t[:]).then_inc(sem("qk_root"), 1)
                for t in range(NT):
                    act.wait_ge(sem("qk_turned"), before(l, "qk_turned") + t + 1)
                    act.activation(q_t[:, :, col(t)], ps[:, 2 * (t % 2), :].rearrange("p (e n) -> p e n", e=HP), ACT.Copy)
                    own.did(act.activation(k_t[:, :, col(t)], ps[:, 2 * (t % 2) + 1, :].rearrange("p (e n) -> p e n", e=HP), ACT.Copy))
                    act.drain().then_inc(sem("qk_out"), 1)

            def level(l, k, d, s):
                act.wait_ge(sem(f"z_done{d}"), before(l, f"z_done{d}") + k * LEVELS + s + 1)
                act.activation(zb[d][0:64, :, :, 0, :], ps[0:64, 2 * d, :].rearrange("p (e c n) -> p e c n", e=HP, c=2), ACT.Copy).then_inc(sem(f"zb_a{d}"), 1)

            def level_x(l, k, d, s):
                act.wait_ge(sem(f"xt_turned{d}"), before(l, f"xt_turned{d}") + k * (LEVELS - 1) + s + 1)
                act.activation(xq[d][:], ps[:, 2 * d, :].rearrange("p (e n) -> p e n", e=HP), ACT.Copy).then_inc(sem(f"xq_new{d}"), 1)

            def delta(l):
                for k in range(NT):
                    for d in range(2):
                        g = 2 * k + d
                        act.wait_ge(sem("diffs"), before(l, "diffs") + 2 * g + 2)
                        if k:
                            act.wait_ge(sem("group_done"), before(l, "group_done") + g - 1)
                        act.activation(e1[d][:].rearrange("p h c -> p (h c)"), ps[:, 2 * d, :], ACT.Exp).then_inc(sem("exps"), 1)
                        act.activation(e2[d][:].rearrange("p h c -> p (h c)"), ps[:, 2 * d + 1, :], ACT.Exp).then_inc(sem("exps"), 1)
                    for s in range(LEVELS):
                        for d in range(2):
                            level(l, k, d, s)
                        if s < LEVELS - 1:
                            for d in range(2):
                                level_x(l, k, d, s)
                    for d in range(2):
                        g = 2 * k + d
                        act.wait_ge(sem("group_done"), before(l, "group_done") + g + 1)
                        if k:
                            act.wait_ge(sem("chained"), before(l, "chained") + 4 * k)
                        for s_ in range(2):
                            wv = ps[64 * s_:64 * s_ + 64, 2 * d, :].rearrange("p (e c n) -> p c e n", e=HP, c=2)
                            qv = ps[64 * s_:64 * s_ + 64, 2 * d + 1, :].rearrange("p (e c n) -> p c e n", e=HP, c=2)
                            act.activation(st_a[d][64:128, :, s_:H:2, :], wv, ACT.Copy)
                            act.activation(st_b[d][64:128, :, s_:H:2, 0:64], qv, ACT.Copy)
                        act.drain().then_inc(sem("w_out_q"), 1)
                        act.drain().then_inc(sem("st_ready_a"), 2)
                    for n in (2 * k, 2 * k + 1):
                        for d in range(2):
                            act.wait_ge(sem(f"vnew_done{d}"), before(l, f"vnew_done{d}") + n + 1)
                            act.activation(mv_b[d][0:64].rearrange("p h c -> p (h c)"), ps[0:64, 4 + d, :], ACT.Copy).then_inc(sem(f"vnew{d}"), 1)
                        for d in range(2):
                            c = n % 2 if d == 0 else 1 - n % 2
                            act.wait_ge(sem("chained"), before(l, "chained") + 2 * n + d + 1)
                            src = ps[64:128, 6 + d, :].rearrange("p (h c) -> p h c", h=H)
                            act.activation(mv_b[d][64:128], src, ACT.Copy)
                            act.activation(mv_a[d][64:128, 1 - c], src, ACT.Copy).then_inc(sem(f"state{d}"), 1)

            def mix_out(l):
                tiles = LT if lat_only(l) else NT
                high_at(l * CHUNKS + 28)
                for t in range(tiles):
                    if t:
                        act.wait_ge(sem("o_summed"), before(l, "o_summed") + t)
                    own.did(act.activation(osq[:], o_g[:, t, :], ACT.Square))
                    act.drain().then_inc(sem("o_sq"), 1)
                act.wait_ge(sem("o_summed"), before(l, "o_summed") + tiles)
                act.activation(o_rt[:, 0:tiles * H], o_ss[:, 0:tiles * H], ACT.Sqrt, bias=eps_t[:], scale=1.0 / DH).then_inc(sem("o_root"), 1)
                n = tiles * P
                for e in range(HP):
                    act.activation(o_hi[:, e, 0:n], o_t[:, e, 0:n], ACT.Copy).then_inc(sem("o_high"), 1)
                for e in range(HP):
                    act.wait_ge(sem("o_turned"), before(l, "o_turned") + e + 1)
                    if e >= 2:
                        act.wait_ge(sem("o_split"), before(l, "o_split") + HP + e - 1)
                    for b, c0, w in ((0, 0, LAT), (1, LAT, CTX)):
                        if b and tiles == LT:
                            continue
                        own.did(act.activation(ov[:, e % 2, c0:c0 + w], ps[:, 2 * (e % 2) + b, 0:w], ACT.Copy, scale=vec[l][:, 120:121]))
                    act.drain().then_inc(sem("ov_out"), 1)
                    own.wait()
                    act.activation(o_hi[:, HP + e, 0:n], ov[:, e % 2, 0:n], ACT.Copy).then_inc(sem("o_high"), 1)

            def gate_rows(l, which, gb):
                for i in range(2 if lat_only(l) else 4):
                    act.wait_ge(sem(f"gate_done{which}"), before(l, f"gate_done{which}") + i + 1)
                    act.activation(gb[:, i // 2, 512 * (i % 2):512 * (i % 2) + 512], ps[:, 6 + i % 2, :], ACT.Copy).then_inc(sem(f"gate_out{which}"), 1)

            def ffn_up(l):
                base = l * CHUNKS + 36
                n = LAT if lat_only(l) else TOK
                with act.Fori(0, FT // 2) as i:
                    for j in range(2):
                        for gv, dst in ((0, cg), (1, cw)):
                            high_loop(i, base, 2 * j + gv + 1, 4)
                            act.wait_ge(w_used, i * 4 + (base + 2 * j + gv + 3))
                            act.wait_ge(sem("g_done"), before(l, "g_done") + i * 2 + (j + 1))
                            src = ps[:, 4 * j + 2 * gv:4 * j + 2 * gv + 2, :].rearrange("p a b -> p (a b)")[:, 0:n]
                            act.activation(dst[:, j, 0:n], src, ACT.Copy,
                                           scale=taps[l][:, ds(i * 2 + (2 * FT + gv * FT + j), 1)]).then_inc(sem("up_mid"), 1)
                        act.wait_ge(sem("up_taps"), before(l, "up_taps") + i * 4 + (2 * j + 5))
                        act.activation(cg[:, j, 0:n], cg[:, j, 0:n], ACT.Silu).then_inc(sem("up_silu"), 1)

            def ffn_down(l):
                base = l * CHUNKS + 36 + 2 * FT
                n = LAT if lat_only(l) else TOK
                tiles = LT if lat_only(l) else NT
                for half in range(2):
                    for j in range(11):
                        c = base + 11 * half + j + 1
                        for kk in range(2):
                            q = 22 * half + 2 * j + kk
                            if q >= 2 and kk == 0:
                                act.wait_ge(sem("g_used"), before(l, "g_used") + q // 2)
                            elif q >= 2:
                                act.wait_ge(w_used, base + q // 2 + 2)
                            act.activation(g_hi[:, kk, 0:n], g_sb[:, 2 * j + kk, 0:n], ACT.Copy).then_inc(sem("g_high"), 1)
                        if c < (l + 1) * CHUNKS:
                            high_at(c)
                    act.wait_ge(w_used, base + 11 * half + 10 + 3)
                    for t in range(0, tiles, 2):
                        act.activation(y2_sb[:, t, 512 * half:512 * half + 512], ps[:, t, :], ACT.Copy).then_inc(sem("y_out_a1"), 1)

            for l in range(DEPTH):
                ph = l * PH
                tiles = LT if lat_only(l) else NT
                vectors(l)
                norm(l, 0, NT)
                phase_ends(act, True, ph + 1)
                project(l)
                phase_ends(act, True, ph + 2)
                attend(l)
                phase_ends(act, True, ph + 3)
                delta_prep(l)
                delta(l)
                phase_ends(act, True, ph + 4)
                mix_out(l)
                for half in range(2):
                    for j in range(4):
                        high_at(l * CHUNKS + 29 + 4 * half + j)
                    act.wait_ge(w_used, l * CHUNKS + 28 + 4 * half + 3 + 3)
                    for t in range(0, tiles, 2):
                        act.activation(y_sb[:, t, 512 * half:512 * half + 512], ps[:, t, :], ACT.Copy).then_inc(sem("y_out_a0"), 1)
                gate_rows(l, 0, gate_b)
                act.wait_ge(sem("y_out_d0"), before(l, "y_out_d0") + tiles)
                act.wait_ge(sem("y_out_a0"), before(l, "y_out_a0") + tiles)
                sums(l, "y_rms0", y_sb, tiles, 16, junk[:])
                phase_ends(act, True, ph + 5)
                norm(l, 1, tiles)
                phase_ends(act, True, ph + 6)
                ffn_up(l)
                act.wait_ge(sem("g_done"), before(l, "g_done") + FT + 2)
                ffn_down(l)
                gate_rows(l, 1, gate_b2)
                act.wait_ge(sem("y_out_d1"), before(l, "y_out_d1") + tiles)
                act.wait_ge(sem("y_out_a1"), before(l, "y_out_a1") + tiles)
                sums(l, "y_rms1", y2_sb, tiles, 32, junk2[:])
                phase_ends(act, True, ph + 7)

        @block.vector
        def _(dve):
            own = Chain(dve, sem("dve_steps"))
            dve.wait_ge(sem("consts"), 16 * (4 + 2 * DEPTH))

            def vectors(l):
                dve.wait_ge(sem("vec_t"), before(l, "vec_t") + 2 + (l == 0))
                dve.tensor_copy(taps[l][:, 0:P], ps[:, 0, 0:P])
                dve.tensor_copy(taps[l][:, P:P + 4], ps[:, 1, 0:4])
                own.did(dve.tensor_copy(vec[l][:, 0:121], ps[:, 1, 0:121]))
                own.wait()
                if l == 0:
                    for u in range(4):
                        dve.wait_ge(sem("ada_used"), 2 + u + 1)
                        dve.tensor_copy(mod_first[:, u], ps[0:2, 4 + u, :]).then_inc(sem("mod_rows"), 1)
                    dve.wait_ge(sem("mods_done"), 1)
                    own.did(modulate(0, 0, 2 * KT, ps[:, 3, 0:4 * KT]))
                else:
                    own.did(modulate(1, 0, NMOD * KT, mod_raw[:].rearrange("p f s -> p (f s)")))
                own.wait()
                scale_of(l, 0)
                if l:
                    scale_of(l, 1)
                    gates_of(l)
                dve.drain().then_inc(sem("mods"), 1)

            def modulate(l, f0, f1, src):
                return dve.tensor_tensor(mod[:, f0:f1], src.rearrange("p (f s) -> p f s", s=2),
                                         vec[l][:, 40 + f0:40 + f1].unsqueeze(2).to_broadcast([P, f1 - f0, 2]), ALU.add)

            m4 = mod[:].rearrange("p (m k) s -> p m k s", m=NMOD)

            def gain(l, o):
                return vec[l][:, o:o + 8].unsqueeze(2).to_broadcast([P, KT, 2])

            def scale_of(l, w):
                own.did(dve.scalar_tensor_tensor(sc_pre[:, w], m4[:, 3 * w + 1], 1.0, gain(l, 88 + 16 * w), ALU.add, ALU.mult))

            def gates_of(l):
                for w in range(2):
                    own.did(dve.tensor_tensor(gate_c[:, w], m4[:, 3 * w + 2], gain(l, 96 + 16 * w), ALU.mult))

            def modulations():
                dve.wait_ge(sem("mods_done"), 1 + UNITS)
                dve.wait_ge(sem("o_out"), HP)
                n0 = 2 * (NMOD - 2) * KT
                own.did(modulate(0, 2 * KT, NMOD * KT, ps[:, 6, 256:256 + n0]))
                own.did(dve.tensor_copy(mod_raw[:].rearrange("p f s -> p (f s)"), ps[:, 6, 256 + n0:256 + 8 * UNITS]))
                own.wait()
                scale_of(0, 1)
                gates_of(0)

            def norm(l, which, tiles):
                dve.wait_ge(sem(f"rms{which}"), before(l, f"rms{which}") + 1)
                own.did(dve.reciprocal(stat[:, 8:8 + tiles], stat[:, 8:8 + tiles]))
                own.wait()
                for t in range(tiles):
                    dve.tensor_scalar(xn[:, t, :], x_sb[:, t, :], stat[:, 8 + t:9 + t], None, ALU.mult).then_inc(sem(f"normed{which}"), 1)

            def low(l, which, tiles):
                n = 0
                for k in range(KT):
                    for b, c0, w in ((0, 0, LAT), (1, LAT, CTX)):
                        if b and tiles == LT:
                            continue
                        n += 1
                        dve.wait_ge(sem(f"hid_h{which}"), before(l, f"hid_h{which}") + n)
                        dve.tensor_tensor(h_lo[:, k, c0:c0 + w], v_ring[:, n % 2, 0:w], h_hi[:, k, c0:c0 + w].bitcast(F32),
                                          ALU.subtract).then_inc(sem(f"h_ready{which}"), 1)

            def outer_taps(dst, src, tap0, tap2, n, step):
                segs = [(0, LAT)] if n == LAT else [(0, LAT), (LAT, TOK)]
                for c0, c1 in segs:
                    step(dve.scalar_tensor_tensor(dst[:, c0 + 1:c1], src[:, c0:c1 - 1], tap0, dst[:, c0 + 1:c1], ALU.mult, ALU.add))
                own.wait()
                for c0, c1 in segs:
                    m = dve.scalar_tensor_tensor(dst[:, c0:c1 - 1], src[:, c0 + 1:c1], tap2, dst[:, c0:c1 - 1], ALU.mult, ALU.add)
                    if (c0, c1) != segs[-1]:
                        step(m)
                return m

            def project(l):
                dve.wait_ge(sem("bd_h"), before(l, "bd_h") + 1)
                dve.tensor_tensor(bd_lo[:], bd_raw[:], bd_hi[:].bitcast(F32), ALU.subtract).then_inc(sem("bd_split"), 1)
                dve.drain().then_inc(sem("qkv_out"), 2)

                def taps_of(i, j):
                    dve.wait_ge(sem("mid"), before(l, "mid") + i * 2 + (j + 1))
                    src = ps[:, 2 * j:2 * j + 2, :].rearrange("p a b -> p (a b)")
                    outer_taps(cv[:, j, :], src, vec[l][:, ds(i * 2 + (4 + j), 1)], vec[l][:, ds(i * 2 + (28 + j), 1)], TOK,
                               own.did).then_inc(sem("taps"), 1)

                def back(t, r):
                    dve.wait_ge(sem("turned"), before(l, "turned") + t + 3)
                    dve.tensor_copy(qkv[:, :, ds(t * P, P)],
                                    ps[:, 4 + 2 * r:6 + 2 * r, :].rearrange("p a (t c) -> p (a t) c", c=P)[:, 0:NT, :]).then_inc(sem("qkv_out"), 1)
                for i in (0,):
                    taps_of(0, 0)
                    taps_of(0, 1)
                    back(0, 0)
                with dve.Fori(1, 6) as i:
                    own.enter(i - 1, 6)
                    taps_of(i, 0)
                    back(i * 2 + (-1), 1)
                    taps_of(i, 1)
                    back(i * 2, 0)
                own.leave(5)
                back(11, 1)
                dve.wait_ge(sem("w_used"), l * CHUNKS + 23 + 3)
                for t in range(1, NT, 2):
                    dve.tensor_copy((v_nat if t < LT else na_v)[:, t, :], ps[:, t, :]).then_inc(sem("v_out_d"), 1)
                dve.wait_ge(sem("bd_done"), before(l, "bd_done") + 1)
                dve.tensor_copy(bd[:], ps[:, 7, 0:192].rearrange("p (t n) -> p t n", t=NT))

            def attend(l):
                dve.wait_ge(sem("rb"), before(l, "rb") + 16 * (2 * ROWS + 1))
                for v in range(2):
                    m = dve.tensor_tensor(rb[:, v].rearrange("p h r c -> p h (r c)"), rb[:, v].rearrange("p h r c -> p h (r c)"),
                                          negm[:, v].rearrange("p r c -> p (r c)").unsqueeze(1).to_broadcast([P, H, 256]), ALU.add)
                own.did(m)
                own.wait()
                dve.drain().then_inc(sem("rb_masked"), 1)
                tiles = LT if lat_only(l) else NT
                items = [(h, u) for h in range(H) for u in range(tiles)]
                steps = len(items)

                def top(n):
                    h, u = items[n]
                    b = n % 2
                    dve.wait_ge(sem("scored"), before(l, "scored") + n + 1)
                    if u < LT:
                        dst = ps[:, b, 0:256].rearrange("p (j r c) -> p j r c", j=2, r=ROWS)
                        bias = rb[:, 0 if u < 3 else 1, h].rearrange("p r (j c) -> p j r c", j=2)
                        own.did(dve.tensor_tensor(dst, dst, bias, ALU.add))
                        own.wait()
                        dve.tensor_reduce(stat[:, b:b + 1], ps[:, b, :], AX.X, ALU.max, negate=True).then_inc(sem("maxed"), 1)
                    else:
                        dve.tensor_reduce(stat[:, b:b + 1], ps[:, b, 256:512], AX.X, ALU.max, negate=True).then_inc(sem("maxed"), 1)

                top(0)
                for n in range(steps + 1):
                    if n + 1 < steps:
                        top(n + 1)
                    if n < steps:
                        h, u = items[n]
                        c0 = 0 if u < LT else 256
                        dve.wait_ge(sem("exped"), before(l, "exped") + n + 1)
                        own.did(dve.reciprocal(stat[:, 4 + n % 2:5 + n % 2], stat[:, 2 + n % 2:3 + n % 2]))
                        own.wait()
                        dve.tensor_scalar(prob[:, n % 2, c0:512], prob[:, n % 2, c0:512], stat[:, 4 + n % 2:5 + n % 2], None, ALU.mult).then_inc(sem("probs"), 1)
                    if l == 0 and n % 2 == 0 and 2 <= n <= 2 * UNITS:
                        v = n // 2 - 1
                        dve.wait_ge(sem("ada_used"), 2 + 4 + v + 1)
                        dve.wait_ge(sem("mods_done"), 1 + v)
                        dve.tensor_copy(mod_row[:], ps[64 * (v % 2):64 * (v % 2) + 2, 7, :]).then_inc(sem("mod_rows"), 1)
                    if n and n % 2 == 0:
                        h, u = items[n - 1]
                        dve.wait_ge(sem("p_turned"), before(l, "p_turned") + n)
                        if h >= 2 and u == 1:
                            dve.wait_ge(sem("valued"), before(l, "valued") + h - 1)
                        for dst, src in turned(n - 1, u, h):
                            dve.tensor_copy(dst, src)
                        dve.drain().then_inc(sem("pt_odd"), 1)

            def delta_prep(l):
                own.did(dve.tensor_tensor(gtmp[:, 0], bd[:, :, 16:32], al_dt[:, l, 1, :].unsqueeze(1).to_broadcast([P, NT, 16]), ALU.add))
                own.wait()
                own.did(dve.tensor_scalar(gtmp[:, 1], gtmp[:, 0], -1.0, None, ALU.mult))
                own.wait()
                dve.tensor_tensor(gtmp[:, 1], gtmp[:, 1], gtmp[:, 0], ALU.max).then_inc(sem("dec_abs"), 1)
                dve.wait_ge(sem("dec_ln"), before(l, "dec_ln") + 1)
                own.did(dve.scalar_tensor_tensor(gtmp[:, 0], gtmp[:, 0], 0.0, gtmp[:, 1], ALU.max, ALU.add))
                own.wait()
                dve.scalar_tensor_tensor(graw[:], gtmp[:, 0], -1.0, stat2[:, 0:16].unsqueeze(1).to_broadcast([P, NT, 16]),
                                         ALU.mult, ALU.mult).then_inc(sem("decays"), 1)
                dve.memset(o_g[:], 0.0)
                for d in range(2):
                    dve.memset(mv_b[d][64:128], 0.0)
                    dve.memset(mv_a[d][64:128], 0.0)
                    own.did(dve.memset(zb[d][:], 0.0))
                dve.wait_ge(sem("e_ready"), before(l, "e_ready") + 1)
                own.did(dve.tensor_scalar(nbe[:], beta[:], -1.0, None, ALU.mult))
                own.wait()
                for d in range(2):
                    own.did(dve.tensor_tensor(nbec[:, d], nbe[:, :, 8 * d:8 * d + 8], e_cum[:, d], ALU.mult))
                dve.drain().then_inc(sem("gates"), 1)
                for t in range(NT):
                    dve.wait_ge(sem("qk_sq"), before(l, "qk_sq") + t + 1)
                    dve.tensor_reduce(qk_ss[:, t, :], sq[:].rearrange("p (n c) -> p n c", c=DH), AX.X, ALU.add).then_inc(sem("qk_summed"), 1)
                dve.wait_ge(sem("qk_root"), before(l, "qk_root") + 1)
                own.did(dve.reciprocal(qk_rt[:], qk_rt[:]))
                own.wait()
                own.did(dve.tensor_scalar(qk_rt[:, :, 0:H], qk_rt[:, :, 0:H], DH ** -0.5, None, ALU.mult))
                own.wait()
                for t in range(NT):
                    x = qkv[:, t, 0:2 * W].rearrange("p (n c) -> p n c", c=DH)
                    own.did(dve.tensor_tensor(x, x, qk_rt[:, t, :].unsqueeze(2).to_broadcast([P, 2 * H, DH]), ALU.mult))
                    own.wait()
                    if t < LT:
                        xx = qkv[:, t, 0:2 * W].rearrange("p (n a c) -> p n a c", a=2, c=32)
                        rr = rot[:].rearrange("p s (n a c) -> p s n a c", a=2, c=32)
                        for a_ in range(2):
                            cb = lambda k: cs[:, t, k, :].unsqueeze(1).to_broadcast([P, 2 * H, 32])
                            dve.tensor_tensor(rr[:, 0, :, a_], xx[:, :, a_], cb(0), ALU.mult)
                            own.did(dve.tensor_tensor(rr[:, 1, :, a_], xx[:, :, a_], cb(1), ALU.mult))
                        own.wait()
                        dve.tensor_tensor(xx[:, :, 0], rr[:, 0, :, 0], rr[:, 1, :, 1], ALU.subtract)
                        own.did(dve.tensor_tensor(xx[:, :, 1], rr[:, 0, :, 1], rr[:, 1, :, 0], ALU.add))
                    dve.drain().then_inc(sem("qk_normed"), 1)
                    own.wait()

            def psum_pairs(p0, p1, b, off):
                return ps[p0:p1, b:b + 2, off:off + 256].rearrange("p s (e c) -> p e s c", e=HP)

            def delta(l):
                for k in range(NT):
                    for d in range(2):
                        g, t = 2 * k + d, TILES[d][k]
                        dve.wait_ge(sem("gram"), before(l, "gram") + g + 1)
                        dve.wait_ge(sem("em"), before(l, "em") + 2 * g + 2)
                        four = lambda x: x.rearrange("p (e s) c -> p e s c", s=2)
                        dve.tensor_tensor(four(e1[d][:]), psum_pairs(0, P, 2 * d, 0), four(e1[d][:]), ALU.mult).then_inc(sem("m_ready"), 1)
                        if k:
                            dve.wait_ge(sem("chained"), before(l, "chained") + 4 * k)
                        for c in range(2):
                            cp = slice(64 * c, 64 * c + 64)
                            dve.tensor_tensor(four(st_b[d][0:64, c, :, 0:64]), psum_pairs(64 * c, 64 * c + 64, 2 * d, 256), four(e2[d][cp]), ALU.mult)
                            kk = qkv[cp, t, W:2 * W].rearrange("p (h c) -> p h c", h=H)
                            vv = qkv[cp, t, 2 * W:3 * W].rearrange("p (h c) -> p h c", h=H)
                            dve.tensor_tensor(st_b[d][0:64, c, :, 64:128], kk, e_tail[cp, d, t, :].unsqueeze(2).to_broadcast([64, H, C]), ALU.mult)
                            own.did(dve.tensor_tensor(mv_a[d][0:64, c], vv, beta[cp, t, 8 * d:8 * d + 8].unsqueeze(2).to_broadcast([64, H, C]), ALU.mult))
                        dve.drain().then_inc(sem("gram_out"), 1)
                    for s in range(LEVELS):
                        for d in range(2):
                            dve.wait_ge(sem(f"z_done{d}"), before(l, f"z_done{d}") + k * LEVELS + s + 1)
                            dve.tensor_copy(zb[d][64:128, :, :, 1, :], ps[64:128, 2 * d, :].rearrange("p (e c n) -> p e c n", e=HP, c=2)).then_inc(sem(f"zb_d{d}"), 1)
                        for d in range(2):
                            dve.wait_ge(sem(f"p_done{d}"), before(l, f"p_done{d}") + k * LEVELS + s + 1)
                            if s == 0:
                                dve.wait_ge(sem("ra"), before(l, "ra") + 4 * (2 * k + d) + 4)
                            pv = lambda p0, p1: ps[p0:p1, 2 * d + 1, :].rearrange("p (h c) -> p h c", h=H)
                            mk = lambda p0, p1: lev[p0:p1, d, s, :].unsqueeze(1).to_broadcast([p1 - p0, H, C])
                            dve.copy_predicated(xtc[d][:], mk(0, P), pv(0, P))
                            dve.copy_predicated(xtb[d][0:64, :, 0, :], mk(0, 64), pv(0, 64))
                            own.did(dve.copy_predicated(xtb[d][64:128, :, 1, :], mk(64, P), pv(64, P)))
                            dve.drain().then_inc(sem(f"xt_new{d}"), 1)
                    own.wait()
                    for d in range(2):
                        dve.tensor_copy(st_a[d][0:64, 0], xtc[d][0:64])
                        dve.tensor_copy(st_a[d][0:64, 1], xtc[d][64:128]).then_inc(sem("st_ready_d"), 1)
                    for n in (2 * k, 2 * k + 1):
                        for d in range(2):
                            t, c = TILES[d][k], (n % 2 if d == 0 else 1 - n % 2)
                            dve.wait_ge(sem("chained"), before(l, "chained") + 2 * n + d + 1)
                            o = o_g[64 * c:64 * c + 64, t, :]
                            own.wait()
                            own.did(dve.tensor_tensor(o, ps[0:64, 6 + d, :], o, ALU.add))
                            dve.drain().then_inc(sem(f"o_added{d}"), 1)


            def mix_out(l):
                tiles = LT if lat_only(l) else NT
                for t in range(tiles):
                    dve.wait_ge(sem("o_sq"), before(l, "o_sq") + t + 1)
                    dve.tensor_reduce(o_ss[:, t * H:t * H + H], osq[:].rearrange("p (h c) -> p h c", h=H), AX.X, ALU.add).then_inc(sem("o_summed"), 1)
                dve.wait_ge(sem("o_root"), before(l, "o_root") + 1)
                own.did(dve.reciprocal(o_rt[:, 0:tiles * H], o_rt[:, 0:tiles * H]))
                own.wait()
                for t in range(tiles):
                    x = o_g[:, t, :].rearrange("p (h c) -> p h c", h=H)
                    own.did(dve.tensor_tensor(on[:, t, :].rearrange("p (h c) -> p h c", h=H), x,
                                              o_rt[:, t * H:t * H + H].unsqueeze(2).to_broadcast([P, H, DH]), ALU.mult))
                    own.wait()
                    dve.tensor_tensor(on[:, t, :], on[:, t, :], z_sb[:, t, :], ALU.mult).then_inc(sem("o_normed"), 1)
                n = tiles * P
                for e in range(HP):
                    dve.wait_ge(sem("o_high"), before(l, "o_high") + e + 1)
                    dve.tensor_tensor(o_lo[:, e, 0:n], o_t[:, e, 0:n], o_hi[:, e, 0:n].bitcast(F32), ALU.subtract).then_inc(sem("o_split"), 1)
                for e in range(HP):
                    dve.wait_ge(sem("o_high"), before(l, "o_high") + HP + e + 1)
                    dve.tensor_tensor(o_lo[:, HP + e, 0:n], ov[:, e % 2, 0:n], o_hi[:, HP + e, 0:n].bitcast(F32), ALU.subtract).then_inc(sem("o_split"), 1)

            def gate_rows(l, which, gd):
                for i in range(2 if lat_only(l) else 4):
                    if i:
                        dve.wait_ge(sem(f"gate_done{which}"), before(l, f"gate_done{which}") + i)
                    for q in range(4):
                        f = 4 * (i % 2) + q
                        own.did(dve.tensor_scalar(gd[:, q * P:q * P + P], ident, gate_c[:, which, f, i // 2:i // 2 + 1], None, ALU.mult))
                    dve.drain().then_inc(sem(f"gdiag{which}"), 1)

            def residual(l, which, y, gb):
                tiles = LT if lat_only(l) else NT
                off = 16 + 16 * which + 8
                dve.wait_ge(sem(f"y_rms{which}"), before(l, f"y_rms{which}") + 1)
                own.did(dve.reciprocal(stat[:, off:off + tiles], stat[:, off:off + tiles]))
                own.wait()
                if which == 0:
                    dve.wait_ge(sem("x_landed"), 64 + 32 * l)
                for t in range(tiles):
                    own.did(dve.scalar_tensor_tensor(y[:, t, :], y[:, t, :], stat[:, off + t:off + t + 1], gb[:, 0 if t < LT else 1, :], ALU.mult, ALU.mult))
                    own.wait()
                    own.did(dve.tensor_tensor(x_sb[:, t, :], x_sb[:, t, :], y[:, t, :], ALU.add))

            def y_out(l, which, y):
                tiles = LT if lat_only(l) else NT
                for half in range(2):
                    dve.wait_ge(sem("w_used"), l * CHUNKS + 28 + 4 * half + 3 + 3)
                    for t in range(1, tiles, 2):
                        dve.tensor_copy(y[:, t, 512 * half:512 * half + 512], ps[:, t, :]).then_inc(sem(f"y_out_d{which}"), 1)

            def ffn_up(l):
                n = LAT if lat_only(l) else TOK
                per = 6 if n == TOK else 2
                dve.drain().then_inc(sem("up_taps"), 4)
                dve.drain().then_inc(sem("g_done"), 2)
                with dve.Fori(0, FT // 2) as i:
                    own.enter(i, 2 * per)
                    for j in range(2):
                        for gv, dst in ((0, cg), (1, cw)):
                            dve.wait_ge(sem("up_mid"), before(l, "up_mid") + i * 4 + (2 * j + gv + 1))
                            src = ps[:, 4 * j + 2 * gv:4 * j + 2 * gv + 2, :].rearrange("p a b -> p (a b)")
                            tap = lambda k: taps[l][:, ds(i * 2 + (k * 2 * FT + gv * FT + j), 1)]
                            outer_taps(dst[:, j, :], src, tap(0), tap(2), n, own.did).then_inc(sem("up_taps"), 1)
                        dve.wait_ge(sem("up_silu"), before(l, "up_silu") + i * 2 + (j + 1))
                        dve.wait_ge(sem("up_taps"), before(l, "up_taps") + i * 4 + (2 * j + 6))
                        dve.tensor_tensor(g_sb[:, ds(i * 2 + j, 1), 0:n].rearrange("p a n -> p (a n)"), cg[:, j, 0:n], cw[:, j, 0:n], ALU.mult).then_inc(sem("g_done"), 1)
                own.leave(FT // 2)

            def ffn_down(l):
                n = LAT if lat_only(l) else TOK
                tiles = LT if lat_only(l) else NT
                for half in range(2):
                    for f in range(FT):
                        dve.wait_ge(sem("g_high"), before(l, "g_high") + FT * half + f + 1)
                        dve.tensor_tensor(g_lo[:, f % 2, 0:n], g_sb[:, f, 0:n], g_hi[:, f % 2, 0:n].bitcast(F32), ALU.subtract).then_inc(sem("g_split"), 1)
                    dve.wait_ge(sem("w_used"), l * CHUNKS + 36 + 2 * FT + 11 * half + 10 + 3)
                    for t in range(1, tiles, 2):
                        dve.tensor_copy(y2_sb[:, t, 512 * half:512 * half + 512], ps[:, t, :]).then_inc(sem("y_out_d1"), 1)

            for l in range(DEPTH):
                ph = l * PH
                tiles = LT if lat_only(l) else NT
                vectors(l)
                norm(l, 0, NT)
                low(l, 0, NT)
                phase_ends(dve, True, ph + 1)
                project(l)
                phase_ends(dve, True, ph + 2)
                attend(l)
                if l == 0:
                    modulations()
                phase_ends(dve, True, ph + 3)
                delta_prep(l)
                delta(l)
                phase_ends(dve, True, ph + 4)
                mix_out(l)
                y_out(l, 0, y_sb)
                gate_rows(l, 0, gdiag)
                dve.wait_ge(sem("gate_out0"), before(l, "gate_out0") + 2 if lat_only(l) else 4)
                residual(l, 0, y_sb, gate_b)
                phase_ends(dve, True, ph + 5)
                norm(l, 1, tiles)
                low(l, 1, tiles)
                phase_ends(dve, True, ph + 6)
                ffn_up(l)
                ffn_down(l)
                gate_rows(l, 1, gdiag2)
                dve.wait_ge(sem("gate_out1"), before(l, "gate_out1") + 2 if lat_only(l) else 4)
                residual(l, 1, y2_sb, gate_b2)
                phase_ends(dve, True, ph + 7)


INS = ["x", "c", "ctx", "c_ctx", "ada_w", "ada_b", "norm_mix_pre", "norm_mix_post", "w_in", "qkv_conv", "a_log",
       "dt_bias", "gdn_norm", "rpb", "w_out", "norm_ffn_pre", "norm_ffn_post", "ffn_up", "ffn_conv", "ffn_down"]


def kernel(**inputs):
    import numpy as _np
    import concourse.bacc as _bacc
    from concourse import mybir as _mybir
    from concourse.bass_utils import run_bass_kernel_spmd as _run

    nc = _bacc.Bacc("TRN2", target_bir_lowering=False, num_devices=1, dynamic_dma_scratch_size=256)
    arrays, args = {}, {}
    table, levels = constants()
    for name, arr in [(n, inputs[n]) for n in INS] + [("cns", table), ("lev", levels)]:
        v = _np.ascontiguousarray(arr)
        arrays[f"in_{name}"] = v
        args[name] = nc.dram_tensor(f"in_{name}", v.shape, _mybir.dt.from_np(v.dtype), kind="ExternalInput").ap()
    args["out"] = nc.dram_tensor("out_0", (1, LAT, D), F32, kind="ExternalOutput").ap()
    build(nc, args)
    r = _run(nc, [arrays], core_ids=[0])
    return r.results[0]["out_0"]
```

```python
from contextlib import ExitStack

import numpy as np

import concourse.bass as bass
from concourse import mybir

ALU = mybir.AluOpType
ACT = mybir.ActivationFunctionType
AX = mybir.AxisListType
F32 = mybir.dt.float32
F32R = mybir.dt.float32r
I32 = mybir.dt.int32
ds = bass.ds

P = 128
D = 1024
KT = D // P
LAT, CTX = 512, 256
TOK = LAT + CTX
NT, LT = TOK // P, LAT // P
H, DH = 8, 64
HP = H // 2
W = H * DH
DEPTH = 2
IN_W = 3 * W + 4 * W + 4 * H
DFF = 2816
FT = DFF // P
NMOD = 6
GRID, ROWS = 64, 8
KH, KW = 8, 16
C = 64
LEVELS = 6
EPS = 1e-6
CHUNKS = 28 + 8 + 2 * FT + FT
NEG = -1e30

C_ID = 0
C_A = C_ID + P
C_ONE = C_A + 4 * P
C_B = C_ONE + 2 * P
C_CS = C_B + 4 * C
C_NEG = C_CS + LT * 2 * 32
C_TI = C_NEG + 2 * ROWS * 32
C_XQ = C_TI + C
C_W = C_XQ + P
LE, GE, GT, LT_ = 0, 1, 2, 3


def constants():
    m = np.arange(P)
    same = (m[:, None] // C) == (m[None, :] // C)
    r, k = m[:, None], m[None, :]
    a = [same & (r <= k), same & (r >= k), same & (r > k), same & (r < k)]
    one = [np.repeat((m // C == c)[:, None], P, 1) for c in range(2)]
    pc, col = (m % C)[:, None], np.arange(C)[None, :]
    b = [pc > col, pc < col, pc <= col, pc >= col]
    t = np.arange(LAT)
    inv = (10000.0 ** (-np.arange(16, dtype=np.float32) / 16)).astype(np.float32)
    ang = np.concatenate([(t // GRID)[:, None].astype(np.float32) * inv,
                          (t % GRID)[:, None].astype(np.float32) * inv], 1)
    cs = np.stack([np.cos(ang), np.sin(ang)], 1).reshape(LT, P, 2, 32).transpose(1, 0, 2, 3)
    k32 = np.arange(32)[None, None, :]
    qc = (m % 16)[:, None, None]
    inner = (k32 - qc >= 0) & (k32 - qc <= 15)
    edge = np.where(((m % 16) // 8)[:, None, None] == 0, k32 < 16, k32 >= 16)
    neg = np.stack([np.broadcast_to(np.where(x, 0.0, NEG), (P, ROWS, 32)) for x in (inner, edge)], 1)
    ti = pc == col
    xq = (m[:, None] % C) == (m[None, :] % C)
    parts = [np.eye(P), *a, *one, *b, cs.reshape(P, -1), neg.reshape(P, -1), ti, xq]
    cns = np.concatenate([np.asarray(x, np.float32) for x in parts], 1)
    i, kk = np.arange(C)[None, :], pc
    lev = []
    for d in range(2):
        for s in range(LEVELS):
            w = 1 << s
            blk = (kk // (2 * w)) == (i // (2 * w))
            lo, hi = (kk // w) % 2 == 0, (i // w) % 2 == 1
            lev.append(blk & lo & hi if d == 0 else blk & ~lo & ~hi)
    return np.ascontiguousarray(cns), np.ascontiguousarray(np.concatenate(lev, 1).astype(np.int32))


def per_layer():
    t = {}
    for names, n in (("bd_done bd_h bd_split dec_abs dec_ln decays e_ready gates mods_done mods o_root qk_root "
                      "rb_masked sums rms0 rms1 y_rms0 y_rms1", 1),
                     ("vec_t v_out_a v_out_d", 3),
                     ("gate_done0 gate_done1 gate_out0 gate_out1 gdiag0 gdiag1 o_out o_turned ov_out", HP),
                     ("summed0 summed1 y_out_a0 y_out_a1 y_out_d0 y_out_d1 normed0 normed1 o_normed o_sq o_summed qk_normed qk_out "
                      "qk_sq qk_summed qk_turned", NT),
                     ("proj_free o_high o_split valued", H),
                     ("conv mid taps xt_init group_done o_added0 o_added1 st_ready_d state0 state1 "
                      "vnew_done0 vnew_done1 vnew0 vnew1 wq_out", 2 * NT),
                     ("turned qkv_out", 2 * NT + 2),
                     ("h_ready0 h_ready1 hid_h0 hid_h1 hid_t0 hid_t1 hid_v0 hid_v1", 2 * KT),
                     ("chained diffs egi em exps kq gram m_ready ra", 4 * NT),
                     ("exped maxed p_turned probs scored", H * NT),
                     ("p_done0 p_done1 xc_new0 xc_new1 xb_new0 xb_new1 xt_new0 xt_new1 z_done0 z_done1 zb_a0 zb_a1 zb_d0 zb_d1", NT * LEVELS),
                     ("xq_new0 xq_new1 xt_turned0 xt_turned1", NT * (LEVELS - 1)),
                     ("pt_even pt_odd", H * NT // 2), ("g_done", FT + 2), ("g_used up_silu", FT), ("g_high g_split up_mid", 2 * FT), ("up_taps", 2 * FT + 4),
                     ("rb", 16 * (2 * ROWS + 1)), ("rows", 16 * 11)):
        for name in names.split():
            t[name] = n
    return t


SIGNALS = per_layer()


def before(l, name):
    return l * SIGNALS[name]


class Chain:

    def __init__(self, eng, sem):
        self.eng, self.sem, self.n, self.i, self.base, self.per = eng, sem, 0, None, 0, 0

    def did(self, ins):
        ins.then_inc(self.sem, 1)
        self.n += 1
        return ins

    def enter(self, i, per):
        self.base, self.i, self.per, self.n = self.n, i, per, 0

    def leave(self, trips):
        assert self.n == self.per
        self.n, self.i = self.base + trips * self.per, None

    def wait(self):
        if self.i is None:
            self.eng.wait_ge(self.sem, self.n)
        else:
            self.eng.wait_ge(self.sem, self.i * self.per + (self.base + self.n))


def build(nc, a):
    ctx = ExitStack()
    with ctx:
        sems = {}

        def sem(name):
            if name not in sems:
                sems[name] = ctx.enter_context(nc.semaphore(name))
            return sems[name]

        here = [512]

        def perm(name, shape, dt=F32):
            t = nc.alloc_sbuf_tensor_at(name, shape, dt, offset=here[0])
            here[0] += -(-int(np.prod(shape[1:])) * 4 // 64) * 64
            return t

        cns = perm("cns", [P, C_W])
        lev = perm("lev", [P, 2, LEVELS, C], I32)
        w_ring = here[0]
        w_raw = perm("w_raw", [P, 2, D])
        w_hi = perm("w_hi", [P, 2, D], F32R)
        w_lo = perm("w_lo", [P, 2, D], F32R)
        taps = [perm(f"taps{l}", [P, 3 * 2 * FT]) for l in range(DEPTH)]
        vec = [perm(f"vec{l}", [P, P]) for l in range(DEPTH)]
        cond = perm("cond", [P, 2 * KT])
        mod = perm("mod", [P, NMOD * KT, 2])
        mod_raw = perm("mod_raw", [P, NMOD * KT, 2])
        sc_pre = perm("sc_pre", [P, 2, KT, 2])
        gate_c = perm("gate_c", [P, 2, KT, 2])
        ones = perm("ones", [P, P])
        eps_t = perm("eps_t", [P, 1])
        stat = perm("stat", [P, 64])
        a_exp = perm("a_exp", [P, 16])
        al_dt = perm("al_dt", [P, DEPTH, 2, 16])
        bd = perm("bd", [P, NT, 32])
        beta = perm("beta", [P, NT, 16])
        graw = perm("graw", [P, NT, 16])
        gtmp = perm("gtmp", [P, 2, NT, 16])
        e_cum = perm("e_cum", [P, 2, NT, H])
        e_tail = perm("e_tail", [P, 2, NT, H])
        e_tot = perm("e_tot", [P, 2, NT, 16])
        nbe = perm("nbe", [P, NT, 16])
        nbec = perm("nbec", [P, 2, NT, H])
        qk_ss = perm("qk_ss", [P, NT, 2 * H])
        qk_rt = perm("qk_rt", [P, NT, 2 * H])
        arena = here[0]
        KB = 1024

        def at(name, kb, shape, dt=F32):
            return nc.alloc_sbuf_tensor_at(name, shape, dt, offset=arena + kb * KB)

        def over(name, kb, shape):
            return nc.alloc_sbuf_tensor_at(name, shape, F32, offset=w_ring + kb * KB)

        x_sb = at("x_sb", 151, [P, NT, D])
        xn = at("xn", 0, [P, NT, D])
        v_nat = at("v_nat", 88, [P, LT, W])
        row_ffn = at("row_ffn", 92, [P, P])
        row_vec = at("row_vec", 93, [P, P])
        row_c = at("row_c", 94, [16, P])
        bd_raw = at("bd_raw", 102, [P, KT, 32])
        bd_hi = at("bd_hi", 85, [P, KT, 32], F32R)
        bd_lo = at("bd_lo", 86, [P, KT, 32], F32R)
        ada_first = [at(f"ada_first{i}", (103, 119, 135, 24)[i], [P, KT, 4 * P]) for i in range(4)]
        ada_ring = [at(f"ada_ring{i}", (103, 143)[i], [P, KT, 4 * P]) for i in range(2)]
        mod_first = at("mod_first", 69, [2, 4, 512])
        mod_row = at("mod_row", 100, [2, 512])
        v_ring = at("v_ring", 96, [P, 2, 512])
        h_hi = at("h_hi", 103, [P, KT, TOK], F32R)
        h_lo = at("h_lo", 127, [P, KT, TOK], F32R)
        qkv = at("qkv", 0, [P, NT, 3 * W])
        z_sb = at("z_sb", 36, [P, NT, W])
        na_q = at("na_q", 48, [P, HP, TOK])
        na_k = at("na_k", 60, [P, HP, TOK])
        na_v = at("na_v", 72, [P, NT, W])
        cv = at("cv", 96, [P, 2, TOK])
        cvs = at("cvs", 151, [P, 2, TOK])
        o_t = at("o_t", 84, [P, HP, TOK])
        rb = at("rb", 159, [P, 2, H, ROWS, 32])
        prob = at("prob", 119, [P, 2, 512])
        pt = at("pt", 123, [P, 2, 20, P])
        o_g = at("o_g", 48, [P, NT, W])
        q_t = at("q_t", 60, [P, HP, TOK])
        k_t = at("k_t", 72, [P, HP, TOK])
        sq = at("sq", 96, [P, D])
        rot = over("rot", 0, [P, 2, D])
        e1 = [[at(f"e1_{d}", 96 + 20 * d, [P, H, C]) for d in range(2)],
              [over(f"e1_b{d}", 0 + 2 * d, [P, H, C]) for d in range(2)]]
        e2 = [[at(f"e2_{d}", 98 + 20 * d, [P, H, C]) for d in range(2)],
              [over(f"e2_b{d}", 4 + 2 * d, [P, H, C]) for d in range(2)]]
        ra = [at(f"ra_{d}", 100 + 20 * d, [P, H, C]) for d in range(2)]
        rbb = [at(f"rbb_{d}", 102 + 20 * d, [P, H, C]) for d in range(2)]
        xtc = [[at(f"xtc_{d}", 104 + 20 * d, [P, H, C]) for d in range(2)],
              [over(f"xtc_b{d}", 16 + 2 * d, [P, H, C]) for d in range(2)]]
        xtb = [[at(f"xtb_{d}", 106 + 20 * d, [P, H, 2, C]) for d in range(2)],
              [over(f"xtb_b{d}", 8 + 4 * d, [P, H, 2, C]) for d in range(2)]]
        xq = [at(f"xq_{d}", 110 + 20 * d, [P, HP, P]) for d in range(2)]
        zb = [at(f"zb_{d}", 112 + 20 * d, [P, HP, 2, 2, C]) for d in range(2)]
        st_a = [at(f"st_a_{d}", 136 + 4 * d, [P, 2, H, C]) for d in range(2)]
        st_b = [at(f"st_b_{d}", 144 + 8 * d, [P, 2, H, P]) for d in range(2)]
        mv_a = [at(f"mv_a_{d}", 160 + 4 * d, [P, 2, H, C]) for d in range(2)]
        mv_b = [at(f"mv_b_{d}", 168 + 2 * d, [P, H, C]) for d in range(2)]
        o_hi = at("o_hi", 103, [P, KT, TOK], F32R)
        o_lo = at("o_lo", 127, [P, KT, TOK], F32R)
        on = at("on", 60, [P, NT, W])
        ov = at("ov", 72, [P, 2, TOK])
        osq = at("osq", 78, [P, W])
        o_ss = at("o_ss", 80, [P, NT * H])
        o_rt = at("o_rt", 81, [P, NT * H])
        v_junk = at("v_junk", 60, [P, D])[:]
        y_sb = at("y_sb", 0, [P, NT, D])
        gate_b = at("gate_b", 24, [P, 2, D])
        gdiag = at("gdiag", 32, [P, 512])
        zeros = at("zeros", 67, [P, 512])
        junk = at("junk", 96, [P, D])
        g_sb = at("g_sb", 0, [P, FT, TOK])
        cg = at("cg", 68, [P, 2, TOK])
        cw = at("cw", 74, [P, 2, TOK])
        g_hi = at("g_hi", 80, [P, 2, TOK], F32R)
        g_lo = at("g_lo", 86, [P, 2, TOK], F32R)
        y2_sb = at("y2_sb", 103, [P, NT, D])
        gate_b2 = at("gate_b2", 127, [P, 2, D])
        gdiag2 = at("gdiag2", 135, [P, 512])
        junk2 = at("junk2", 140, [P, D])

        ps = ctx.enter_context(nc.psum_tensor("ps", [P, 8, 512], F32))
        x_mid = nc.dram_tensor("x_mid", (P, NT, D), F32, kind="Internal").ap()
        v_mid = nc.dram_tensor("v_mid", (LAT, W), F32, kind="Internal").ap()
        bias_rows = nc.dram_tensor("bias_rows", (DEPTH, ROWS, 64, 31), F32, kind="Internal").ap()
        bias_wide = nc.dram_tensor("bias_wide", (DEPTH, ROWS, 16, 64, 48), F32, kind="Internal").ap()

        ident = cns[:, C_ID:C_ID + P]
        amask = [cns[:, C_A + P * i:C_A + P * (i + 1)] for i in range(4)]
        onec = [cns[:, C_ONE + P * i:C_ONE + P * (i + 1)] for i in range(2)]
        bmask = [cns[:, C_B + C * i:C_B + C * (i + 1)] for i in range(4)]
        cs = cns[:, C_CS:C_CS + LT * 64].rearrange("p (t a c) -> p t a c", t=LT, a=2)
        negm = cns[:, C_NEG:C_NEG + 512].rearrange("p (v r c) -> p v r c", v=2, r=ROWS)
        ti = cns[:, C_TI:C_TI + C]
        xq0 = cns[:, C_XQ:C_XQ + P]

        phase_end = sem("phase_end")
        block = ctx.enter_context(nc.Block())

        def phase_ends(eng, counts, n):
            if counts:
                eng.drain().then_inc(phase_end, 1)
            eng.wait_ge(phase_end, 4 * n)

        PH = 7
        UNITS = DEPTH * NMOD * 2 - 4
        def lat_only(l):
            return l == DEPTH - 1

        def col(t):
            return slice(t * P, (t + 1) * P)

        def turned(n, u, h):
            pairs = []
            if u < LT:
                i0, i1 = ((0, 2), (3, 4), (5, 6), (1, 7))[u]
                pairs.append((pt[:, h % 2, i0:i1 + 1:i1 - i0, :], ps[:, 2 + n % 2, 0:256].rearrange("p (a b) -> p a b", a=2)))
            c = ((8 + u, 12 + u) if u < LT else (12 + u, 14 + u))
            pairs.append((pt[:, h % 2, c[0]:c[1] + 1:c[1] - c[0], :], ps[:, 2 + n % 2, 256:512].rearrange("p (a b) -> p a b", a=2)))
            return pairs

        BETWEEN = {(0, "p"): ("a", 0), (1, "z"): ("b", 0), (1, "p"): ("diff", 0, 0), (1, "t"): ("a", 1),
                   (2, "z"): ("diff", 0, 1), (2, "p"): ("b", 1), (2, "t"): ("diff", 1, 0), (3, "z"): ("diff", 1, 1),
                   (3, "t"): ("gram", 0, 0), (4, "z"): ("gram", 0, 1), (4, "p"): ("gram", 1, 0), (4, "t"): ("gram", 1, 1)}

        def between(k, s, place, parts):
            it = BETWEEN.get((s, place))
            if it is None or it[0] not in parts:
                return
            if it[0] in ("a", "b"):
                if k:
                    parts[it[0]](2 * (k - 1) + it[1])
            elif k + 1 < NT:
                parts[it[0]](k + 1, *it[1:])

        def start_and_end(parts, run):
            for kind in ("diff", "gram"):
                for d in range(2):
                    for i in range(2):
                        if kind in parts:
                            parts[kind](0, d, i)
            for k in range(NT):
                run(k)
            for n in (2 * NT - 2, 2 * NT - 1):
                for kind in ("a", "b"):
                    if kind in parts:
                        parts[kind](n)

        FWD, BWD = [4, 5, 0, 1, 2, 3], [5, 4, 3, 2, 1, 0]
        TILES = [FWD, BWD]

        @block.sync
        def _(sp):
            wl = [sem("w_landed0"), sem("w_landed1")]
            al = [sem(f"ada_landed{i}") for i in range(2)]
            w_free, ada_used = sem("w_lo_ready"), sem("ada_used")
            consts = sem("consts")
            sp.dma_start(cns[:], a["cns"]).then_inc(consts, 16)
            sp.dma_start(lev[:].rearrange("p a b c -> p (a b c)"), a["lev"]).then_inc(consts, 16)
            for l in range(DEPTH):
                for k, v in enumerate(("a_log", "dt_bias")):
                    src = a[v][l].rearrange("a b -> (a b)").unsqueeze(0).to_broadcast([P, 16])
                    sp.dma_start(al_dt[:, l, k, :], src).then_inc(consts, 16)
            sp.dma_start(row_c[0:8, :], a["c"].rearrange("a (k p) -> (a k) p", p=P)).then_inc(consts, 16)
            sp.dma_start(row_c[8:16, :], a["c_ctx"].rearrange("(k p) -> k p", p=P)).then_inc(consts, 16)

            def w_chunk(n, src, split, first):
                slot = n % 2 if isinstance(n, int) else first % 2
                sp.wait_ge(w_free, n + 1)
                dst = w_raw[:, slot, :]
                if split:
                    dst = dst.rearrange("p (k n) -> p k n", k=split)
                sp.dma_start(dst, src).then_inc(wl[slot], 16)

            def columns(base, w, col0, tiles):
                v = w.rearrange("(k p) n -> p k n", p=P)
                with sp.Fori(0, tiles // 2) as i:
                    for j in range(2):
                        w_chunk(i * 2 + (base + j), v[:, :, ds(i * 256 + (col0 + j * P), P)], KT, base + j)

            def rows(base, w, col0, chunks):
                v = w.rearrange("(j two p) n -> j p two n", p=P, two=2)
                for j in range(chunks):
                    w_chunk(base + j, v[j, :, :, col0:col0 + 512], 2, base + j)

            def vector_loads(l):
                rows_l = sem("rows")
                cvw = a["ffn_conv"][l].rearrange("t (f p) -> (t f) p", p=P)
                sp.dma_start(row_ffn[:], cvw[0:P]).then_inc(rows_l, 16)
                sp.dma_start(row_vec[0:4, :], cvw[P:P + 4]).then_inc(rows_l, 16)
                sp.dma_start(row_vec[4:40, :], a["qkv_conv"][l].rearrange("t (f p) -> (t f) p", p=P)).then_inc(rows_l, 16)
                sp.dma_start(row_vec[40:88, :], a["ada_b"][l].rearrange("(f p) -> f p", p=P)).then_inc(rows_l, 16)
                for k, v in enumerate(("norm_mix_pre", "norm_mix_post", "norm_ffn_pre", "norm_ffn_post")):
                    sp.dma_start(row_vec[88 + 8 * k:96 + 8 * k, :], a[v][l].rearrange("(f p) -> f p", p=P)).then_inc(rows_l, 16)
                for k in range(2):
                    sp.dma_start(row_vec[120:121, 64 * k:64 * k + 64], a["gdn_norm"][l].unsqueeze(0)).then_inc(rows_l, 16)
                sp.dma_start(bd_raw[:], a["w_in"][l].rearrange("(k p) n -> p k n", p=P)[:, :, 7 * W:7 * W + 32]).then_inc(rows_l, 16)

            for l in range(DEPTH):
                w_in, base, ph = a["w_in"][l], l * CHUNKS, l * PH
                if l == 0:
                    vector_loads(0)
                av = a["ada_w"][l].rearrange("(k p) n -> p k n", p=P)
                if l == 0:
                    for i in range(4):
                        sp.dma_start(ada_first[i][:], av[:, :, i * 4 * P:(i + 1) * 4 * P]).then_inc(sem(f"ada_first{i}"), 16)
                        if i == 1:
                            sp.dma_start(x_sb[:, 0:LT, :], a["x"][0].rearrange("(t p) n -> p t n", p=P)).then_inc(sem("x_landed"), 16)
                            sp.dma_start(x_sb[:, LT:NT, :], a["ctx"][0].rearrange("(t p) n -> p t n", p=P)).then_inc(sem("x_landed"), 16)
                columns(base, w_in, 0, 4)
                columns(base + 4, w_in, W, 4)
                columns(base + 8, w_in, 3 * W, 12)
                sp.wait_ge(phase_end, 4 * (ph + 1))
                rb_l = sem("rb")
                if l == 0:
                    sp.wait_ge(sem("bias_spread"), 16 * DEPTH * ROWS)
                src = lambda q, c0, c1, at_: bias_wide[l, q, c0:c1, :, at_:at_ + 32]
                sp.dma_start(rb[:, 0].rearrange("p h r c -> p (h r) c"),
                             bias_wide[l].rearrange("q c r k -> (q c) r k")[:, :, 8:40]).then_inc(rb_l, 16)
                for q in range(ROWS):
                    for e in range(2):
                        sp.dma_start(rb[16 * q + 8 * e:16 * q + 8 * e + 8, 1].rearrange("p h r c -> p (h r) c"),
                                     src(q, 8 * e, 8 * e + 8, 16 - 16 * e)).then_inc(rb_l, 16)
                rows(base + 20, w_in, 2 * W, 4)
                rows(base + 24, w_in, 6 * W, 4)
                sp.wait_ge(sem("v_out_a"), before(l, "v_out_a") + 3)
                sp.wait_ge(sem("v_out_d"), before(l, "v_out_d") + 3)
                sp.dma_start(v_mid.rearrange("(t p) n -> p t n", p=P), v_nat[:]).then_inc(sem("v_saved"), 16)
                sp.wait_ge(sem("v_saved"), 16 * (l + 1))
                for j in range(LT):
                    sp.dma_start(na_v[:, j, :], v_mid.rearrange("(r j c) n -> j r c n", j=4, c=16)[j]).then_inc(sem("v_sorted"), 16)
                sp.wait_ge(phase_end, 4 * (ph + 2))
                if l == 0:
                    for la, i0, i1 in ((0, 2, 6), (1, 0, 6)):
                        va = a["ada_w"][la].rearrange("(k p) n -> p k n", p=P)
                        with sp.Fori(i0, i1) as i:
                            for j in range(2):
                                sp.wait_ge(ada_used, i * 2 + ((12 if la else 0) + j + 1))
                                sp.dma_start(ada_ring[j][:], va[:, :, ds(i * 1024 + j * 512, 512)]).then_inc(al[j], 16)
                sp.wait_ge(phase_end, 4 * (ph + 4))
                wo = a["w_out"][l].rearrange("(j two p) n -> j p two n", p=P, two=2)
                for j in range(8):
                    w_chunk(base + 28 + j, wo[j % 4, :, :, 512 * (j // 4):512 * (j // 4) + 512], 2, base + j)
                    if j == 1:
                        for t0, t1, first in ((0, LT, a["x"][0]), (LT, NT, a["ctx"][0])):
                            src = first.rearrange("(t p) n -> p t n", p=P) if l == 0 else x_mid[:, t0:t1, :]
                            sp.dma_start(x_sb[:, t0:t1, :], src).then_inc(sem("x_landed"), 16)
                up = a["ffn_up"][l].rearrange("(k p) n -> p k n", p=P)
                with sp.Fori(0, FT) as i:
                    for j in range(2):
                        w_chunk(i * 2 + (base + 36 + j), up[:, :, ds(i * P + j * DFF, P)], KT, j)
                for h in range(2):
                    rows(base + 36 + 2 * FT + 11 * h, a["ffn_down"][l], 512 * h, 11)
                if l < DEPTH - 1:
                    vector_loads(l + 1)
                sp.wait_ge(phase_end, 4 * (ph + PH))
                if l < DEPTH - 1:
                    sp.dma_start(x_mid, x_sb[:]).then_inc(sem("x_saved"), 16)
                    sp.wait_ge(sem("x_saved"), 16)
                else:
                    sp.dma_start(a["out"][0].rearrange("(t p) n -> p t n", p=P), x_sb[:, 0:LT, :]).then_inc(sem("stored"), 16)
                    sp.wait_ge(sem("stored"), 16)

        @block.gpsimd
        def _(pool):
            w_hi_ready, w_lo_ready, w_used = sem("w_hi_ready"), sem("w_lo_ready"), sem("w_used")
            own = Chain(pool, sem("pool_steps"))
            own.did(pool.memset(eps_t[:], EPS))
            own.did(pool.memset(ones[:], 1.0))
            pool.memset(zeros[:], 0.0).then_inc(sem("zero_tile"), 1)
            pool.drain().then_inc(w_lo_ready, 2)

            def low_parts(first, chunks):
                with pool.Fori(0, chunks // 2) as i:
                    for j in range(2):
                        pool.wait_ge(w_hi_ready, i * 2 + (first + j + 1))
                        pool.wait_ge(w_used, i * 2 + (first + j + 1))
                        pool.tensor_tensor(w_lo[:, j, :], w_raw[:, j, :], w_hi[:, j, :].bitcast(F32),
                                           ALU.subtract).then_inc(w_lo_ready, 1)

            def delta(l):
                def wide(x):
                    return x.unsqueeze(2).to_broadcast([P, H, C])

                def start(k):
                    mask = lambda i: bmask[i].unsqueeze(1).to_broadcast([P, H, C])
                    if k > 1:
                        pool.wait_ge(sem("egi"), before(l, "egi") + 4 * (k - 1))
                    for d in range(2):
                        t = TILES[d][k]
                        if k > 1:
                            pool.wait_ge(sem("group_done"), before(l, "group_done") + 2 * (k - 2) + d + 1)
                        gb = wide(graw[:, t, 8 * d:8 * d + 8])
                        pool.tensor_tensor(ra[d][:], mask(d), gb, ALU.mult).then_inc(sem("ra"), 1)
                        pool.tensor_tensor(rbb[d][:], mask(2 + d), gb, ALU.mult).then_inc(sem("ra"), 1)
                    for d in range(2):
                        t = TILES[d][k]
                        x1, x2 = e1[k % 2][d], e2[k % 2][d]
                        pool.wait_ge(sem("exps"), before(l, "exps") + 4 * k + 2 * d + 2)
                        own.did(pool.tensor_tensor(x1[:], x1[:], wide(nbe[:, t, 8 * d:8 * d + 8]), ALU.mult))
                        pool.tensor_tensor(x2[:], x2[:], mask(2 + d), ALU.mult).then_inc(sem("em"), 1)
                        own.wait()
                        pool.tensor_tensor(x1[:], x1[:], mask(d), ALU.mult).then_inc(sem("em"), 1)

                def finish(k):
                    for d in range(2):
                        g, t = 2 * k + d, TILES[d][k]
                        if d == 0:
                            n = 4 * min(k + 2, NT)
                            pool.wait_ge(sem("diffs"), before(l, "diffs") + n)
                        kk = qkv[:, t, W:2 * W].rearrange("p (h c) -> p h c", h=H)
                        qq = qkv[:, t, 0:W].rearrange("p (h c) -> p h c", h=H)
                        if k == NT - 1 and d == 0:
                            pool.wait_ge(sem("group_done"), before(l, "group_done") + 2 * k)
                        if g:
                            pool.wait_ge(sem("egi"), before(l, "egi") + 2 * g)
                        pool.tensor_tensor(ra[d][:], kk, wide(nbec[:, d, t, :]), ALU.mult).then_inc(sem("kq"), 1)
                        pool.tensor_tensor(rbb[d][:], qq, wide(e_cum[:, d, t, :]), ALU.mult).then_inc(sem("kq"), 1)
                        if k:
                            pool.wait_ge(sem("chained"), before(l, "chained") + 4 * k)
                        pool.wait_ge(sem("kq"), before(l, "kq") + 2 * g + 2)
                        for c in range(2):
                            tot = e_tot[64:128, c, t, 8 * d:8 * d + 8].unsqueeze(2).to_broadcast([64, H, C])
                            pool.tensor_tensor(st_b[d][64:128, c, :, 64:128], ti[64:128].unsqueeze(1).to_broadcast([64, H, C]), tot, ALU.mult).then_inc(sem("egi"), 1)

                pool.wait_ge(sem("gates"), before(l, "gates") + 1)
                pool.wait_ge(sem("qk_normed"), before(l, "qk_normed") + NT)
                start(0)
                for k in range(NT):
                    if k + 1 < NT:
                        start(k + 1)
                    finish(k)

            def rotate(l):
                for t in range(NT):
                    x = qkv[:, t, 0:2 * W].rearrange("p (n c) -> p n c", c=DH)
                    m = pool.tensor_tensor(x, x, qk_rt[:, t, :].unsqueeze(2).to_broadcast([P, 2 * H, DH]), ALU.mult)
                    if t < LT:
                        own.did(m)
                        own.wait()
                        xx = qkv[:, t, 0:2 * W].rearrange("p (n a c) -> p n a c", a=2, c=32)
                        rr = rot[:].rearrange("p s (n a c) -> p s n a c", a=2, c=32)
                        for a_ in range(2):
                            for k in range(2):
                                m = pool.tensor_tensor(rr[:, k, :, a_], xx[:, :, a_], cs[:, t, k, :].unsqueeze(1).to_broadcast([P, 2 * H, 32]), ALU.mult)
                        own.did(m)
                        own.wait()
                        pool.tensor_tensor(xx[:, :, 0], rr[:, 0, :, 0], rr[:, 1, :, 1], ALU.subtract)
                        m = pool.tensor_tensor(xx[:, :, 1], rr[:, 0, :, 1], rr[:, 1, :, 0], ALU.add)
                        own.did(m)
                        own.wait()
                        pool.drain().then_inc(sem("qk_normed"), 1)
                    else:
                        m.then_inc(sem("qk_normed"), 1)

            for l in range(DEPTH):
                ph, base = l * PH, l * CHUNKS
                phase_ends(pool, True, ph + 1)
                low_parts(base, 28)
                phase_ends(pool, True, ph + 2)
                rotate(l)
                phase_ends(pool, True, ph + 3)
                delta(l)
                phase_ends(pool, True, ph + 4)
                low_parts(base + 28, 8)
                phase_ends(pool, True, ph + 5)
                phase_ends(pool, True, ph + 6)
                low_parts(base + 36, 3 * FT)
                phase_ends(pool, True, ph + 7)

        @block.tensor
        def _(pe):
            w_lo_ready, w_used = sem("w_lo_ready"), sem("w_used")
            al = [sem(f"ada_landed{i}") for i in range(2)]
            pe.drain().then_inc(w_used, 2)
            pe.drain().then_inc(sem("ada_used"), 2)
            pe.wait_ge(sem("consts"), 16 * (4 + 2 * DEPTH))
            pe.wait_ge(sem("pool_steps"), 2)

            def spans(l):
                return [(0, 0, LAT)] if lat_only(l) else [(0, 0, LAT), (1, LAT, CTX)]

            def column_tile(slot, bank, sp_):
                for b, c0, n in sp_:
                    for k in range(KT):
                        wk = slice(k * P, k * P + P)
                        o = ps[:, bank + b, 0:n]
                        pe.matmul(o, w_hi[:, slot, wk], h_hi[:, k, c0:c0 + n], start=(k == 0), stop=False)
                        pe.matmul(o, w_hi[:, slot, wk], h_lo[:, k, c0:c0 + n], start=False, stop=False)
                        last = pe.matmul(o, w_lo[:, slot, wk], h_hi[:, k, c0:c0 + n], start=False, stop=(k == KT - 1))
                last.then_inc(w_used, 1)

            def row_chunk(n, hi, lo, tiles, first, last_, banks=0):
                pe.wait_ge(w_lo_ready, n + 3)
                s = n % 2
                for kk in range(2):
                    rhs_h, rhs_l = w_hi[:, s, kk * 512:kk * 512 + 512], w_lo[:, s, kk * 512:kk * 512 + 512]
                    for t in range(tiles):
                        o = ps[:, banks + t, :]
                        pe.matmul(o, hi(kk, t), rhs_h, start=(first and kk == 0), stop=False)
                        pe.matmul(o, hi(kk, t), rhs_l, start=False, stop=False)
                        m = pe.matmul(o, lo(kk, t), rhs_h, start=False, stop=(last_ and kk == 1))
                m.then_inc(w_used, 1)

            def vectors(l):
                pe.wait_ge(sem("rows"), before(l, "rows") + 16 * 11)
                pe.transpose(ps[:, 0, 0:P], row_ffn[:], ident).then_inc(sem("vec_t"), 1)
                pe.transpose(ps[:, 1, 0:121], row_vec[0:121, :], ident[0:121, 0:121]).then_inc(sem("vec_t"), 1)
                if l == 0:
                    pe.transpose(ps[:, 2, 0:16], row_c[:], ident[0:16, 0:16]).then_inc(sem("vec_t"), 1)
                    pe.wait_ge(sem("cond_ready"), 1)
                    for u in range(4):
                        pe.wait_ge(sem(f"ada_first{u}"), 16)
                        for half in range(2):
                            modulation(ps[0:2, 4 + u, :], ada_first[u], half)
                    pe.wait_ge(sem("mod_rows"), 4)
                    for u in range(4):
                        m = mod_columns(ps[:, 3, 8 * u:8 * u + 8], mod_first[:, u])
                    m.then_inc(sem("mods_done"), 1)

            def modulation(o, w, half):
                cc = cond[:].rearrange("p (s k) -> p k s", s=2)
                for k in range(half * KT // 2, (half + 1) * KT // 2):
                    m = pe.matmul(o, cc[:, k, :], w[:, k, :], start=(k == 0), stop=(k == KT - 1))
                if half:
                    m.then_inc(sem("ada_used"), 1)

            def mod_columns(o, rows_):
                for i in range(4):
                    m = pe.transpose(o[:, 2 * i:2 * i + 2], rows_[:, i * P:i * P + P], ident[0:2, 0:2])
                return m

            def hidden(l, which):
                s = sem(f"hid_t{which}")
                tiles = LT if (which and lat_only(l)) else NT
                for k in range(KT):
                    for b, t0, t1 in ((0, 0, LT), (1, LT, tiles)):
                        if k >= 2:
                            pe.wait_ge(sem(f"hid_v{which}"), before(l, f"hid_v{which}") + (k - 1) * (2 if tiles == NT else 1))
                        for t in range(t0, t1):
                            if k == 0:
                                pe.wait_ge(sem(f"normed{which}"), before(l, f"normed{which}") + t + 1)
                            m = pe.transpose(ps[:, 2 * (k % 2) + b, (t - t0) * P:(t - t0 + 1) * P], xn[:, t, k * P:k * P + P], ident)
                        if t1 > t0:
                            m.then_inc(s, 1)

            def project(l):
                base = l * CHUNKS
                free = sem("proj_free")
                sp_ = [(0, 0, LAT), (1, LAT, CTX)]
                pe.wait_ge(sem("h_ready0"), before(l, "h_ready0") + 2 * KT)
                for t in range(8):
                    pe.wait_ge(w_lo_ready, base + t + 3)
                    if t >= 2:
                        pe.wait_ge(free, t - 1)
                    column_tile(t % 2, 2 * (t % 2), spans(l) if t < 4 else sp_)

                def turn(t, r):
                    pe.wait_ge(sem("conv"), before(l, "conv") + t + 1)
                    pe.wait_ge(sem("qkv_out"), before(l, "qkv_out") + t + 1)
                    for tt in range(NT):
                        m = pe.transpose(ps[:, 4 + 2 * r + tt // 4, (tt % 4) * P:(tt % 4 + 1) * P], cvs[:, r, col(tt)], ident)
                    m.then_inc(sem("turned"), 1)

                def pair(i, first):
                    for j in range(2):
                        pe.wait_ge(w_lo_ready, i * 2 + (base + 8 + j + 3))
                        if first:
                            pe.wait_ge(free, 7 + j)
                        else:
                            pe.wait_ge(sem("taps"), before(l, "taps") + i * 2 + (j - 1))
                        column_tile(j, 2 * j, sp_)
                        if not (first and j == 0):
                            turn(i * 2 + (j - 1), (j - 1) % 2)
                pair(0, True)
                with pe.Fori(1, 6) as i:
                    pair(i, False)
                turn(11, 1)
                pe.wait_ge(sem("taps"), before(l, "taps") + 12)
                pe.wait_ge(sem("qkv_out"), before(l, "qkv_out") + 14)
                for j in range(4):
                    row_chunk(base + 20 + j, lambda kk, t: h_hi[:, 2 * j + kk, col(t)],
                              lambda kk, t: h_lo[:, 2 * j + kk, col(t)], NT, j == 0, j == 3)
                pe.wait_ge(sem("bd_split"), before(l, "bd_split") + 1)
                for t in range(NT):
                    for k in range(KT):
                        o = ps[:, 7, 32 * t:32 * t + 32]
                        pe.matmul(o, h_hi[:, k, col(t)], bd_hi[:, k, :], start=(k == 0), stop=False)
                        pe.matmul(o, h_hi[:, k, col(t)], bd_lo[:, k, :], start=False, stop=False)
                        m = pe.matmul(o, h_lo[:, k, col(t)], bd_hi[:, k, :], start=False, stop=(k == KT - 1))
                m.then_inc(sem("bd_done"), 1)
                pe.wait_ge(sem("v_out_a"), before(l, "v_out_a") + 3)
                pe.wait_ge(sem("v_out_d"), before(l, "v_out_d") + 3)
                for j in range(4):
                    row_chunk(base + 24 + j, lambda kk, t: h_hi[:, 2 * j + kk, col(t)],
                              lambda kk, t: h_lo[:, 2 * j + kk, col(t)], LT if lat_only(l) else NT, j == 0, j == 3)

            def attend(l):
                items = [(h, u) for h in range(H) for u in range(LT if lat_only(l) else NT)]
                per = LT if lat_only(l) else NT
                kt4 = lambda hp_, pr: na_k[64 * hp_:64 * hp_ + 64, pr, 0:LAT].rearrange("p (j n) -> p j n", j=4)

                def scores(n):
                    h, u = items[n]
                    s_, e_ = h % 2, h // 2
                    q = na_q[64 * s_:64 * s_ + 64, e_, u * P:u * P + P]
                    b = n % 2
                    if n >= 2:
                        pe.wait_ge(sem("exped"), before(l, "exped") + n - 1)
                    kc = na_k[64 * s_:64 * s_ + 64, e_, LAT:TOK]
                    if u < LT:
                        win = kt4(s_, e_)[:, u:u + 2, :] if u < 3 else kt4(s_, e_)[:, 0:4:3, :]
                        pe.matmul(ps[:, b, 0:256], q, win, start=True, stop=True)
                        pe.matmul(ps[:, b, 256:512], q, kc, start=True, stop=True).then_inc(sem("scored"), 1)
                    else:
                        pe.matmul(ps[:, b, 256:512], q, kc, start=True, stop=True).then_inc(sem("scored"), 1)

                def turn(n):
                    h, u = items[n]
                    b = 2 + n % 2
                    pe.wait_ge(sem("probs"), before(l, "probs") + n + 1)
                    if l == 0 and n % 2 and 3 <= n < 2 * UNITS + 3:
                        v = (n - 3) // 2
                        pe.wait_ge(sem("mod_rows"), 4 + v + 1)
                        pairs = h // 2 if h % 2 or u >= 5 else h // 2 - 1
                        if pairs > 0:
                            pe.wait_ge(sem("o_out"), pairs)
                        mod_columns(ps[:, 6, 256 + 8 * v:264 + 8 * v], mod_row[:]).then_inc(sem("mods_done"), 1)
                    if n >= 2:
                        out = "pt_odd" if n % 2 else "pt_even"
                        pe.wait_ge(sem(out), before(l, out) + n // 2)
                    for w in range(0 if u < LT else 2, 4):
                        m = pe.transpose(ps[:, b, w * P:w * P + P], prob[:, n % 2, w * P:w * P + P], ident)
                    m.then_inc(sem("p_turned"), 1)

                def values(h):
                    s_, e_, r = h % 2, h // 2, h % 2
                    pe.wait_ge(sem("pt_even"), before(l, "pt_even") + per * (h + 1) // 2)
                    pe.wait_ge(sem("pt_odd"), before(l, "pt_odd") + per * (h + 1) // 2)
                    if h >= 4 and h % 2 == 0:
                        pe.wait_ge(sem("o_out"), before(l, "o_out") + e_ - 1)
                    o = ps[64 * s_:64 * s_ + 64, 4 + e_ % 2, :]
                    vh = lambda t: na_v[:, t, 64 * h:64 * h + 64]
                    for e in range(2):
                        pe.matmul(o, vh(4 + e), pt[:, r, 8 + 4 * e:12 + 4 * e, :], start=(e == 0), stop=False, skip_group_check=True)
                    o4 = o.rearrange("p (u n) -> p u n", u=4)
                    outs = [o4[:, 0:4:3, :], o4[:, 0:2, :], o4[:, 1:3, :], o4[:, 2:4, :]]
                    for j in range(4):
                        m = pe.matmul(outs[j], vh(j), pt[:, r, 2 * j:2 * j + 2, :], start=False, stop=(j == 3), skip_group_check=True)
                    if not lat_only(l):
                        if e_ and s_ == 0:
                            pe.wait_ge(sem("o_out"), before(l, "o_out") + e_)
                        o = ps[64 * s_:64 * s_ + 64, 6, 0:256]
                        for e in range(2):
                            m = pe.matmul(o, vh(4 + e), pt[:, r, 16 + 2 * e:18 + 2 * e, :], start=(e == 0), stop=(e == 1))
                    m.then_inc(sem("valued"), 1)

                pe.wait_ge(sem("rb_masked"), before(l, "rb_masked") + 1)
                pe.wait_ge(sem("v_sorted"), 16 * LT * (l + 1))
                scores(0)
                scores(1)
                for n in range(len(items)):
                    if n + 2 < len(items):
                        scores(n + 2)
                    if l == 0 and n < 2 * UNITS:
                        v = n // 2
                        pe.wait_ge(al[v % 2], 16 * (v // 2 + 1))
                        modulation(ps[64 * (v % 2):64 * (v % 2) + 2, 7, :], ada_ring[v % 2], n % 2)
                    turn(n)
                    if n % per == 2 and n >= per:
                        values(n // per - 1)
                values(H - 1)

            def delta_prep(l):
                pe.wait_ge(sem("decays"), before(l, "decays") + 1)
                gd = lambda d: graw[:, :, 8 * d:8 * d + 8]
                for d in range(2):
                    pe.matmul(ps[:, 4, 48 * d:48 * d + 48], amask[(LE, GE)[d]], gd(d), start=True, stop=True)
                    pe.matmul(ps[:, 4, 96 + 48 * d:144 + 48 * d], amask[(GT, LT_)[d]], gd(d), start=True, stop=True)
                for c in range(2):
                    m = pe.matmul(ps[:, 5, 96 * c:96 * c + 96], onec[c], graw[:].rearrange("p t n -> p (t n)"), start=True, stop=True)
                m.then_inc(sem("sums"), 1)
                for t in range(NT):
                    pe.wait_ge(sem("qk_normed"), before(l, "qk_normed") + t + 1)
                    if t >= 2:
                        pe.wait_ge(sem("qk_out"), before(l, "qk_out") + t - 1)
                    for i in range(8):
                        m = pe.transpose(ps[:, 2 * (t % 2) + i // 4, (i % 4) * P:(i % 4 + 1) * P], qkv[:, t, i * P:i * P + P], ident)
                    m.then_inc(sem("qk_turned"), 1)
                pe.wait_ge(sem("qk_out"), before(l, "qk_out") + NT)
                pe.wait_ge(sem("gates"), before(l, "gates") + 1)

            def diff(l, k, d, i):
                n = 4 * k + 2 * d + i
                pe.wait_ge(sem("ra"), before(l, "ra") + n + 1)
                if k and not (d or i):
                    pe.wait_ge(sem("m_ready"), before(l, "m_ready") + 4 * k)
                elif d or i:
                    pe.wait_ge(sem("exps"), before(l, "exps") + n)
                mask, x = amask[((LE, GE)[d], (GT, LT_)[d])[i]], (ra, rbb)[i][d]
                pe.matmul(ps[:, 5, :], mask, x[:].rearrange("p h c -> p (h c)"), start=True, stop=True).then_inc(sem("diffs"), 1)

            def gram(l, k, d, s_):
                n, t = 4 * k + 2 * d + s_, TILES[d][k]
                if d or s_:
                    pe.wait_ge(sem("m_ready"), before(l, "m_ready") + n)
                else:
                    pe.wait_ge(sem("exps"), before(l, "exps") + 4 * k + 4)
                for e_ in range(HP):
                    for c in range(2):
                        tk = slice(t * P + 64 * c, t * P + 64 * c + 64)
                        kk = k_t[64 * s_:64 * s_ + 64, e_, tk]
                        pe.matmul(ps[64 * c:64 * c + 64, 5, 64 * e_:64 * e_ + 64], kk, kk, start=True, stop=True)
                        m = pe.matmul(ps[64 * c:64 * c + 64, 5, 256 + 64 * e_:320 + 64 * e_], kk,
                                      q_t[64 * s_:64 * s_ + 64, e_, tk], start=True, stop=True)
                m.then_inc(sem("gram"), 1)

            def level_z(l, k, d, s):
                if s == 0:
                    pe.wait_ge(sem("m_ready"), before(l, "m_ready") + 4 * k + 4)
                    pe.wait_ge(sem("xt_init"), before(l, "xt_init") + 2 * k + d + 1)
                    if k:
                        pe.wait_ge(sem("wq_out"), before(l, "wq_out") + 2 * (k - 1) + d + 1)
                else:
                    pe.wait_ge(sem(f"xt_new{d}"), before(l, f"xt_new{d}") + k * LEVELS + s)
                    pe.wait_ge(sem(f"xb_new{d}"), before(l, f"xb_new{d}") + k * LEVELS + s)
                for h in range(H):
                    m = pe.matmul(ps[64 * (h % 2):64 * (h % 2) + 64, 2 * d, P * (h // 2):P * (h // 2) + P], e1[k % 2][d][:, h, :],
                                  xtb[k % 2][d][:, h, :, :].rearrange("p a b -> p (a b)"), start=True, stop=True)
                m.then_inc(sem(f"z_done{d}"), 1)

            def level_p(l, k, d, s):
                i = k * LEVELS + s
                if s:
                    pe.wait_ge(sem(f"xq_new{d}"), before(l, f"xq_new{d}") + k * (LEVELS - 1) + s)
                pe.wait_ge(sem(f"zb_a{d}"), before(l, f"zb_a{d}") + i + 1)
                pe.wait_ge(sem(f"zb_d{d}"), before(l, f"zb_d{d}") + i + 1)
                for e_ in range(HP):
                    for c in range(2):
                        lhs = (xq0 if s == 0 else xq[d][:, e_, :])[:, 64 * c:64 * c + 64]
                        m = pe.matmul(ps[64 * c:64 * c + 64, 2 * d + 1, P * e_:P * e_ + P], lhs,
                                      zb[d][:, e_, c, :, :].rearrange("p a b -> p (a b)"), start=True, stop=True)
                m.then_inc(sem(f"p_done{d}"), 1)

            def level_t(l, k, d, s):
                pe.wait_ge(sem(f"xc_new{d}"), before(l, f"xc_new{d}") + k * LEVELS + s + 1)
                pe.wait_ge(sem(f"xt_new{d}"), before(l, f"xt_new{d}") + k * LEVELS + s + 1)
                for e_ in range(HP):
                    m = pe.transpose(ps[:, 2 * d + 1, P * e_:P * e_ + P], xtc[k % 2][d][:, 2 * e_:2 * e_ + 2, :].rearrange("p a b -> p (a b)"), ident)
                m.then_inc(sem(f"xt_turned{d}"), 1)

            def group_end(l, k, d):
                g = 2 * k + d
                pe.wait_ge(sem(f"xt_new{d}"), before(l, f"xt_new{d}") + k * LEVELS + LEVELS)
                pe.wait_ge(sem(f"xb_new{d}"), before(l, f"xb_new{d}") + k * LEVELS + LEVELS)
                pe.wait_ge(sem("kq"), before(l, "kq") + 2 * g + 2)
                for h in range(H):
                    pe.matmul(ps[64 * (h % 2):64 * (h % 2) + 64, 2 * d, P * (h // 2):P * (h // 2) + P], ra[d][:, h, :],
                              xtb[k % 2][d][:, h, :, :].rearrange("p a b -> p (a b)"), start=True, stop=True)
                for e_ in range(HP):
                    m = pe.transpose(ps[:, 2 * d + 1, P * e_:P * e_ + P], rbb[d][:, 2 * e_:2 * e_ + 2, :].rearrange("p a b -> p (a b)"), ident)
                m.then_inc(sem("group_done"), 1)

            def chain_a(l, n, d):
                k, c = n // 2, (n % 2 if d == 0 else 1 - n % 2)
                i = 2 * n + d
                if n % 2 == 0:
                    pe.wait_ge(sem("wq_out"), before(l, "wq_out") + 2 * k + d + 1)
                    pe.wait_ge(sem("st_ready_d"), before(l, "st_ready_d") + 2 * k + d + 1)
                    pe.wait_ge(sem("egi"), before(l, "egi") + 2 * (2 * k + d) + 2)
                if n:
                    pe.wait_ge(sem(f"state{d}"), before(l, f"state{d}") + n)
                for h in range(H):
                    m = pe.matmul(ps[64 * d:64 * d + 64, 4, 64 * h:64 * h + 64], st_a[d][:, c, h, :], mv_a[d][:, c, h, :], start=True, stop=True)
                m.then_inc(sem(f"vnew_done{d}"), 1)

            def chain_b(l, n, d):
                c = n % 2 if d == 0 else 1 - n % 2
                pe.wait_ge(sem(f"vnew{d}"), before(l, f"vnew{d}") + n + 1)
                if n:
                    pe.wait_ge(sem(f"o_added{d}"), before(l, f"o_added{d}") + n)
                for h in range(H):
                    m = pe.matmul(ps[:, 6 + d, 64 * h:64 * h + 64], st_b[d][:, c, h, :], mv_b[d][:, h, :], start=True, stop=True)
                m.then_inc(sem("chained"), 1)

            def delta(l):
                def both(f):
                    return lambda n: [f(l, n, d) for d in range(2)]
                parts = {"a": both(chain_a), "b": both(chain_b), "diff": lambda k, d, i: diff(l, k, d, i),
                         "gram": lambda k, d, i: gram(l, k, d, i)}

                def group(k):
                    def products(product, s):
                        for d in range(2):
                            product(l, k, d, s)
                    products(level_z, 0)
                    between(k, 0, "z", parts)
                    for s in range(LEVELS):
                        products(level_p, s)
                        between(k, s, "p", parts)
                        if s < LEVELS - 1:
                            products(level_z, s + 1)
                            products(level_t, s)
                            between(k, s, "t", parts)
                            between(k, s + 1, "z", parts)
                    for d in range(2):
                        group_end(l, k, d)
                start_and_end(parts, group)

            def mix_out(l):
                tiles = LT if lat_only(l) else NT
                base = l * CHUNKS + 28

                def chunk(half, j):
                    row_chunk(base + 4 * half + j, lambda kk, t: o_hi[:, 2 * j + kk, col(t)],
                              lambda kk, t: o_lo[:, 2 * j + kk, col(t)], tiles, j == 0, j == 3)
                pe.wait_ge(sem("o_split"), before(l, "o_split") + HP)
                chunk(0, 0)
                chunk(0, 1)
                for t in range(tiles):
                    pe.wait_ge(sem("o_normed"), before(l, "o_normed") + t + 1)
                for e_ in range(HP):
                    if e_:
                        pe.wait_ge(sem("ov_out"), before(l, "ov_out") + e_)
                    for t in range(tiles):
                        m = pe.transpose(ps[:, 6 + t // LT, (t % LT) * P:(t % LT + 1) * P], on[:, t, e_ * P:e_ * P + P], ident)
                    m.then_inc(sem("o_turned"), 1)
                pe.wait_ge(sem("ov_out"), before(l, "ov_out") + HP)
                pe.wait_ge(sem("o_split"), before(l, "o_split") + 2 * HP)
                chunk(0, 2)
                chunk(0, 3)
                pe.wait_ge(sem("y_out_a0"), before(l, "y_out_a0") + tiles // 2)
                pe.wait_ge(sem("y_out_d0"), before(l, "y_out_d0") + tiles // 2)
                for j in range(4):
                    chunk(1, j)

            def gate_rows(l, which):
                n = 2 if lat_only(l) else 4
                for i in range(n):
                    pe.wait_ge(sem(f"gdiag{which}"), before(l, f"gdiag{which}") + i + 1)
                    if i >= 2:
                        pe.wait_ge(sem(f"gate_out{which}"), before(l, f"gate_out{which}") + i - 1)
                    pe.matmul(ps[:, 6 + i % 2, :], ones[:], (gdiag2 if which else gdiag)[:], start=True, stop=True).then_inc(sem(f"gate_done{which}"), 1)

            def ffn_up(l):
                base = l * CHUNKS + 36
                pe.wait_ge(sem("h_ready1"), before(l, "h_ready1") + KT * (1 if lat_only(l) else 2))
                free = sem("up_taps")
                with pe.Fori(0, FT // 2) as i:
                    for j in range(2):
                        for gv in range(2):
                            pe.wait_ge(w_lo_ready, i * 4 + (base + 2 * j + gv + 3))
                            pe.wait_ge(free, i * 4 + (2 * j + gv + 1))
                            column_tile(gv, 4 * j + 2 * gv, spans(l))

            def ffn_down(l):
                base = l * CHUNKS + 36 + 2 * FT
                tiles = LT if lat_only(l) else NT
                used = sem("g_used")
                for half in range(2):
                    if half:
                        pe.wait_ge(sem("y_out_a1"), before(l, "y_out_a1") + tiles // 2)
                        pe.wait_ge(sem("y_out_d1"), before(l, "y_out_d1") + tiles // 2)
                    for j in range(11):
                        n = base + 11 * half + j
                        pe.wait_ge(w_lo_ready, n + 3)
                        s = n % 2
                        for kk in range(2):
                            q = 22 * half + 2 * j + kk
                            pe.wait_ge(sem("g_split"), before(l, "g_split") + q + 1)
                            rh, rl = w_hi[:, s, kk * 512:kk * 512 + 512], w_lo[:, s, kk * 512:kk * 512 + 512]
                            for t in range(tiles):
                                o = ps[:, t, :]
                                pe.matmul(o, g_hi[:, kk, col(t)], rh, start=(j == 0 and kk == 0), stop=False)
                                pe.matmul(o, g_hi[:, kk, col(t)], rl, start=False, stop=False)
                                m = pe.matmul(o, g_lo[:, kk, col(t)], rh, start=False, stop=(j == 10 and kk == 1))
                            if kk == 0:
                                m.then_inc(used, 1)
                            else:
                                m.then_inc(w_used, 1)

            for l in range(DEPTH):
                ph = l * PH
                vectors(l)
                hidden(l, 0)
                phase_ends(pe, True, ph + 1)
                project(l)
                phase_ends(pe, True, ph + 2)
                attend(l)
                phase_ends(pe, True, ph + 3)
                delta_prep(l)
                delta(l)
                phase_ends(pe, True, ph + 4)
                mix_out(l)
                gate_rows(l, 0)
                phase_ends(pe, True, ph + 5)
                hidden(l, 1)
                phase_ends(pe, True, ph + 6)
                ffn_up(l)
                ffn_down(l)
                gate_rows(l, 1)
                phase_ends(pe, True, ph + 7)

        @block.scalar
        def _(act):
            own = Chain(act, sem("act_steps"))
            wl = [sem("w_landed0"), sem("w_landed1")]
            w_hi_ready, w_used = sem("w_hi_ready"), sem("w_used")
            act.wait_ge(sem("consts"), 16 * (4 + 2 * DEPTH))
            act.wait_ge(sem("pool_steps"), 2)

            def high(n, slot, landed):
                act.wait_ge(wl[slot], landed)
                act.wait_ge(w_used, n + 1)
                act.activation(w_hi[:, slot, :], w_raw[:, slot, :], ACT.Copy).then_inc(w_hi_ready, 1)

            def high_at(n):
                high(n, n % 2, 16 * (n // 2 + 1))

            def high_loop(i, base, j, per):
                high(i * per + (base + j), j % 2, i * (8 * per) + 16 * ((base + j) // 2 + 1))

            def vectors(l):
                if l == 0:
                    act.wait_ge(sem("vec_t"), before(l, "vec_t") + 3)
                    act.activation(cond[:], ps[:, 2, 0:16], ACT.Silu).then_inc(sem("cond_ready"), 1)

            def sums(l, name, src, tiles, off, jk):
                for t in range(tiles):
                    own.did(act.activation(jk, src[:, t, :], ACT.Square, accum_out=stat[:, off + t:off + t + 1]))
                    own.wait()
                act.activation(stat[:, off + 8:off + 8 + tiles], stat[:, off:off + tiles], ACT.Sqrt, bias=eps_t[:],
                               scale=1.0 / D).then_inc(sem(name), 1)

            def bias_begin():
                act.wait_ge(sem("zero_tile"), 1)
                for l in range(DEPTH):
                    act.dma_start(bias_wide[l].rearrange("q c r k -> (q c) (r k)").rearrange("p (a n) -> p a n", n=512),
                                  zeros[:].unsqueeze(1).to_broadcast([P, 6, 512])).then_inc(sem("bias_begun"), 16)
                    for q in range(ROWS):
                        act.dma_start(bias_rows[l, q].rearrange("(h r) c -> h r c", h=H), a["rpb"][l, :, 7 - q:15 - q, :]).then_inc(sem("bias_begun"), 16)

            def bias_spread():
                act.wait_ge(sem("bias_begun"), 16 * DEPTH * (ROWS + 1))
                for l in range(DEPTH):
                    for q in range(ROWS):
                        wide = bass.AP(bias_wide.tensor, (l * ROWS + q) * 16 * 64 * 48 + 1, [[64 * 48 + 1, 16], [48, 64], [1, 31]])
                        act.dma_start(wide, bias_rows[l, q].unsqueeze(0).to_broadcast([16, 64, 31])).then_inc(sem("bias_spread"), 16)

            def norm(l, which, tiles):
                if which == 0 and l == 0:
                    act.wait_ge(sem("x_landed"), 32)
                    sums(l, "rms0", x_sb, tiles, 0, v_junk)
                    bias_begin()
                n = 0
                for k in range(KT):
                    for b, c0, w in ((0, 0, LAT), (1, LAT, CTX)):
                        if b and tiles == LT:
                            continue
                        n += 1
                        act.wait_ge(sem(f"hid_t{which}"), before(l, f"hid_t{which}") + n)
                        if n == 1:
                            act.wait_ge(sem("mods"), before(l, "mods") + 1)
                        act.activation(h_hi[:, k, c0:c0 + w], ps[:, 2 * (k % 2) + b, 0:w], ACT.Identity,
                                       scale=sc_pre[:, which, k, b:b + 1], bias=mod[:, (3 * which) * KT + k, b:b + 1]).then_inc(sem(f"hid_h{which}"), 1)

            def next_norm(l, which, name, tiles, jk):
                for t in range(tiles):
                    act.wait_ge(sem(f"summed{which}"), before(l, f"summed{which}") + t + 1)
                    own.did(act.activation(jk, x_sb[:, t, :], ACT.Square, accum_out=stat[:, t:t + 1]))
                    own.wait()
                act.activation(stat[:, 8:8 + tiles], stat[:, 0:tiles], ACT.Sqrt, bias=eps_t[:], scale=1.0 / D).then_inc(sem(name), 1)

            def project(l):
                base = l * CHUNKS
                free = sem("proj_free")
                high_at(base)
                if l == 0:
                    bias_spread()
                own.did(act.activation(bd_hi[:], bd_raw[:], ACT.Copy))
                act.drain().then_inc(sem("bd_h"), 1)
                for t in range(8):
                    high_at(base + t + 1)
                    act.wait_ge(w_used, base + t + 3)
                    b = 2 * (t % 2)
                    e = t % 4
                    if t < 4:
                        src = ps[:, b, :].rearrange("p (r c) -> p r c", c=GRID)
                        act.activation(na_q[:, e, 0:384].rearrange("p (u r c) -> p u r c", u=3, r=ROWS),
                                       src[:, :, 8:56].rearrange("p r (u c) -> p u r c", c=16), ACT.Copy, scale=DH ** -0.5)
                        for s_ in range(2):
                            m = act.activation(na_q[:, e, 384:512].rearrange("p (r s c) -> p s r c", r=ROWS, s=2)[:, s_],
                                               src[:, :, 56 * s_:56 * s_ + 8], ACT.Copy, scale=DH ** -0.5)
                        if not lat_only(l):
                            m = act.activation(na_q[:, e, LAT:TOK], ps[:, b + 1, 0:CTX], ACT.Copy, scale=DH ** -0.5)
                        m.then_inc(free, 1)
                    else:
                        act.activation(na_k[:, e, 0:LAT].rearrange("p (j r c) -> p j r c", j=4, r=ROWS),
                                       ps[:, b, :].rearrange("p (r j c) -> p j r c", j=4, c=16), ACT.Copy)
                        act.activation(na_k[:, e, LAT:TOK], ps[:, b + 1, 0:CTX], ACT.Copy).then_inc(free, 1)

                def conv(i, j):
                    high_loop(i, base + 8, j + 1, 2)
                    act.wait_ge(w_used, i * 2 + (base + 8 + j + 3))
                    act.wait_ge(sem("turned"), before(l, "turned") + i * 2 + (j + 1))
                    act.activation(cv[:, j, :], ps[:, 2 * j:2 * j + 2, :].rearrange("p a b -> p (a b)")[:, 0:TOK], ACT.Copy,
                                   scale=vec[l][:, ds(i * 2 + (16 + j), 1)]).then_inc(sem("mid"), 1)
                    act.wait_ge(sem("taps"), before(l, "taps") + i * 2 + (j + 1))
                    act.activation(cvs[:, j, :], cv[:, j, :], ACT.Silu).then_inc(sem("conv"), 1)
                act.drain().then_inc(sem("turned"), 2)
                with act.Fori(0, 6) as i:
                    for j in range(2):
                        conv(i, j)
                for j in range(4):
                    high_at(base + 21 + j)
                act.wait_ge(w_used, base + 23 + 3)
                for t in range(0, NT, 2):
                    act.activation((v_nat if t < LT else na_v)[:, t, :], ps[:, t, :], ACT.Copy).then_inc(sem("v_out_a"), 1)
                act.wait_ge(sem("qkv_out"), before(l, "qkv_out") + 14)
                for j in range(3):
                    high_at(base + 25 + j)
                    for t in (2 * j, 2 * j + 1):
                        if t:
                            act.wait_ge(sem("qk_summed"), before(l, "qk_summed") + t)
                        own.did(act.activation(sq[:], qkv[:, t, 0:2 * W], ACT.Square))
                        act.drain().then_inc(sem("qk_sq"), 1)
                act.wait_ge(sem("qk_summed"), before(l, "qk_summed") + NT)
                act.activation(qk_rt[:], qk_ss[:], ACT.Sqrt, bias=eps_t[:]).then_inc(sem("qk_root"), 1)
                act.wait_ge(w_used, base + 27 + 3)
                for t in range(LT if lat_only(l) else NT):
                    own.did(act.activation(z_sb[:, t, :], ps[:, t, :], ACT.Silu))

            def attend(l):
                tiles = LT if lat_only(l) else NT
                items = [(h, u) for h in range(H) for u in range(tiles)]
                steps = len(items)
                for n in range(steps + 1):
                    if n < steps:
                        h, u = items[n]
                        act.wait_ge(sem("maxed"), before(l, "maxed") + n + 1)
                        if n >= 2:
                            act.wait_ge(sem("p_turned"), before(l, "p_turned") + n - 1)
                        c0 = 0 if u < LT else 256
                        own.did(act.activation(prob[:, n % 2, c0:512], ps[:, n % 2, c0:512], ACT.Exp, bias=stat[:, n % 2:n % 2 + 1],
                                               accum_out=stat[:, 2 + n % 2:3 + n % 2]))
                        act.drain().then_inc(sem("exped"), 1)
                    if n >= 1:
                        h, u = items[n - 1]
                        if n % 2:
                            act.wait_ge(sem("p_turned"), before(l, "p_turned") + n)
                            if h >= 2 and u == 0:
                                act.wait_ge(sem("valued"), before(l, "valued") + h - 1)
                            for dst, src in turned(n - 1, u, h):
                                act.activation(dst, src, ACT.Copy)
                            act.drain().then_inc(sem("pt_even"), 1)
                        if u == 3 and h >= 2 and h % 2 == 0:
                            act.wait_ge(sem("p_turned"), before(l, "p_turned") + n)
                            out_pair(l, h // 2 - 1)
                out_pair(l, HP - 1)

            def out_pair(l, e):
                act.wait_ge(sem("valued"), before(l, "valued") + 2 * e + 2)
                b = 4 + e % 2
                dst = o_t[:, e, 0:LAT].rearrange("p (r c) -> p r c", c=GRID)
                act.activation(dst[:, :, 8:56].rearrange("p r (u c) -> p u r c", c=16),
                               ps[:, b, 0:384].rearrange("p (u r c) -> p u r c", u=3, r=ROWS), ACT.Copy)
                for s_ in range(2):
                    own.did(act.activation(dst[:, :, 56 * s_:56 * s_ + 8],
                                           ps[:, b, 384:512].rearrange("p (r s c) -> p s r c", r=ROWS, s=2)[:, s_], ACT.Copy))
                if not lat_only(l):
                    own.did(act.activation(o_t[:, e, LAT:TOK], ps[:, 6, 0:CTX], ACT.Copy))
                act.drain().then_inc(sem("o_out"), 1)

            def delta_prep(l):
                own.did(act.activation(beta[:], bd[:, :, 0:16], ACT.Sigmoid))
                act.wait_ge(sem("dec_abs"), before(l, "dec_abs") + 1)
                own.did(act.activation(gtmp[:, 1], gtmp[:, 1], ACT.Exp, scale=-1.0))
                own.wait()
                act.activation(gtmp[:, 1], gtmp[:, 1], ACT.Ln, bias=1.0)
                own.did(act.activation(a_exp[:], al_dt[:, l, 0, :], ACT.Exp))
                act.drain().then_inc(sem("dec_ln"), 1)
                act.wait_ge(sem("sums"), before(l, "sums") + 1)
                for d in range(2):
                    act.activation(e_cum[:, d], ps[:, 4, 48 * d:48 * d + 48].rearrange("p (t h) -> p t h", h=H), ACT.Exp)
                    act.activation(e_tail[:, d], ps[:, 4, 96 + 48 * d:144 + 48 * d].rearrange("p (t h) -> p t h", h=H), ACT.Exp)
                own.did(act.activation(e_tot[:], ps[:, 5, 0:192].rearrange("p (c t h) -> p c t h", c=2, t=NT), ACT.Exp))
                act.drain().then_inc(sem("e_ready"), 1)
                for t in range(NT):
                    act.wait_ge(sem("qk_turned"), before(l, "qk_turned") + t + 1)
                    act.activation(q_t[:, :, col(t)], ps[:, 2 * (t % 2), :].rearrange("p (e n) -> p e n", e=HP), ACT.Copy)
                    own.did(act.activation(k_t[:, :, col(t)], ps[:, 2 * (t % 2) + 1, :].rearrange("p (e n) -> p e n", e=HP), ACT.Copy))
                    act.drain().then_inc(sem("qk_out"), 1)

            def level(l, k, d, s):
                act.wait_ge(sem(f"z_done{d}"), before(l, f"z_done{d}") + k * LEVELS + s + 1)
                act.activation(zb[d][0:64, :, :, 0, :], ps[0:64, 2 * d, :].rearrange("p (e c n) -> p e c n", e=HP, c=2), ACT.Copy).then_inc(sem(f"zb_a{d}"), 1)

            def level_x(l, k, d, s):
                act.wait_ge(sem(f"xt_turned{d}"), before(l, f"xt_turned{d}") + k * (LEVELS - 1) + s + 1)
                act.activation(xq[d][:], ps[:, 2 * d + 1, :].rearrange("p (e n) -> p e n", e=HP), ACT.Copy).then_inc(sem(f"xq_new{d}"), 1)

            def delta(l):
                def diff(k, d, i):
                    n = 4 * k + 2 * d + i
                    if k > 1 and i == 0:
                        act.wait_ge(sem("group_done"), before(l, "group_done") + 2 * (k - 2) + d + 1)
                    act.wait_ge(sem("diffs"), before(l, "diffs") + n + 1)
                    act.activation((e1, e2)[i][k % 2][d][:].rearrange("p h c -> p (h c)"), ps[:, 5, :], ACT.Exp).then_inc(sem("exps"), 1)
                    if d and i:
                        for d_ in range(2):
                            if k > 1:
                                act.wait_ge(sem("st_ready_d"), before(l, "st_ready_d") + 2 * (k - 2) + d_ + 1)
                            act.activation(xtc[k % 2][d_][:], ti.unsqueeze(1).to_broadcast([P, H, C]), ACT.Copy)
                            act.activation(xtb[k % 2][d_][:].rearrange("p h a b -> p h (a b)"),
                                           ident.unsqueeze(1).to_broadcast([P, H, P]), ACT.Copy)
                            act.drain().then_inc(sem("xt_init"), 1)

                def new_values(n):
                    for d in range(2):
                        act.wait_ge(sem(f"vnew_done{d}"), before(l, f"vnew_done{d}") + n + 1)
                        act.activation(mv_b[d][0:64].rearrange("p h c -> p (h c)"), ps[64 * d:64 * d + 64, 4, :], ACT.Copy).then_inc(sem(f"vnew{d}"), 1)

                def state(n):
                    for d in range(2):
                        c = n % 2 if d == 0 else 1 - n % 2
                        act.wait_ge(sem("chained"), before(l, "chained") + 2 * n + d + 1)
                        src = ps[64:128, 6 + d, :].rearrange("p (h c) -> p h c", h=H)
                        act.activation(mv_b[d][64:128], src, ACT.Copy)
                        act.activation(mv_a[d][64:128, 1 - c], src, ACT.Copy)
                        act.drain().then_inc(sem(f"state{d}"), 1)
                parts = {"a": new_values, "b": state, "diff": diff}

                def group(k):
                    for d in range(2):
                        level(l, k, d, 0)
                    between(k, 0, "z", parts)
                    for s in range(LEVELS):
                        for d in range(2):
                            act.wait_ge(sem(f"xc_new{d}"), before(l, f"xc_new{d}") + k * LEVELS + s + 1)
                            act.activation(xtb[k % 2][d][0:64, :, 0, :], xtc[k % 2][d][0:64], ACT.Copy).then_inc(sem(f"xb_new{d}"), 1)
                        between(k, s, "p", parts)
                        if s < LEVELS - 1:
                            for d in range(2):
                                level(l, k, d, s + 1)
                            for d in range(2):
                                level_x(l, k, d, s)
                            between(k, s, "t", parts)
                            between(k, s + 1, "z", parts)
                    for d in range(2):
                        act.wait_ge(sem("group_done"), before(l, "group_done") + 2 * k + d + 1)
                        if k:
                            act.wait_ge(sem("chained"), before(l, "chained") + 4 * k)
                        for s_ in range(2):
                            wv = ps[64 * s_:64 * s_ + 64, 2 * d, :].rearrange("p (e c n) -> p c e n", e=HP, c=2)
                            qv = ps[64 * s_:64 * s_ + 64, 2 * d + 1, :].rearrange("p (e c n) -> p c e n", e=HP, c=2)
                            act.activation(st_a[d][64:128, :, s_:H:2, :], wv, ACT.Copy)
                            act.activation(st_b[d][64:128, :, s_:H:2, 0:64], qv, ACT.Copy)
                        for c in range(2):
                            act.activation(st_b[d][0:64, c, :, 0:64], e2[k % 2][d][64 * c:64 * c + 64], ACT.Copy)
                        act.drain().then_inc(sem("wq_out"), 1)
                start_and_end(parts, group)

            def mix_out(l):
                tiles = LT if lat_only(l) else NT
                n = tiles * P
                high_at(l * CHUNKS + 28)
                for e in range(HP):
                    act.activation(o_hi[:, e, 0:n], o_t[:, e, 0:n], ACT.Copy).then_inc(sem("o_high"), 1)
                high_at(l * CHUNKS + 29)
                for t in range(tiles):
                    if t:
                        act.wait_ge(sem("o_summed"), before(l, "o_summed") + t)
                    own.did(act.activation(osq[:], o_g[:, t, :], ACT.Square))
                    act.drain().then_inc(sem("o_sq"), 1)
                act.wait_ge(sem("o_summed"), before(l, "o_summed") + tiles)
                act.activation(o_rt[:, 0:tiles * H], o_ss[:, 0:tiles * H], ACT.Sqrt, bias=eps_t[:], scale=1.0 / DH).then_inc(sem("o_root"), 1)
                high_at(l * CHUNKS + 30)
                for e in range(HP):
                    act.wait_ge(sem("o_turned"), before(l, "o_turned") + e + 1)
                    if e >= 2:
                        act.wait_ge(sem("o_split"), before(l, "o_split") + HP + e - 1)
                    for b, c0, w in ((0, 0, LAT), (1, LAT, CTX)):
                        if b and tiles == LT:
                            continue
                        own.did(act.activation(ov[:, e % 2, c0:c0 + w], ps[:, 6 + b, 0:w], ACT.Copy, scale=vec[l][:, 120:121]))
                    act.drain().then_inc(sem("ov_out"), 1)
                    own.wait()
                    act.activation(o_hi[:, HP + e, 0:n], ov[:, e % 2, 0:n], ACT.Copy).then_inc(sem("o_high"), 1)

            def gate_rows(l, which, gb):
                for i in range(2 if lat_only(l) else 4):
                    act.wait_ge(sem(f"gate_done{which}"), before(l, f"gate_done{which}") + i + 1)
                    act.activation(gb[:, i // 2, 512 * (i % 2):512 * (i % 2) + 512], ps[:, 6 + i % 2, :], ACT.Copy).then_inc(sem(f"gate_out{which}"), 1)

            def ffn_up(l):
                base = l * CHUNKS + 36
                n = LAT if lat_only(l) else TOK
                with act.Fori(0, FT // 2) as i:
                    for j in range(2):
                        for gv, dst in ((0, cg), (1, cw)):
                            high_loop(i, base, 2 * j + gv + 1, 4)
                            act.wait_ge(w_used, i * 4 + (base + 2 * j + gv + 3))
                            act.wait_ge(sem("g_done"), before(l, "g_done") + i * 2 + (j + 1))
                            src = ps[:, 4 * j + 2 * gv:4 * j + 2 * gv + 2, :].rearrange("p a b -> p (a b)")[:, 0:n]
                            act.activation(dst[:, j, 0:n], src, ACT.Copy,
                                           scale=taps[l][:, ds(i * 2 + (2 * FT + gv * FT + j), 1)]).then_inc(sem("up_mid"), 1)
                        act.wait_ge(sem("up_taps"), before(l, "up_taps") + i * 4 + (2 * j + 5))
                        act.activation(cg[:, j, 0:n], cg[:, j, 0:n], ACT.Silu).then_inc(sem("up_silu"), 1)

            def ffn_down(l):
                base = l * CHUNKS + 36 + 2 * FT
                n = LAT if lat_only(l) else TOK
                tiles = LT if lat_only(l) else NT
                for half in range(2):
                    for j in range(11):
                        c = base + 11 * half + j + 1
                        for kk in range(2):
                            q = 22 * half + 2 * j + kk
                            if q >= 2 and kk == 0:
                                act.wait_ge(sem("g_used"), before(l, "g_used") + q // 2)
                            elif q >= 2:
                                act.wait_ge(w_used, base + q // 2 + 2)
                            act.activation(g_hi[:, kk, 0:n], g_sb[:, 2 * j + kk, 0:n], ACT.Copy).then_inc(sem("g_high"), 1)
                        if c < (l + 1) * CHUNKS:
                            high_at(c)
                    act.wait_ge(w_used, base + 11 * half + 10 + 3)
                    for t in range(0, tiles, 2):
                        act.activation(y2_sb[:, t, 512 * half:512 * half + 512], ps[:, t, :], ACT.Copy).then_inc(sem("y_out_a1"), 1)

            for l in range(DEPTH):
                ph = l * PH
                tiles = LT if lat_only(l) else NT
                vectors(l)
                norm(l, 0, NT)
                phase_ends(act, True, ph + 1)
                project(l)
                phase_ends(act, True, ph + 2)
                attend(l)
                phase_ends(act, True, ph + 3)
                delta_prep(l)
                delta(l)
                phase_ends(act, True, ph + 4)
                mix_out(l)
                for half in range(2):
                    for j in range(0 if half else 2, 4):
                        high_at(l * CHUNKS + 29 + 4 * half + j)
                    act.wait_ge(w_used, l * CHUNKS + 28 + 4 * half + 3 + 3)
                    for t in range(0, tiles, 2):
                        act.activation(y_sb[:, t, 512 * half:512 * half + 512], ps[:, t, :], ACT.Copy).then_inc(sem("y_out_a0"), 1)
                gate_rows(l, 0, gate_b)
                act.wait_ge(sem("y_out_d0"), before(l, "y_out_d0") + tiles)
                act.wait_ge(sem("y_out_a0"), before(l, "y_out_a0") + tiles)
                sums(l, "y_rms0", y_sb, tiles, 16, junk[:])
                next_norm(l, 0, "rms1", tiles, junk[:])
                phase_ends(act, True, ph + 5)
                norm(l, 1, tiles)
                phase_ends(act, True, ph + 6)
                ffn_up(l)
                act.wait_ge(sem("g_done"), before(l, "g_done") + FT + 2)
                ffn_down(l)
                gate_rows(l, 1, gate_b2)
                act.wait_ge(sem("y_out_d1"), before(l, "y_out_d1") + tiles)
                act.wait_ge(sem("y_out_a1"), before(l, "y_out_a1") + tiles)
                sums(l, "y_rms1", y2_sb, tiles, 32, junk2[:])
                if l < DEPTH - 1:
                    next_norm(l, 1, "rms0", tiles, junk2[:])
                phase_ends(act, True, ph + 7)

        @block.vector
        def _(dve):
            own = Chain(dve, sem("dve_steps"))
            dve.wait_ge(sem("consts"), 16 * (4 + 2 * DEPTH))

            def vectors(l):
                dve.wait_ge(sem("vec_t"), before(l, "vec_t") + 2 + (l == 0))
                dve.tensor_copy(taps[l][:, 0:P], ps[:, 0, 0:P])
                dve.tensor_copy(taps[l][:, P:P + 4], ps[:, 1, 0:4])
                own.did(dve.tensor_copy(vec[l][:, 0:121], ps[:, 1, 0:121]))
                own.wait()
                if l == 0:
                    for u in range(4):
                        dve.wait_ge(sem("ada_used"), 2 + u + 1)
                        dve.tensor_copy(mod_first[:, u], ps[0:2, 4 + u, :]).then_inc(sem("mod_rows"), 1)
                    dve.wait_ge(sem("mods_done"), 1)
                    own.did(modulate(0, 0, 2 * KT, ps[:, 3, 0:4 * KT]))
                else:
                    own.did(modulate(1, 0, NMOD * KT, mod_raw[:].rearrange("p f s -> p (f s)")))
                own.wait()
                scale_of(l, 0)
                if l:
                    scale_of(l, 1)
                    gates_of(l)
                dve.drain().then_inc(sem("mods"), 1)

            def modulate(l, f0, f1, src):
                return dve.tensor_tensor(mod[:, f0:f1], src.rearrange("p (f s) -> p f s", s=2),
                                         vec[l][:, 40 + f0:40 + f1].unsqueeze(2).to_broadcast([P, f1 - f0, 2]), ALU.add)

            m4 = mod[:].rearrange("p (m k) s -> p m k s", m=NMOD)

            def gain(l, o):
                return vec[l][:, o:o + 8].unsqueeze(2).to_broadcast([P, KT, 2])

            def scale_of(l, w):
                own.did(dve.scalar_tensor_tensor(sc_pre[:, w], m4[:, 3 * w + 1], 1.0, gain(l, 88 + 16 * w), ALU.add, ALU.mult))

            def gates_of(l):
                for w in range(2):
                    own.did(dve.tensor_tensor(gate_c[:, w], m4[:, 3 * w + 2], gain(l, 96 + 16 * w), ALU.mult))

            def modulations():
                dve.wait_ge(sem("mods_done"), 1 + UNITS)
                dve.wait_ge(sem("o_out"), HP)
                n0 = 2 * (NMOD - 2) * KT
                own.did(modulate(0, 2 * KT, NMOD * KT, ps[:, 6, 256:256 + n0]))
                own.did(dve.tensor_copy(mod_raw[:].rearrange("p f s -> p (f s)"), ps[:, 6, 256 + n0:256 + 8 * UNITS]))
                own.wait()
                scale_of(0, 1)
                gates_of(0)

            def norm(l, which, tiles):
                dve.wait_ge(sem(f"rms{which}"), before(l, f"rms{which}") + 1)
                own.did(dve.reciprocal(stat[:, 8:8 + tiles], stat[:, 8:8 + tiles]))
                own.wait()
                for t in range(tiles):
                    dve.tensor_scalar(xn[:, t, :], x_sb[:, t, :], stat[:, 8 + t:9 + t], None, ALU.mult).then_inc(sem(f"normed{which}"), 1)

            def low(l, which, tiles):
                n = 0
                for k in range(KT):
                    for b, c0, w in ((0, 0, LAT), (1, LAT, CTX)):
                        if b and tiles == LT:
                            continue
                        n += 1
                        dve.wait_ge(sem(f"hid_h{which}"), before(l, f"hid_h{which}") + n)
                        dve.tensor_scalar(v_ring[:, n % 2, 0:w], ps[:, 2 * (k % 2) + b, 0:w], sc_pre[:, which, k, b:b + 1],
                                          mod[:, (3 * which) * KT + k, b:b + 1], ALU.mult, ALU.add).then_inc(sem(f"hid_v{which}"), 1)
                        dve.wait_ge(sem(f"hid_v{which}"), before(l, f"hid_v{which}") + n)
                        dve.tensor_tensor(h_lo[:, k, c0:c0 + w], v_ring[:, n % 2, 0:w], h_hi[:, k, c0:c0 + w].bitcast(F32),
                                          ALU.subtract).then_inc(sem(f"h_ready{which}"), 1)

            def outer_taps(dst, src, tap0, tap2, n, step):
                segs = [(0, LAT)] if n == LAT else [(0, LAT), (LAT, TOK)]
                for c0, c1 in segs:
                    step(dve.scalar_tensor_tensor(dst[:, c0 + 1:c1], src[:, c0:c1 - 1], tap0, dst[:, c0 + 1:c1], ALU.mult, ALU.add))
                own.wait()
                for c0, c1 in segs:
                    m = dve.scalar_tensor_tensor(dst[:, c0:c1 - 1], src[:, c0 + 1:c1], tap2, dst[:, c0:c1 - 1], ALU.mult, ALU.add)
                    if (c0, c1) != segs[-1]:
                        step(m)
                return m

            def project(l):
                dve.wait_ge(sem("bd_h"), before(l, "bd_h") + 1)
                dve.tensor_tensor(bd_lo[:], bd_raw[:], bd_hi[:].bitcast(F32), ALU.subtract).then_inc(sem("bd_split"), 1)
                dve.drain().then_inc(sem("qkv_out"), 2)

                def taps_of(i, j):
                    dve.wait_ge(sem("mid"), before(l, "mid") + i * 2 + (j + 1))
                    src = ps[:, 2 * j:2 * j + 2, :].rearrange("p a b -> p (a b)")
                    outer_taps(cv[:, j, :], src, vec[l][:, ds(i * 2 + (4 + j), 1)], vec[l][:, ds(i * 2 + (28 + j), 1)], TOK,
                               own.did).then_inc(sem("taps"), 1)

                def back(t, r):
                    dve.wait_ge(sem("turned"), before(l, "turned") + t + 3)
                    dve.tensor_copy(qkv[:, :, ds(t * P, P)],
                                    ps[:, 4 + 2 * r:6 + 2 * r, :].rearrange("p a (t c) -> p (a t) c", c=P)[:, 0:NT, :]).then_inc(sem("qkv_out"), 1)
                for i in (0,):
                    taps_of(0, 0)
                    taps_of(0, 1)
                    back(0, 0)
                with dve.Fori(1, 6) as i:
                    own.enter(i - 1, 6)
                    taps_of(i, 0)
                    back(i * 2 + (-1), 1)
                    taps_of(i, 1)
                    back(i * 2, 0)
                own.leave(5)
                back(11, 1)
                dve.wait_ge(sem("w_used"), l * CHUNKS + 23 + 3)
                for t in range(1, NT, 2):
                    dve.tensor_copy((v_nat if t < LT else na_v)[:, t, :], ps[:, t, :]).then_inc(sem("v_out_d"), 1)
                dve.wait_ge(sem("bd_done"), before(l, "bd_done") + 1)
                dve.tensor_copy(bd[:], ps[:, 7, 0:192].rearrange("p (t n) -> p t n", t=NT))
                for t in range(NT):
                    dve.wait_ge(sem("qk_sq"), before(l, "qk_sq") + t + 1)
                    dve.tensor_reduce(qk_ss[:, t, :], sq[:].rearrange("p (n c) -> p n c", c=DH), AX.X, ALU.add).then_inc(sem("qk_summed"), 1)
                dve.wait_ge(sem("qk_root"), before(l, "qk_root") + 1)
                own.did(dve.reciprocal(qk_rt[:], qk_rt[:]))
                own.wait()
                own.did(dve.tensor_scalar(qk_rt[:, :, 0:H], qk_rt[:, :, 0:H], DH ** -0.5, None, ALU.mult))
                dve.wait_ge(sem("rb"), before(l, "rb") + 16 * (2 * ROWS + 1))
                for v in range(2):
                    m = dve.tensor_tensor(rb[:, v].rearrange("p h r c -> p h (r c)"), rb[:, v].rearrange("p h r c -> p h (r c)"),
                                          negm[:, v].rearrange("p r c -> p (r c)").unsqueeze(1).to_broadcast([P, H, 256]), ALU.add)
                own.did(m)
                own.wait()
                dve.drain().then_inc(sem("rb_masked"), 1)

            def attend(l):
                tiles = LT if lat_only(l) else NT
                items = [(h, u) for h in range(H) for u in range(tiles)]
                steps = len(items)

                def top(n):
                    h, u = items[n]
                    b = n % 2
                    dve.wait_ge(sem("scored"), before(l, "scored") + n + 1)
                    if u < LT:
                        dst = ps[:, b, 0:256].rearrange("p (j r c) -> p j r c", j=2, r=ROWS)
                        bias = rb[:, 0 if u < 3 else 1, h].rearrange("p r (j c) -> p j r c", j=2)
                        own.did(dve.tensor_tensor(dst, dst, bias, ALU.add))
                        own.wait()
                        dve.tensor_reduce(stat[:, b:b + 1], ps[:, b, :], AX.X, ALU.max, negate=True).then_inc(sem("maxed"), 1)
                    else:
                        dve.tensor_reduce(stat[:, b:b + 1], ps[:, b, 256:512], AX.X, ALU.max, negate=True).then_inc(sem("maxed"), 1)

                top(0)
                for n in range(steps + 1):
                    if n + 1 < steps:
                        top(n + 1)
                    if n < steps:
                        h, u = items[n]
                        c0 = 0 if u < LT else 256
                        dve.wait_ge(sem("exped"), before(l, "exped") + n + 1)
                        own.did(dve.reciprocal(stat[:, 4 + n % 2:5 + n % 2], stat[:, 2 + n % 2:3 + n % 2]))
                        own.wait()
                        dve.tensor_scalar(prob[:, n % 2, c0:512], prob[:, n % 2, c0:512], stat[:, 4 + n % 2:5 + n % 2], None, ALU.mult).then_inc(sem("probs"), 1)
                    if l == 0 and n % 2 == 0 and 2 <= n <= 2 * UNITS:
                        v = n // 2 - 1
                        dve.wait_ge(sem("ada_used"), 2 + 4 + v + 1)
                        dve.wait_ge(sem("mods_done"), 1 + v)
                        dve.tensor_copy(mod_row[:], ps[64 * (v % 2):64 * (v % 2) + 2, 7, :]).then_inc(sem("mod_rows"), 1)
                    if n and n % 2 == 0:
                        h, u = items[n - 1]
                        dve.wait_ge(sem("p_turned"), before(l, "p_turned") + n)
                        if h >= 2 and u == 1:
                            dve.wait_ge(sem("valued"), before(l, "valued") + h - 1)
                        for dst, src in turned(n - 1, u, h):
                            dve.tensor_copy(dst, src)
                        dve.drain().then_inc(sem("pt_odd"), 1)

            def delta_prep(l):
                own.did(dve.tensor_tensor(gtmp[:, 0], bd[:, :, 16:32], al_dt[:, l, 1, :].unsqueeze(1).to_broadcast([P, NT, 16]), ALU.add))
                own.wait()
                own.did(dve.tensor_scalar(gtmp[:, 1], gtmp[:, 0], -1.0, None, ALU.mult))
                own.wait()
                dve.tensor_tensor(gtmp[:, 1], gtmp[:, 1], gtmp[:, 0], ALU.max).then_inc(sem("dec_abs"), 1)
                dve.wait_ge(sem("dec_ln"), before(l, "dec_ln") + 1)
                own.did(dve.scalar_tensor_tensor(gtmp[:, 0], gtmp[:, 0], 0.0, gtmp[:, 1], ALU.max, ALU.add))
                own.wait()
                dve.scalar_tensor_tensor(graw[:], gtmp[:, 0], -1.0, a_exp[:].unsqueeze(1).to_broadcast([P, NT, 16]),
                                         ALU.mult, ALU.mult).then_inc(sem("decays"), 1)
                dve.memset(o_g[:], 0.0)
                for d in range(2):
                    dve.memset(mv_b[d][64:128], 0.0)
                    dve.memset(mv_a[d][64:128], 0.0)
                    own.did(dve.memset(zb[d][:], 0.0))
                dve.wait_ge(sem("e_ready"), before(l, "e_ready") + 1)
                own.did(dve.tensor_scalar(nbe[:], beta[:], -1.0, None, ALU.mult))
                own.wait()
                for d in range(2):
                    own.did(dve.tensor_tensor(nbec[:, d], nbe[:, :, 8 * d:8 * d + 8], e_cum[:, d], ALU.mult))
                dve.drain().then_inc(sem("gates"), 1)
            def delta(l):
                def gram(k, d, s_):
                    n = 4 * k + 2 * d + s_
                    dve.wait_ge(sem("gram"), before(l, "gram") + n + 1)
                    dve.wait_ge(sem("em"), before(l, "em") + 4 * k + 2 * d + 2)
                    for x, off in ((e1, 0), (e2, 256)):
                        x = x[k % 2][d][:, s_:H:2, :]
                        dve.tensor_tensor(x, ps[:, 5, off:off + 256].rearrange("p (e c) -> p e c", e=HP), x, ALU.mult)
                    dve.drain().then_inc(sem("m_ready"), 1)

                def outputs(n):
                    for d in range(2):
                        t, c = TILES[d][n // 2], (n % 2 if d == 0 else 1 - n % 2)
                        dve.wait_ge(sem("chained"), before(l, "chained") + 2 * n + d + 1)
                        o = o_g[64 * c:64 * c + 64, t, :]
                        own.wait()
                        own.did(dve.tensor_tensor(o, ps[0:64, 6 + d, :], o, ALU.add))
                        dve.drain().then_inc(sem(f"o_added{d}"), 1)
                parts = {"b": outputs, "gram": gram}

                def group(k):
                    def lower_z(s):
                        for d in range(2):
                            dve.wait_ge(sem(f"z_done{d}"), before(l, f"z_done{d}") + k * LEVELS + s + 1)
                            dve.tensor_copy(zb[d][64:128, :, :, 1, :], ps[64:128, 2 * d, :].rearrange("p (e c n) -> p e c n", e=HP, c=2)).then_inc(sem(f"zb_d{d}"), 1)
                    lower_z(0)
                    between(k, 0, "z", parts)
                    for s in range(LEVELS):
                        for d in range(2):
                            dve.wait_ge(sem(f"p_done{d}"), before(l, f"p_done{d}") + k * LEVELS + s + 1)
                            if s == 0:
                                dve.wait_ge(sem("xt_init"), before(l, "xt_init") + 2 * k + d + 1)
                            pv = lambda p0, p1: ps[p0:p1, 2 * d + 1, :].rearrange("p (h c) -> p h c", h=H)
                            mk = lambda p0, p1: lev[p0:p1, d, s, :].unsqueeze(1).to_broadcast([p1 - p0, H, C])
                            dve.copy_predicated(xtc[k % 2][d][:], mk(0, P), pv(0, P)).then_inc(sem(f"xc_new{d}"), 1)
                            dve.copy_predicated(xtb[k % 2][d][64:128, :, 1, :], mk(64, P), pv(64, P)).then_inc(sem(f"xt_new{d}"), 1)
                        between(k, s, "p", parts)
                        if s < LEVELS - 1:
                            lower_z(s + 1)
                            between(k, s, "t", parts)
                            between(k, s + 1, "z", parts)
                    for d in range(2):
                        dve.wait_ge(sem(f"xc_new{d}"), before(l, f"xc_new{d}") + (k + 1) * LEVELS)
                    if k:
                        dve.wait_ge(sem("chained"), before(l, "chained") + 4 * k)
                    for d in range(2):
                        t = TILES[d][k]
                        for c in range(2):
                            cp = slice(64 * c, 64 * c + 64)
                            dve.tensor_copy(st_a[d][0:64, c], xtc[k % 2][d][cp])
                            kk = qkv[cp, t, W:2 * W].rearrange("p (h c) -> p h c", h=H)
                            vv = qkv[cp, t, 2 * W:3 * W].rearrange("p (h c) -> p h c", h=H)
                            dve.tensor_tensor(st_b[d][0:64, c, :, 64:128], kk, e_tail[cp, d, t, :].unsqueeze(2).to_broadcast([64, H, C]), ALU.mult)
                            dve.tensor_tensor(mv_a[d][0:64, c], vv, beta[cp, t, 8 * d:8 * d + 8].unsqueeze(2).to_broadcast([64, H, C]), ALU.mult)
                        dve.drain().then_inc(sem("st_ready_d"), 1)
                start_and_end(parts, group)

            def mix_out(l):
                tiles = LT if lat_only(l) else NT
                n = tiles * P
                for e in range(HP):
                    dve.wait_ge(sem("o_high"), before(l, "o_high") + e + 1)
                    dve.tensor_tensor(o_lo[:, e, 0:n], o_t[:, e, 0:n], o_hi[:, e, 0:n].bitcast(F32), ALU.subtract).then_inc(sem("o_split"), 1)
                for t in range(tiles):
                    dve.wait_ge(sem("o_sq"), before(l, "o_sq") + t + 1)
                    dve.tensor_reduce(o_ss[:, t * H:t * H + H], osq[:].rearrange("p (h c) -> p h c", h=H), AX.X, ALU.add).then_inc(sem("o_summed"), 1)
                dve.wait_ge(sem("o_root"), before(l, "o_root") + 1)
                own.did(dve.reciprocal(o_rt[:, 0:tiles * H], o_rt[:, 0:tiles * H]))
                own.wait()
                for t in range(tiles):
                    x = o_g[:, t, :].rearrange("p (h c) -> p h c", h=H)
                    own.did(dve.tensor_tensor(on[:, t, :].rearrange("p (h c) -> p h c", h=H), x,
                                              o_rt[:, t * H:t * H + H].unsqueeze(2).to_broadcast([P, H, DH]), ALU.mult))
                    own.wait()
                    dve.tensor_tensor(on[:, t, :], on[:, t, :], z_sb[:, t, :], ALU.mult).then_inc(sem("o_normed"), 1)
                for e in range(HP):
                    dve.wait_ge(sem("o_high"), before(l, "o_high") + HP + e + 1)
                    dve.tensor_tensor(o_lo[:, HP + e, 0:n], ov[:, e % 2, 0:n], o_hi[:, HP + e, 0:n].bitcast(F32), ALU.subtract).then_inc(sem("o_split"), 1)

            def gate_rows(l, which, gd):
                for i in range(2 if lat_only(l) else 4):
                    if i:
                        dve.wait_ge(sem(f"gate_done{which}"), before(l, f"gate_done{which}") + i)
                    for q in range(4):
                        f = 4 * (i % 2) + q
                        own.did(dve.tensor_scalar(gd[:, q * P:q * P + P], ident, gate_c[:, which, f, i // 2:i // 2 + 1], None, ALU.mult))
                    dve.drain().then_inc(sem(f"gdiag{which}"), 1)

            def residual(l, which, y, gb):
                tiles = LT if lat_only(l) else NT
                off = 16 + 16 * which + 8
                dve.wait_ge(sem(f"y_rms{which}"), before(l, f"y_rms{which}") + 1)
                own.did(dve.reciprocal(stat[:, off:off + tiles], stat[:, off:off + tiles]))
                own.wait()
                if which == 0:
                    dve.wait_ge(sem("x_landed"), 64 + 32 * l)
                for t in range(tiles):
                    own.did(dve.scalar_tensor_tensor(y[:, t, :], y[:, t, :], stat[:, off + t:off + t + 1], gb[:, 0 if t < LT else 1, :], ALU.mult, ALU.mult))
                    own.wait()
                    dve.tensor_tensor(x_sb[:, t, :], x_sb[:, t, :], y[:, t, :], ALU.add).then_inc(sem(f"summed{which}"), 1)

            def y_out(l, which, y):
                tiles = LT if lat_only(l) else NT
                for half in range(2):
                    dve.wait_ge(sem("w_used"), l * CHUNKS + 28 + 4 * half + 3 + 3)
                    for t in range(1, tiles, 2):
                        dve.tensor_copy(y[:, t, 512 * half:512 * half + 512], ps[:, t, :]).then_inc(sem(f"y_out_d{which}"), 1)

            def ffn_up(l):
                n = LAT if lat_only(l) else TOK
                per = 6 if n == TOK else 2
                dve.drain().then_inc(sem("up_taps"), 4)
                dve.drain().then_inc(sem("g_done"), 2)
                with dve.Fori(0, FT // 2) as i:
                    own.enter(i, 2 * per)
                    for j in range(2):
                        for gv, dst in ((0, cg), (1, cw)):
                            dve.wait_ge(sem("up_mid"), before(l, "up_mid") + i * 4 + (2 * j + gv + 1))
                            src = ps[:, 4 * j + 2 * gv:4 * j + 2 * gv + 2, :].rearrange("p a b -> p (a b)")
                            tap = lambda k: taps[l][:, ds(i * 2 + (k * 2 * FT + gv * FT + j), 1)]
                            outer_taps(dst[:, j, :], src, tap(0), tap(2), n, own.did).then_inc(sem("up_taps"), 1)
                        dve.wait_ge(sem("up_silu"), before(l, "up_silu") + i * 2 + (j + 1))
                        dve.wait_ge(sem("up_taps"), before(l, "up_taps") + i * 4 + (2 * j + 6))
                        dve.tensor_tensor(g_sb[:, ds(i * 2 + j, 1), 0:n].rearrange("p a n -> p (a n)"), cg[:, j, 0:n], cw[:, j, 0:n], ALU.mult).then_inc(sem("g_done"), 1)
                own.leave(FT // 2)

            def ffn_down(l):
                n = LAT if lat_only(l) else TOK
                tiles = LT if lat_only(l) else NT
                for half in range(2):
                    for f in range(FT):
                        dve.wait_ge(sem("g_high"), before(l, "g_high") + FT * half + f + 1)
                        dve.tensor_tensor(g_lo[:, f % 2, 0:n], g_sb[:, f, 0:n], g_hi[:, f % 2, 0:n].bitcast(F32), ALU.subtract).then_inc(sem("g_split"), 1)
                    dve.wait_ge(sem("w_used"), l * CHUNKS + 36 + 2 * FT + 11 * half + 10 + 3)
                    for t in range(1, tiles, 2):
                        dve.tensor_copy(y2_sb[:, t, 512 * half:512 * half + 512], ps[:, t, :]).then_inc(sem("y_out_d1"), 1)

            for l in range(DEPTH):
                ph = l * PH
                tiles = LT if lat_only(l) else NT
                vectors(l)
                norm(l, 0, NT)
                low(l, 0, NT)
                phase_ends(dve, True, ph + 1)
                project(l)
                phase_ends(dve, True, ph + 2)
                attend(l)
                if l == 0:
                    modulations()
                phase_ends(dve, True, ph + 3)
                delta_prep(l)
                delta(l)
                phase_ends(dve, True, ph + 4)
                mix_out(l)
                y_out(l, 0, y_sb)
                gate_rows(l, 0, gdiag)
                dve.wait_ge(sem("gate_out0"), before(l, "gate_out0") + 2 if lat_only(l) else 4)
                residual(l, 0, y_sb, gate_b)
                phase_ends(dve, True, ph + 5)
                norm(l, 1, tiles)
                low(l, 1, tiles)
                phase_ends(dve, True, ph + 6)
                ffn_up(l)
                ffn_down(l)
                gate_rows(l, 1, gdiag2)
                dve.wait_ge(sem("gate_out1"), before(l, "gate_out1") + 2 if lat_only(l) else 4)
                residual(l, 1, y2_sb, gate_b2)
                phase_ends(dve, True, ph + 7)


INS = ["x", "c", "ctx", "c_ctx", "ada_w", "ada_b", "norm_mix_pre", "norm_mix_post", "w_in", "qkv_conv", "a_log",
       "dt_bias", "gdn_norm", "rpb", "w_out", "norm_ffn_pre", "norm_ffn_post", "ffn_up", "ffn_conv", "ffn_down"]


def kernel(**inputs):
    import numpy as _np
    import concourse.bacc as _bacc
    from concourse import mybir as _mybir
    from concourse.bass_utils import run_bass_kernel_spmd as _run

    nc = _bacc.Bacc("TRN2", target_bir_lowering=False, num_devices=1, dynamic_dma_scratch_size=256)
    arrays, args = {}, {}
    table, levels = constants()
    for name, arr in [(n, inputs[n]) for n in INS] + [("cns", table), ("lev", levels)]:
        v = _np.ascontiguousarray(arr)
        arrays[f"in_{name}"] = v
        args[name] = nc.dram_tensor(f"in_{name}", v.shape, _mybir.dt.from_np(v.dtype), kind="ExternalInput").ap()
    args["out"] = nc.dram_tensor("out_0", (1, LAT, D), F32, kind="ExternalOutput").ap()
    build(nc, args)
    r = _run(nc, [arrays], core_ids=[0])
    return r.results[0]["out_0"]
```
